# Optimizing a Trainium2 kernel written in Bass

```python
import jax, jax.numpy as jnp
from jax import lax
import numpy as np

D_MODEL = 1024
BATCH = 1
SEQ = 1024
DEPTH = 1

N_META = 16
D_MIX = D_MODEL
LRU_WIDTH = D_MIX // 2
LRU_HEADS = 8
LRU_HEAD_DIM = LRU_WIDTH // LRU_HEADS
LRU_CONV = 4
LRU_C = 8.0
MLA_HEADS = 8
QK_NOPE = 64
QK_ROPE = 32
QK_DIM = QK_NOPE + QK_ROPE
V_DIM = (D_MIX - LRU_WIDTH) // MLA_HEADS
Q_LORA = 256
KV_LORA = 128
ROPE_THETA = 10000.0
Q_BLOCK = 128
D_FF = 2816
FFN_CONV = 3
EPS = 1e-6
NEG_INF = -1e30
IN_COLS = 2 * LRU_WIDTH + Q_LORA + KV_LORA + QK_ROPE

kernel_name = "hymba_rglru_mla_convglu_encoder"

def rmsnorm(x, g):
    xf = x.astype(jnp.float32)
    y = xf * lax.rsqrt(jnp.mean(xf * xf, axis=-1, keepdims=True) + EPS)
    return (y * g.astype(jnp.float32)).astype(x.dtype)

def dwconv(x, w, b, left):
    K = w.shape[0]
    T = x.shape[1]
    xp = jnp.pad(x, ((0, 0), (left, K - 1 - left), (0, 0)))
    y = xp[:, 0:T] * w[0]
    for k in range(1, K):
        y = y + xp[:, k:k + T] * w[k]
    return y + b

def rope(x, pos):
    R = x.shape[-1]
    inv_freq = ROPE_THETA ** (-jnp.arange(0, R, 2, dtype=jnp.float32) / R)
    ang = pos[:, None] * inv_freq[None, :]
    cos = jnp.cos(ang)[:, None, :]
    sin = jnp.sin(ang)[:, None, :]
    xf = x.astype(jnp.float32)
    x1, x2 = xf[..., :R // 2], xf[..., R // 2:]
    out = jnp.concatenate([x1 * cos - x2 * sin, x1 * sin + x2 * cos], axis=-1)
    return out.astype(x.dtype)

def _lin_combine(left, right):
    a1, b1 = left
    a2, b2 = right
    return a1 * a2, a2 * b1 + b2

def rg_lru_bidir(xc, w_a, b_a, w_x, b_x, lam):
    B, T, W = xc.shape
    xf = xc.astype(jnp.float32)
    xh = xf.reshape(B, T, LRU_HEADS, LRU_HEAD_DIM)
    r = jax.nn.sigmoid(jnp.einsum('bthi,nhij->nbthj', xh, w_a.astype(jnp.float32)).reshape(2, B, T, W)
                       + b_a.astype(jnp.float32)[:, None, None, :])
    i = jax.nn.sigmoid(jnp.einsum('bthi,nhij->nbthj', xh, w_x.astype(jnp.float32)).reshape(2, B, T, W)
                       + b_x.astype(jnp.float32)[:, None, None, :])
    log_a = -LRU_C * r * jax.nn.softplus(-lam.astype(jnp.float32))[:, None, None, :]
    a = jnp.exp(log_a)
    u = jnp.sqrt(-jnp.expm1(2.0 * log_a)) * (i * xf[None])
    _, h_fwd = lax.associative_scan(_lin_combine, (a[0], u[0]), axis=1)
    _, h_bwd = lax.associative_scan(_lin_combine, (a[1], u[1]), axis=1, reverse=True)
    return (h_fwd + h_bwd).astype(xc.dtype)

def block_attention(q, k, v):
    B, T, H, Dk = q.shape
    n_blocks = -(-T // Q_BLOCK)
    T_pad = n_blocks * Q_BLOCK
    pad = ((0, 0), (0, T_pad - T), (0, 0), (0, 0))
    q, k, v = jnp.pad(q, pad), jnp.pad(k, pad), jnp.pad(v, pad)
    key_valid = jnp.arange(T_pad) < T
    scale = 1.0 / np.sqrt(Dk).astype(np.float32)
    qb = q.reshape(B, n_blocks, Q_BLOCK, H, Dk).transpose(1, 0, 2, 3, 4)

    def one_block(qblk):
        s = jnp.einsum('bqhd,bkhd->bhqk', qblk, k).astype(jnp.float32) * scale
        s = jnp.where(key_valid[None, None, None, :], s, NEG_INF)
        p = jax.nn.softmax(s, axis=-1).astype(v.dtype)
        return jnp.einsum('bhqk,bkhd->bqhd', p, v)

    o = lax.map(one_block, qb)
    o = o.transpose(1, 0, 2, 3, 4).reshape(B, T_pad, H, v.shape[-1])
    return o[:, :T]

def setup_inputs(seed: int = 0) -> dict:
    key = jax.random.key(seed)
    ks = jax.random.split(key, 32)
    f32 = jnp.float32

    def nrm(k, shape, fan_in):
        return jax.random.normal(k, shape, f32) * (fan_in ** -0.5)

    def gain(k, shape):
        return 1.0 + 0.02 * jax.random.normal(k, shape, f32)

    L = DEPTH
    a0 = jax.random.uniform(ks[10], (L, 2, LRU_WIDTH), f32, 0.9, 0.999)
    return {
        "x": jax.random.normal(ks[0], (BATCH, SEQ, D_MODEL), f32),
        "meta_tokens": jax.random.normal(ks[1], (N_META, D_MODEL), f32),
        "norm_mix_g": gain(ks[2], (L, D_MODEL)),
        "w_in": nrm(ks[3], (L, D_MODEL, IN_COLS), D_MODEL),
        "conv_lru_w": nrm(ks[4], (L, LRU_CONV, LRU_WIDTH), LRU_CONV),
        "conv_lru_b": 0.01 * jax.random.normal(ks[5], (L, LRU_WIDTH), f32),
        "lru_w_a": nrm(ks[6], (L, 2, LRU_HEADS, LRU_HEAD_DIM, LRU_HEAD_DIM), LRU_HEAD_DIM),
        "lru_b_a": 0.1 * jax.random.normal(ks[7], (L, 2, LRU_WIDTH), f32),
        "lru_w_x": nrm(ks[8], (L, 2, LRU_HEADS, LRU_HEAD_DIM, LRU_HEAD_DIM), LRU_HEAD_DIM),
        "lru_b_x": 0.1 * jax.random.normal(ks[9], (L, 2, LRU_WIDTH), f32),
        "lru_lambda": jnp.log(a0) - jnp.log1p(-a0),
        "lru_gate_g": gain(ks[11], (L, LRU_WIDTH)),
        "q_latent_g": gain(ks[12], (L, Q_LORA)),
        "w_uq": nrm(ks[13], (L, Q_LORA, MLA_HEADS * QK_DIM), Q_LORA),
        "kv_latent_g": gain(ks[14], (L, KV_LORA)),
        "w_ukv": nrm(ks[15], (L, KV_LORA, MLA_HEADS * (QK_NOPE + V_DIM)), KV_LORA),
        "q_norm_g": gain(ks[16], (L, QK_DIM)),
        "k_norm_g": gain(ks[17], (L, QK_DIM)),
        "mla_out_g": gain(ks[18], (L, MLA_HEADS * V_DIM)),
        "w_out": nrm(ks[19], (L, D_MIX, D_MODEL), D_MIX),
        "norm_ffn_g": gain(ks[20], (L, D_MODEL)),
        "w_ffn_up": nrm(ks[21], (L, D_MODEL, 2 * D_FF), D_MODEL),
        "conv_ffn_w": nrm(ks[22], (L, FFN_CONV, D_FF), FFN_CONV),
        "conv_ffn_b": 0.01 * jax.random.normal(ks[23], (L, D_FF), f32),
        "w_ffn_down": nrm(ks[24], (L, D_FF, D_MODEL), D_FF),
    }

def reference(x, meta_tokens, norm_mix_g, w_in, conv_lru_w, conv_lru_b, lru_w_a, lru_b_a,
              lru_w_x, lru_b_x, lru_lambda, lru_gate_g, q_latent_g, w_uq, kv_latent_g, w_ukv,
              q_norm_g, k_norm_g, mla_out_g, w_out, norm_ffn_g, w_ffn_up, conv_ffn_w,
              conv_ffn_b, w_ffn_down):
    B = x.shape[0]
    meta = jnp.broadcast_to(meta_tokens.astype(x.dtype)[None], (B, N_META, D_MODEL))
    h = jnp.concatenate([meta, x], axis=1)
    T = h.shape[1]
    pos = jnp.arange(T, dtype=jnp.float32)
    splits = np.cumsum([LRU_WIDTH, LRU_WIDTH, Q_LORA, KV_LORA]).tolist()

    for l in range(DEPTH):
        hn = rmsnorm(h, norm_mix_g[l])
        proj = hn @ w_in[l]
        x_lru, g_lru, c_q, c_kv, k_pe = jnp.split(proj, splits, axis=-1)

        xc = dwconv(x_lru, conv_lru_w[l], conv_lru_b[l], left=LRU_CONV // 2)
        y_lru = rg_lru_bidir(xc, lru_w_a[l], lru_b_a[l], lru_w_x[l], lru_b_x[l], lru_lambda[l])
        y_lru = y_lru * jax.nn.gelu(g_lru)

        q = (rmsnorm(c_q, q_latent_g[l]) @ w_uq[l]).reshape(B, T, MLA_HEADS, QK_DIM)
        kv = (rmsnorm(c_kv, kv_latent_g[l]) @ w_ukv[l]).reshape(B, T, MLA_HEADS, QK_NOPE + V_DIM)
        k_nope, v = kv[..., :QK_NOPE], kv[..., QK_NOPE:]
        k_rope = jnp.broadcast_to(k_pe[:, :, None, :], (B, T, MLA_HEADS, QK_ROPE))
        k = jnp.concatenate([k_nope, k_rope], axis=-1)
        q = rmsnorm(q, q_norm_g[l])
        k = rmsnorm(k, k_norm_g[l])
        q = jnp.concatenate([q[..., :QK_NOPE], rope(q[..., QK_NOPE:], pos)], axis=-1)
        k = jnp.concatenate([k[..., :QK_NOPE], rope(k[..., QK_NOPE:], pos)], axis=-1)
        y_mla = block_attention(q, k, v).reshape(B, T, MLA_HEADS * V_DIM)

        y = jnp.concatenate([rmsnorm(y_lru, lru_gate_g[l]), rmsnorm(y_mla, mla_out_g[l])], axis=-1)
        h = h + y @ w_out[l]

        hn = rmsnorm(h, norm_ffn_g[l])
        gate, up = jnp.split(hn @ w_ffn_up[l], 2, axis=-1)
        gate = dwconv(gate, conv_ffn_w[l], conv_ffn_b[l], left=FFN_CONV // 2)
        h = h + (jax.nn.silu(gate) * up) @ w_ffn_down[l]

    return h[:, N_META:]


_drawn_inputs = setup_inputs


def setup_inputs(seed=0):
    import zlib

    import numpy as np

    out = dict(_drawn_inputs(seed))
    spreads = {}
    factors = {'lru_b_a': 4.846,
     'lru_b_x': 3.138,
     'lru_gate_g': 5.191,
     'q_latent_g': 5.53,
     'kv_latent_g': 3.043,
     'q_norm_g': 5.045,
     'k_norm_g': 5.48,
     'mla_out_g': 5.512,
     'norm_ffn_g': 5.176,
     'conv_ffn_b': 8.0}
    for name, (base, spread) in spreads.items():
        noise = np.random.default_rng([zlib.crc32(name.encode()), seed]).standard_normal(out[name].shape)
        drawn = base * np.exp(spread * noise) if base else spread * noise
        out[name] = __import__('jax').numpy.asarray(drawn.astype(out[name].dtype))
    for name, factor in factors.items():
        out[name] = (out[name] * factor).astype(out[name].dtype)
    return out
```

```python
from contextlib import ExitStack

import numpy as np

import concourse.bass as bass
from concourse import mybir

F32 = mybir.dt.float32
F32R = mybir.dt.float32r
ACT = mybir.ActivationFunctionType
ALU = mybir.AluOpType
AX = mybir.AxisListType

P = 128
D = 1024
KD = D // P
META = 16
SEQ = 1024
T = META + SEQ
XT = SEQ // P
NT = XT + 1
LRU = 512
LF = LRU // P
TAPS = 4
LRU_C = 8.0
HEADS = 8
NOPE, ROPE = 64, 32
QK = NOPE + ROPE
VD = 64
QL, KVL = 256, 128
FF = 2816
NFF = FF // P
EPS = 1e-6
CH = [(0, 348), (348, 346), (694, 346)]
WORD = 4


def token_rows(i):
    return (P, META + P * i) if i < XT else (META, 0)


COLS = {}
_at = 0
for _name, _n in [("mix_g", KD), ("conv_w", LF * TAPS), ("conv_b", LF), ("gate_b", LF * 4), ("lam", LF * 2),
                  ("q_g", QL // P), ("kv_g", KVL // P), ("out_g", KD), ("ffn_w", NFF * 3), ("ffn_b", NFF)]:
    COLS[_name] = _at
    _at += _n
NCOL = _at


class Place:

    BASE = 16512

    def __init__(self, nc):
        self.nc = nc

    def __call__(self, name, at, shape, dtype=F32, parts=P):
        words = int(np.prod(shape))
        t = self.nc.alloc_sbuf_tensor_at(name, [parts, words], dtype, offset=self.BASE + WORD * at)
        ap = t[:, :]
        if len(shape) == 2:
            ap = ap.rearrange("p (a b) -> p a b", a=shape[0])
        if len(shape) == 3:
            ap = ap.rearrange("p (a b c) -> p a b c", a=shape[0], b=shape[1])
        return ap


def f32(ap):
    return ap.bitcast(F32)


def chain(eng, sem):
    n = [0]

    def link(ins):
        n[0] += 1
        ins.then_inc(sem, 1)
        eng.wait_ge(sem, n[0])

    return link


def split_products(nc, out, w_h, w_l, x_h, x_l, first, last):
    nc.tensor.matmul(out, w_h, x_h, start=first, stop=False)
    nc.tensor.matmul(out, w_h, x_l, start=False, stop=False)
    return nc.tensor.matmul(out, w_l, x_h, start=False, stop=last)


M_SMALL = 0
M_YL = 1400
M_A = M_YL + LF * T


def constants(place):
    c = {}
    at = M_SMALL
    for name, shape in [("ident", (P,)), ("par", (NCOL,)), ("sp4", (LF * 2,)), ("sp4n", (LF * 2,)), ("hb", (LF * 4,)),
                        ("ones", (P,)), ("gqk", (2, QK)), ("rope_c", (NT, ROPE)), ("rope_s", (NT, ROPE)),
                        ("lam_t", (6, LF * 2)), ("stat", (2, 64))]:
        c[name] = place(name, at, shape)
        at += -(-int(np.prod(shape)) // 8) * 8
    assert at <= M_YL, at
    return c


def mix_phase(nc, place, con, yl, cq, kpe_fm, psum, dram, sem):
    at = M_A
    xn_h = place("xn_h", at, (KD, T), F32R); at += KD * T
    xn_l = place("xn_l", at, (KD, T), F32R); at += KD * T
    w_h = [place(f"win_h{b}", at + 2048 * b, (KD, P), F32R) for b in range(2)]
    w_l = [place(f"win_l{b}", at + 2048 * b + 1024, (KD, P), F32R) for b in range(2)]; at += 4096
    gw_h = place("gw_h", at, (4 * LF, P), F32R); at += 2048
    gw_l = place("gw_l", at, (4 * LF, P), F32R); at += 2048
    xc_h = place("xc_h", at, (T,), F32R); at += T
    xc_l = place("xc_l", at, (T,), F32R); at += T
    w_raw = [place(f"win_raw{b}", at + 1024 * b, (KD, P)) for b in range(2)]; at += 2048
    xpad = kpe_fm[1]
    xc = [place(f"xc{b}", at + T * b, (T,)) for b in range(2)]; at += 2 * T
    gel = [place(f"gelu{b}", at + T * b, (T,)) for b in range(2)]; at += 2 * T
    rb = place("rb", at, (T,)); at += T
    A = [place(f"lru_a{d}", at + T * d, (T,)) for d in range(2)]
    W = [place(f"lru_w{d}", at + T * (2 + d), (T,)) for d in range(2)]
    X = [place(f"lru_x{d}", at + T * (4 + d), (T,)) for d in range(2)]
    S = [place(f"lru_s{d}", at + T * (6 + d), (T,)) for d in range(2)]
    xt = [place(f"xt{b}", at + T * b, (T,)) for b in range(4)]
    sq = [place(f"xsq{b}", at + T * (4 + b), (T,)) for b in range(2)]
    acc = place("xacc", at + T * 6, (T,)); at += 8 * T
    assert at <= M_CQ, (at, M_CQ)
    gw_raw = place("gw_raw", M_YL, (4 * LF, P))
    par = con["par"]

    def col(name, i):
        return par[:, COLS[name] + i:COLS[name] + i + 1]

    tiles = [("x", 0), ("x", 1), ("g", 0), ("g", 1), ("x", 2), ("g", 2), ("x", 3), ("g", 3),
             ("c", 0), ("c", 1), ("c", 2), ("k", 0)]
    first_col = {"x": 0, "g": LRU, "c": 2 * LRU, "k": 2 * LRU + QL + KVL}
    order = [("x", 0), ("x", 1), ("s", 0), ("g", 0), ("G", 0), ("g", 1), ("G", 1), ("x", 2), ("g", 2), ("G", 2),
             ("x", 3), ("g", 3), ("G", 3), ("c", 0), ("c", 1), ("c", 2), ("k", 0)]
    units = []
    for kind, f in order:
        if kind == "G":
            units += [(kind, f, d, w, c) for d in range(2) for w in range(2) for c in range(3)]
        else:
            units += [(kind, f, c) for c in range(3)]
    at_unit = {u: n for n, u in enumerate(units)}
    dve_reads = [("s", 0, 0), ("s", 0, 1), ("x", 0, 0), ("x", 0, 1), ("s", 0, 2), ("x", 0, 2)]
    dve_reads += [u for u in units if u[0] != "G" and u not in dve_reads]
    act_reads = [u for u in units if u[0] == "G"]

    def bank(u):
        return psum[at_unit[u] % 8]

    def wait_unit(eng, u):
        eng.wait_ge(sem["unit_done"], at_unit[u] + 1)

    def wait_bank(eng, u):
        n = at_unit[u] - 8
        if n >= 0:
            v = units[n]
            if v[0] == "G":
                eng.wait_ge(sem["unit_read_act"], act_reads.index(v) + 1)
            else:
                eng.wait_ge(sem["unit_read_dve"], dve_reads.index(v) + 1)

    def wait_tile(eng, n):
        kind, f = tiles[n]
        eng.wait_ge(sem["unit_done"], at_unit[(kind, f, 2)] + 1)

    with nc.Block() as block:
        @block.sync
        def _(sp):
            sp.dma_start(par, dram["par"]).then_inc(sem["par_in"], 16)

            def load_x(k):
                if k >= 4:
                    sp.wait_ge(sem["x_sq"], k - 3)
                    sp.wait_ge(sem["x_lo"], k - 3)
                sp.dma_start(xt[k % 4], dram["x_fm"][k]).then_inc(sem["xt_in"][k % 4], 16)

            def load_w(n):
                if n >= 2:
                    sp.wait_ge(sem["w_split"], n - 1)
                cols = ROPE if tiles[n][0] == "k" else P
                c0 = first_col[tiles[n][0]] + P * tiles[n][1]
                sp.dma_start(w_raw[n % 2][:, :, 0:cols],
                             dram["w_in"].rearrange("(k p) n -> p k n", p=P)[:, :, c0:c0 + cols])\
                  .then_inc(sem["w_in"][n % 2], 16)

            load_x(0)
            load_w(0)
            load_x(1)
            load_w(1)
            for k in range(2, KD):
                load_x(k)
            sp.dma_start(gw_raw, dram["gate_w"]).then_inc(sem["gw_in"], 16)
            for n, name in enumerate(["ident", "gqk", "rope_c", "rope_s"]):
                sp.dma_start(con[name], dram[name]).then_inc(sem["con_in"], 16)
            for n in range(2, len(tiles)):
                load_w(n)

        @block.gpsimd
        def _(pool):
            link = chain(pool, sem["pool_link"])
            nc.gpsimd.memset(con["ones"], 1.0).then_inc(sem["ones"], 1)
            nc.gpsimd.memset(xpad[:, 0:2], 0.0).then_inc(sem["pads"], 1)
            nc.gpsimd.memset(xpad[:, T + 2:T + 3], 0.0).then_inc(sem["pads"], 1)

            def split_w(n):
                cols = ROPE if tiles[n][0] == "k" else P
                pool.wait_ge(sem["w_in"][n % 2], 16 * (n // 2 + 1))
                if n >= 2:
                    wait_tile(pool, n - 2)
                raw = w_raw[n % 2][:, :, 0:cols]
                link(nc.gpsimd.tensor_copy(w_h[n % 2][:, :, 0:cols], raw))
                nc.gpsimd.tensor_tensor(w_l[n % 2][:, :, 0:cols], raw, f32(w_h[n % 2][:, :, 0:cols]),
                                        ALU.subtract).then_inc(sem["w_split"], 1)

            def split_gates():
                pool.wait_ge(sem["gw_in"], 16)
                link(nc.gpsimd.tensor_copy(gw_h, gw_raw))
                nc.gpsimd.tensor_tensor(gw_l, gw_raw, f32(gw_h), ALU.subtract).then_inc(sem["gw_split"], 1)

            def low_xc(f):
                pool.wait_ge(sem["xc_hi"], f + 1)
                nc.gpsimd.tensor_tensor(xc_l, xc[f % 2], f32(xc_h), ALU.subtract).then_inc(sem["xc_lo"], 1)

            def square_a(f):
                if f:
                    pool.wait_ge(sem["y_lru"], f)
                for d in range(2):
                    pool.wait_ge(sem["a_ready"], 2 * f + d + 1)
                    nc.gpsimd.tensor_tensor(S[d], A[d], A[d], ALU.mult).then_inc(sem["a_sq"], 1)

            def join(f):
                pool.wait_ge(sem["scanned"], 2 * f + 2)
                link(nc.gpsimd.tensor_tensor(S[0], S[0], S[1], ALU.add))
                pool.wait_ge(sem["gelu"], f + 1)
                if f == 0:
                    pool.wait_ge(sem["gw_split"], 1)
                nc.gpsimd.tensor_tensor(yl[:, f, :], S[0], gel[f % 2], ALU.mult).then_inc(sem["y_lru"], 1)

            split_w(0)
            split_w(1)
            split_gates()
            split_w(2)
            low_xc(0)
            split_w(3)
            square_a(0)
            low_xc(1)
            for f in range(LF):
                if f < LF:
                    split_w(4 + 2 * f)
                    split_w(5 + 2 * f)
                join(f)
                if f + 1 < LF:
                    square_a(f + 1)
                if f + 2 < LF:
                    low_xc(f + 2)

        @block.scalar
        def _(act):
            link = chain(act, sem["act_link"])
            act.wait_ge(sem["par_in"], 16)
            for k in range(KD):
                act.wait_ge(sem["xt_in"][k % 4], 16 * (k // 4 + 1))
                nc.scalar.activation(xn_h[:, k, :], xt[k % 4], ACT.Copy, scale=col("mix_g", k)).then_inc(sem["x_hi"], 1)
                if k >= 2:
                    act.wait_ge(sem["x_acc"], k - 1)
                nc.scalar.activation(sq[k % 2], xt[k % 4], ACT.Square).then_inc(sem["x_sq"], 1)
            lam = par[:, COLS["lam"]:COLS["lam"] + 2 * LF]
            link(nc.scalar.activation(con["lam_t"][:, 0, :], lam, ACT.Abs))
            nc.scalar.activation(con["lam_t"][:, 1, :], con["lam_t"][:, 0, :], ACT.Exp, scale=-1.0).then_inc(sem["lam_e"], 1)
            for c, (c0, cn) in enumerate(CH):
                act.wait_ge(sem["unit_read_dve"], dve_reads.index(("s", 0, c)) + 1)
                nc.scalar.activation(rb[:, c0:c0 + cn], rb[:, c0:c0 + cn], ACT.Sqrt).then_inc(sem["std"], 1)
            for f in range(LF):
                act.wait_ge(sem["conv"], f + 1)
                if f:
                    act.wait_ge(sem["unit_done"], at_unit[("G", f - 1, 1, 1, 2)] + 1)
                nc.scalar.activation(xc_h, xc[f % 2], ACT.Copy).then_inc(sem["xc_hi"], 1)
                act.wait_ge(sem["unit_read_dve"], dve_reads.index(("g", f, 2)) + 1)
                nc.scalar.activation(gel[f % 2], gel[f % 2], ACT.Gelu_apprx_tanh).then_inc(sem["gelu"], 1)
                if f == 0:
                    act.wait_ge(sem["lam_done"], 1)
                for d in range(2):
                    if f:
                        act.wait_ge(sem["scanned"], 2 * (f - 1) + d + 1)
                    for w, out in ((0, A[d]), (1, X[d])):
                        hb = con["hb"][:, 4 * f + 2 * d + w:4 * f + 2 * d + w + 1]
                        for c, (c0, cn) in enumerate(CH):
                            wait_unit(act, ("G", f, d, w, c))
                            nc.scalar.activation(out[:, c0:c0 + cn], bank(("G", f, d, w, c))[:, 0:cn], ACT.Tanh,
                                                 bias=hb, scale=0.5).then_inc(sem["unit_read_act"], 1)
                    act.wait_ge(sem["unit_read_act"], 12 * f + 6 * d + 6)
                    p4 = con["sp4"][:, 2 * f + d:2 * f + d + 1]
                    n4 = con["sp4n"][:, 2 * f + d:2 * f + d + 1]
                    link(nc.scalar.activation(W[d], A[d], ACT.Tanh, bias=p4, scale=p4))
                    nc.scalar.activation(A[d], A[d], ACT.Exp, bias=n4, scale=n4).then_inc(sem["a_ready"], 1)
                for d in range(2):
                    act.wait_ge(sem["var_lru"], 2 * f + d + 1)
                    nc.scalar.activation(W[d], W[d], ACT.Sqrt).then_inc(sem["sqrt_lru"], 1)

        @block.vector
        def _(dve):
            link = chain(dve, sem["dve_link"])
            dve.wait_ge(sem["par_in"], 16)
            for k in range(KD):
                dve.wait_ge(sem["x_hi"], k + 1)
                nc.vector.scalar_tensor_tensor(out=xn_l[:, k, :], in0=xt[k % 4], scalar=col("mix_g", k),
                                               in1=f32(xn_h[:, k, :]), op0=ALU.mult, op1=ALU.subtract)\
                  .then_inc(sem["x_lo"], 1)
                dve.wait_ge(sem["x_sq"], k + 1)
                if k == 0:
                    nc.vector.tensor_copy(acc, sq[0]).then_inc(sem["x_acc"], 1)
                else:
                    dve.wait_ge(sem["x_acc"], k)
                    nc.vector.tensor_tensor(acc, acc, sq[k % 2], ALU.add).then_inc(sem["x_acc"], 1)

            link(nc.vector.tensor_scalar(con["hb"], par[:, COLS["gate_b"]:COLS["gate_b"] + 4 * LF], 0.5, None, ALU.mult))
            lt = con["lam_t"]
            z, e, w, w2, s, m = (lt[:, i, :] for i in (0, 1, 2, 3, 4, 5))
            dve.wait_ge(sem["lam_e"], 1)
            lam = par[:, COLS["lam"]:COLS["lam"] + 2 * LF]
            link(nc.vector.tensor_scalar(m, lam, -1.0, 0.0, ALU.mult, ALU.max))
            link(nc.vector.tensor_scalar(w2, e, 2.0, None, ALU.add))
            link(nc.vector.reciprocal(w, w2))
            link(nc.vector.tensor_tensor(w, w, e, ALU.mult))
            link(nc.vector.tensor_tensor(w2, w, w, ALU.mult))
            n_terms = 10
            link(nc.vector.tensor_scalar(s, w2, 1.0 / (2 * n_terms + 1), 1.0 / (2 * n_terms - 1), ALU.mult, ALU.add))
            for j in range(n_terms - 2, -1, -1):
                link(nc.vector.tensor_tensor(s, s, w2, ALU.mult))
                link(nc.vector.tensor_scalar(s, s, 1.0 / (2 * j + 1), None, ALU.add))
            link(nc.vector.tensor_tensor(s, s, w, ALU.mult))
            link(nc.vector.scalar_tensor_tensor(out=s, in0=s, scalar=2.0, in1=m, op0=ALU.mult, op1=ALU.add))
            link(nc.vector.tensor_scalar(con["sp4"], s, LRU_C / 2, None, ALU.mult))
            nc.vector.tensor_scalar(con["sp4n"], s, -LRU_C / 2, None, ALU.mult).then_inc(sem["lam_done"], 1)

            def variance(c):
                c0, cn = CH[c]
                wait_unit(dve, ("s", 0, c))
                nc.vector.tensor_scalar(rb[:, c0:c0 + cn], bank(("s", 0, c))[:, 0:cn], 1.0 / D, EPS,
                                        ALU.mult, ALU.add).then_inc(sem["unit_read_dve"], 1)

            def scale_rows(c):
                c0, cn = CH[c]
                dve.wait_ge(sem["std"], c + 1)
                link(nc.vector.reciprocal(rb[:, c0:c0 + cn], rb[:, c0:c0 + cn]))

            def read(u, out, m=P):
                c0, cn = CH[u[-1]]
                wait_unit(dve, u)
                nc.vector.tensor_tensor(out[:, c0:c0 + cn], bank(u)[0:m, 0:cn], rb[0:m, c0:c0 + cn], ALU.mult)\
                  .then_inc(sem["unit_read_dve"], 1)

            def done_reading(u):
                dve.wait_ge(sem["unit_read_dve"], dve_reads.index(u) + 1)

            def conv(f):
                done_reading(("x", f, 2))
                if f >= 2:
                    dve.wait_ge(sem["xc_lo"], f - 1)
                taps = [col("conv_w", TAPS * f + k) for k in range(TAPS)]
                link(nc.vector.tensor_scalar(xc[f % 2], xpad[:, 0:T], taps[0], col("conv_b", f), ALU.mult, ALU.add))
                for k in range(1, TAPS):
                    ins = nc.vector.scalar_tensor_tensor(out=xc[f % 2], in0=xpad[:, k:k + T], scalar=taps[k],
                                                         in1=xc[f % 2], op0=ALU.mult, op1=ALU.add)
                    if k < TAPS - 1:
                        link(ins)
                ins.then_inc(sem["conv"], 1)
                dve.wait_ge(sem["conv"], f + 1)

            def read_gate(f):
                if f >= 2:
                    dve.wait_ge(sem["y_lru"], f - 1)
                for c in range(3):
                    read(("g", f, c), gel[f % 2])

            def recurrence(f):
                for d in range(2):
                    dve.wait_ge(sem["a_sq"], 2 * f + d + 1)
                    nc.vector.scalar_tensor_tensor(out=W[d], in0=S[d], scalar=1.0, in1=W[d], op0=ALU.add, op1=ALU.mult)\
                      .then_inc(sem["var_lru"], 1)
                    link(nc.vector.scalar_tensor_tensor(out=X[d], in0=X[d], scalar=1.0, in1=xc[f % 2],
                                                        op0=ALU.add, op1=ALU.mult))
                for d in range(2):
                    dve.wait_ge(sem["sqrt_lru"], 2 * f + d + 1)
                    link(nc.vector.scalar_tensor_tensor(out=X[d], in0=W[d], scalar=0.5, in1=X[d],
                                                        op0=ALU.mult, op1=ALU.mult))
                    if d == 0:
                        nc.vector.tensor_tensor_scan(S[0], A[0], X[0], 0.0, ALU.mult, ALU.add).then_inc(sem["scanned"], 1)
                    else:
                        nc.vector.tensor_tensor_scan(S[1][:, ::-1], A[1][:, ::-1], X[1][:, ::-1], 0.0,
                                                     ALU.mult, ALU.add).then_inc(sem["scanned"], 1)

            variance(0)
            variance(1)
            scale_rows(0)
            dve.wait_ge(sem["pads"], 2)
            read(("x", 0, 0), xpad[:, 2:])
            scale_rows(1)
            read(("x", 0, 1), xpad[:, 2:])
            variance(2)
            scale_rows(2)
            read(("x", 0, 2), xpad[:, 2:])
            conv(0)
            for f in range(LF):
                if f < LF - 1 and f != 1:
                    pass
                if f == 0:
                    for c in range(3):
                        read(("x", 1, c), xpad[:, 2:])
                    conv(1)
                if f >= 2:
                    for c in range(3):
                        read(("x", f, c), xpad[:, 2:])
                    conv(f)
                read_gate(f)
                recurrence(f)
            for n in range(3):
                for c in range(3):
                    read(("c", n, c), cq[:, n, :])
            for c in range(3):
                read(("k", 0, c), kpe_fm[0], ROPE)

        @block.tensor
        def _(pe):
            def project(kinds, n0):
                for n, _ in enumerate(kinds):
                    pe.wait_ge(sem["w_split"], n0 + n + 1)
                us = [(kind, f, c) for kind, f in kinds for c in range(3)]
                for u in us:
                    wait_bank(pe, u)
                for k in range(KD):
                    if n0 == 0:
                        pe.wait_ge(sem["x_lo"], k + 1)
                    for u in us:
                        n = tiles.index(u[:2])
                        m = ROPE if u[0] == "k" else P
                        c0, cn = CH[u[2]]
                        ins = split_products(nc, bank(u)[0:m, 0:cn], w_h[n % 2][:, k, 0:m], w_l[n % 2][:, k, 0:m],
                                             xn_h[:, k, c0:c0 + cn], xn_l[:, k, c0:c0 + cn], k == 0, k == KD - 1)
                        if k == KD - 1:
                            ins.then_inc(sem["unit_done"], 1)

            for kind, f in order:
                if kind == "x" and f == 1:
                    continue
                if kind == "x" and f == 0:
                    project([("x", 0), ("x", 1)], 0)
                elif kind == "s":
                    pe.wait_ge(sem["ones"], 1)
                    pe.wait_ge(sem["x_acc"], KD)
                    for c, (c0, cn) in enumerate(CH):
                        wait_bank(pe, ("s", 0, c))
                        nc.tensor.matmul(bank(("s", 0, c))[:, 0:cn], con["ones"], acc[:, c0:c0 + cn],
                                         start=True, stop=True).then_inc(sem["unit_done"], 1)
                elif kind == "G":
                    pe.wait_ge(sem["gw_split"], 1)
                    pe.wait_ge(sem["xc_lo"], f + 1)
                    for u in units:
                        if u[:2] != ("G", f):
                            continue
                        _, _, d, w, c = u
                        c0, cn = CH[c]
                        m = 4 * f + 2 * d + w
                        wait_bank(pe, u)
                        split_products(nc, bank(u)[:, 0:cn], gw_h[:, m, :], gw_l[:, m, :], xc_h[:, c0:c0 + cn],
                                       xc_l[:, c0:c0 + cn], True, True).then_inc(sem["unit_done"], 1)
                else:
                    project([(kind, f)], tiles.index((kind, f)))


M_KPE = 53208 - (T + 8)
M_CQ = M_KPE - 3 * T


M_QK = M_A
M_V = M_QK + NT * 2 * HEADS * QK
M_2 = M_V + NT * HEADS * 2 * VD


def qkv_phase(nc, place, con, cq, kpe_fm, qk, v, bank, dram, sem):
    at = M_2
    c_h = place("c_h", at, (3, T), F32R); at += 3 * T
    c_l = place("c_l", at, (3, T), F32R); at += 3 * T
    NQ, NKV = HEADS * QK, HEADS * (NOPE + VD)
    uq_h = place("uq_h", at, (2, NQ), F32R); at += 2 * NQ
    uq_l = place("uq_l", at, (2, NQ), F32R); at += 2 * NQ
    ukv_h = place("ukv_h", at, (NKV,), F32R); at += NKV
    ukv_l = place("ukv_l", at, (NKV,), F32R); at += NKV
    csq = place("csq", at, (3, T)); at += 3 * T
    uq_raw = place("uq_raw", at, (2, NQ))
    kv1 = place("kvs1", at, (HEADS, NOPE + VD)); at += 2 * NQ
    ukv_raw = place("ukv_raw", at, (NKV,)); at += NKV
    sqs = place("squares", at, (1344,)); at += 1344
    kvs = [place("kvs0", at, (HEADS, NOPE + VD)), kv1]; at += NKV
    ra = place("rope_a", at, (2 * HEADS, ROPE)); at += 512
    rp = place("rope_b", at, (2 * HEADS, ROPE)); at += 512
    assert at <= M_CQ, (at, M_CQ)
    qsq = sqs[:, 0:NQ].rearrange("p (h d) -> p h d", h=HEADS)
    ksq = sqs[:, NQ:NQ + HEADS * NOPE].rearrange("p (h d) -> p h d", h=HEADS)
    psq = sqs[:, 1280:1280 + ROPE]
    par, ident, ones, stat = con["par"], con["ident"], con["ones"], con["stat"]
    half = ROPE // 2

    q_ps = bank(0, 2).rearrange("p (b n) -> p b n", b=2)[:, :, 0:NQ // 2]

    def kv_ps(i):
        return bank(2 if i % 2 == 0 else 6, 2)

    def st_ps(i):
        return bank(4 + i % 2, 1)

    def tok(i):
        n, t0 = token_rows(i)
        return slice(t0, t0 + n)

    with nc.Block() as block:
        @block.sync
        def _(sp):
            sp.dma_start(uq_raw, dram["w_uq"].rearrange("(k p) n -> p k n", p=P)).then_inc(sem["uq_in"], 16)
            sp.dma_start(ukv_raw, dram["w_ukv"]).then_inc(sem["ukv_in"], 16)

        @block.gpsimd
        def _(pool):
            for k in range(3):
                nc.gpsimd.tensor_tensor(csq[:, k, :], cq[:, k, :], cq[:, k, :], ALU.mult).then_inc(sem["csq"], 1)
            pool.wait_ge(sem["uq_hi"], 1)
            nc.gpsimd.tensor_tensor(uq_l, uq_raw, f32(uq_h), ALU.subtract).then_inc(sem["uq_lo"], 1)
            pool.wait_ge(sem["ukv_hi"], 1)
            nc.gpsimd.tensor_tensor(ukv_l, ukv_raw, f32(ukv_h), ALU.subtract).then_inc(sem["uq_lo"], 1)
            for i in range(NT):
                n, _ = token_rows(i)
                pool.wait_ge(sem["v_hi"], i + 1)
                vt = v[0:n, i, :].rearrange("p (h d) -> p h d", h=HEADS)
                nc.gpsimd.tensor_tensor(vt[:, :, VD:], kvs[i % 2][0:n, :, NOPE:], f32(vt[:, :, 0:VD]), ALU.subtract)\
                  .then_inc(sem["v_lo"], 1)
                pool.wait_ge(sem["gained"], i + 1)
                if i:
                    pool.wait_ge(sem["roped"], 4 * i)
                x = qk[0:n, i, :].rearrange("p (h d) -> p h d", d=QK)[:, :, NOPE:QK]
                cs = con["rope_c"][0:n, i, :].unsqueeze(1).broadcast_to((n, 2 * HEADS, ROPE))
                sn = con["rope_s"][0:n, i, :].unsqueeze(1).broadcast_to((n, 2 * HEADS, ROPE))
                nc.gpsimd.tensor_tensor(ra[0:n], x, cs, ALU.mult).then_inc(sem["roped"], 1)
                nc.gpsimd.tensor_tensor(rp[0:n, :, 0:half], x[:, :, half:], sn[:, :, 0:half], ALU.mult)\
                  .then_inc(sem["roped"], 1)
                nc.gpsimd.tensor_tensor(rp[0:n, :, half:], x[:, :, 0:half], sn[:, :, half:], ALU.mult)\
                  .then_inc(sem["roped"], 1)
                pool.wait_ge(sem["roped"], 4 * i + 3)
                nc.gpsimd.tensor_tensor(x, ra[0:n], rp[0:n], ALU.add).then_inc(sem["roped"], 1)

        @block.scalar
        def _(act):
            for k in range(3):
                g = par[:, COLS["q_g"] + k:COLS["q_g"] + k + 1]
                nc.scalar.activation(c_h[:, k, :], cq[:, k, :], ACT.Copy, scale=g).then_inc(sem["c_hi"], 1)
            act.wait_ge(sem["uq_in"], 16)
            nc.scalar.activation(uq_h, uq_raw, ACT.Copy).then_inc(sem["uq_hi"], 1)
            act.wait_ge(sem["ukv_in"], 16)
            nc.scalar.activation(ukv_h, ukv_raw, ACT.Copy).then_inc(sem["ukv_hi"], 1)

            def kv_std(i):
                n, _ = token_rows(i)
                act.wait_ge(sem["kv_var"], i + 1)
                nc.scalar.activation(stat[0:n, i % 2, 1:2], stat[0:n, i % 2, 1:2], ACT.Sqrt).then_inc(sem["kv_std"], 1)

            kv_std(0)
            for i in range(NT):
                n, _ = token_rows(i)
                st = stat[0:n, i % 2]
                act.wait_ge(sem["q_mm"], i + 1)
                if i:
                    act.wait_ge(sem["summed"], 3 * i)
                nc.scalar.activation(qsq[0:n].rearrange("p (b h) d -> p b (h d)", b=2), q_ps[0:n], ACT.Square)\
                  .then_inc(sem["squares"], 1)
                act.wait_ge(sem["kv_mm"], i + 1)
                act.wait_ge(sem["kv_rstd"], i + 1)
                if i == 1:
                    act.wait_ge(sem["uq_lo"], 2)
                if i >= 2:
                    act.wait_ge(sem["v_lo"], i - 1)
                    act.wait_ge(sem["k_scaled"], i - 1)
                nc.scalar.activation(kvs[i % 2][0:n].rearrange("p h d -> p (h d)"), kv_ps(i)[0:n], ACT.Copy,
                                     scale=st[:, 2:3]).then_inc(sem["kvs"], 1)
                act.wait_ge(sem["kvs"], i + 1)
                nc.scalar.activation(ksq[0:n], kvs[i % 2][0:n, :, 0:NOPE], ACT.Square).then_inc(sem["squares"], 1)
                nc.scalar.activation(psq[0:n], st_ps(i)[0:n, 32:32 + ROPE], ACT.Square).then_inc(sem["squares"], 1)
                vt = v[0:n, i, :].rearrange("p (h d) -> p h d", h=HEADS)
                nc.scalar.activation(vt[:, :, 0:VD], kvs[i % 2][0:n, :, NOPE:], ACT.Copy).then_inc(sem["v_hi"], 1)
                if i + 1 < NT:
                    kv_std(i + 1)
                act.wait_ge(sem["head_var"], i + 1)
                nc.scalar.activation(st[:, 16:32], st[:, 16:32], ACT.Sqrt).then_inc(sem["head_std"], 1)

        @block.vector
        def _(dve):
            link = chain(dve, sem["dve_link2"])
            for k in range(3):
                g = par[:, COLS["q_g"] + k:COLS["q_g"] + k + 1]
                dve.wait_ge(sem["c_hi"], k + 1)
                nc.vector.scalar_tensor_tensor(out=c_l[:, k, :], in0=cq[:, k, :], scalar=g, in1=f32(c_h[:, k, :]),
                                               op0=ALU.mult, op1=ALU.subtract).then_inc(sem["c_lo"], 1)

            def latent_stats(i):
                n, _ = token_rows(i)
                dve.wait_ge(sem["st_mm"], i + 1)
                link(nc.vector.tensor_scalar(stat[0:n, i % 2, 0:1], st_ps(i)[0:n, 0:1], EPS / QL, EPS * EPS,
                                             ALU.mult, ALU.add))
                nc.vector.tensor_scalar(stat[0:n, i % 2, 1:2], st_ps(i)[0:n, 2:3], 1.0 / KVL, EPS, ALU.mult, ALU.add)\
                  .then_inc(sem["kv_var"], 1)

            def kv_rstd(i):
                n, _ = token_rows(i)
                dve.wait_ge(sem["kv_std"], i + 1)
                nc.vector.reciprocal(stat[0:n, i % 2, 2:3], stat[0:n, i % 2, 1:2]).then_inc(sem["kv_rstd"], 1)

            latent_stats(0)
            kv_rstd(0)
            for i in range(NT):
                n, _ = token_rows(i)
                st = stat[0:n, i % 2]
                if i + 1 < NT:
                    latent_stats(i + 1)
                dve.wait_ge(sem["squares"], 3 * i + 1)
                nc.vector.tensor_reduce(st[:, 16:24], qsq[0:n], AX.X, ALU.add).then_inc(sem["summed"], 1)
                dve.wait_ge(sem["squares"], 3 * i + 3)
                nc.vector.tensor_reduce(st[:, 24:32], ksq[0:n], AX.X, ALU.add).then_inc(sem["summed"], 1)
                nc.vector.tensor_reduce(st[:, 3:4], psq[0:n], AX.X, ALU.add).then_inc(sem["summed"], 1)
                if i + 1 < NT:
                    kv_rstd(i + 1)
                dve.wait_ge(sem["summed"], 3 * i + 3)
                link(nc.vector.tensor_scalar(st[:, 4:5], st[:, 3:4], QK * EPS, None, ALU.add))
                link(nc.vector.tensor_scalar(st[:, 16:24], st[:, 16:24], 1.0 / QK, st[:, 0:1], ALU.mult, ALU.add))
                nc.vector.tensor_scalar(st[:, 24:32], st[:, 24:32], st[:, 4:5], 1.0 / QK, ALU.add, ALU.mult)\
                  .then_inc(sem["head_var"], 1)
                dve.wait_ge(sem["head_std"], i + 1)
                link(nc.vector.reciprocal(st[:, 32:48], st[:, 16:32]))
                x = qk[0:n, i, :].rearrange("p (h d) -> p h d", d=QK)
                xq = x[:, 0:HEADS].rearrange("p (b h) d -> p b h d", b=2)
                for b in range(2):
                    rq = st[:, 32 + 4 * b:36 + 4 * b].unsqueeze(2).broadcast_to((n, 4, QK))
                    ins = nc.vector.tensor_tensor(xq[:, b], q_ps[0:n, b].rearrange("p (h d) -> p h d", h=4), rq, ALU.mult)
                    ins.then_inc(sem["q_scaled"], 1)
                rk = st[:, 40:48].unsqueeze(2)
                link(nc.vector.tensor_tensor(x[:, HEADS:, 0:NOPE], kvs[i % 2][0:n, :, 0:NOPE],
                                             rk.broadcast_to((n, HEADS, NOPE)), ALU.mult))
                kp = st_ps(i)[0:n, 32:32 + ROPE].unsqueeze(1).broadcast_to((n, HEADS, ROPE))
                nc.vector.tensor_tensor(x[:, HEADS:, NOPE:QK], kp, rk.broadcast_to((n, HEADS, ROPE)), ALU.mult)\
                  .then_inc(sem["k_scaled"], 1)
                dve.wait_ge(sem["k_scaled"], i + 1)
                dve.wait_ge(sem["q_scaled"], 2 * i + 2)
                x4 = qk[0:n, i, :].rearrange("p (g h d) -> p g h d", g=2, h=HEADS)
                gg = con["gqk"][0:n].unsqueeze(2).broadcast_to((n, 2, HEADS, QK))
                nc.vector.tensor_tensor(x4, x4, gg, ALU.mult).then_inc(sem["gained"], 1)

        @block.tensor
        def _(pe):
            pe.wait_ge(sem["con_in"], 64)
            for i in range(NT):
                n, _ = token_rows(i)
                if i == 0:
                    pe.wait_ge(sem["csq"], 3)
                if i >= 2:
                    pe.wait_ge(sem["k_scaled"], i - 1)
                st = st_ps(i)[0:n]
                for k in range(2):
                    nc.tensor.matmul(st[:, 0:2], csq[:, k, tok(i)], ones[:, 0:2], start=k == 0, stop=k == 1)
                nc.tensor.matmul(st[:, 2:4], csq[:, 2, tok(i)], ones[:, 0:2], start=True, stop=True)
                nc.tensor.transpose(st[:, 32:32 + ROPE], kpe_fm[:, tok(i)], ident[0:ROPE, 0:ROPE]).then_inc(sem["st_mm"], 1)
                if i == 0:
                    pe.wait_ge(sem["c_lo"], 3)
                    pe.wait_ge(sem["uq_lo"], 2)
                if i:
                    pe.wait_ge(sem["q_scaled"], 2 * i)
                for b in range(2):
                    cols = slice(b * NQ // 2, (b + 1) * NQ // 2)
                    for k in range(2):
                        ins = split_products(nc, q_ps[0:n, b], c_h[:, k, tok(i)], c_l[:, k, tok(i)],
                                             uq_h[:, k, cols], uq_l[:, k, cols], k == 0, k == 1)
                ins.then_inc(sem["q_mm"], 1)
                if i >= 2:
                    pe.wait_ge(sem["kvs"], i - 1)
                for b in range(2):
                    cols = slice(b * NKV // 2, (b + 1) * NKV // 2)
                    ins = split_products(nc, kv_ps(i)[0:n, cols], c_h[:, 2, tok(i)], c_l[:, 2, tok(i)],
                                         ukv_h[:, cols], ukv_l[:, cols], True, True)
                ins.then_inc(sem["kv_mm"], 1)


M_YM = 53208 - (KD // 2) * (SEQ + 2) - 8
M_YM -= M_YM % 8
KPAD = 1152
SLOTS = NT


def attention_phase(nc, place, con, qk, v, ym, bank, dram, sem):
    at = M_2
    q_h = [place(f"q_h{b}", at + T * b, (T,), F32R, QK + 1) for b in range(2)]; at += 2 * T
    q_l = [place(f"q_l{b}", at + T * b, (T,), F32R, QK) for b in range(2)]; at += 2 * T
    k_h = [place(f"k_h{b}", at + KPAD * b, (KPAD,), F32R, QK + 1) for b in range(2)]; at += 2 * KPAD
    k_l = [place(f"k_l{b}", at + KPAD * b, (KPAD,), F32R, QK) for b in range(2)]; at += 2 * KPAD
    e_h = [place(f"e_h{b}", at + SEQ * b, (SEQ,), F32R) for b in range(2)]; at += 2 * SEQ
    e_l = [place(f"e_l{b}", at + SEQ * b, (SEQ,), F32R) for b in range(2)]; at += 2 * SEQ
    e_f = [place(f"e_f{b}", at + SEQ * b, (SEQ,)) for b in range(2)]; at += 2 * SEQ
    es = place("esum", at, (SEQ,))
    sel = place("sel", at, (XT, VD)); at += SEQ
    es_h = place("esum_h", at, (SEQ,), F32R); at += SEQ
    es_l = place("esum_l", at, (SEQ,), F32R); at += SEQ
    osum = place("osum", at, (SEQ,), parts=VD); at += SEQ
    sel_r = place("sel_r", at, (XT, VD), F32R, 40); at += XT * VD
    rl_r = place("rl_r", at, (P,), F32R, 40); at += P
    ones_r = place("ones_r", at, (VD,), F32R); at += VD
    NX = 2 * NT
    x_f = place("x_f", at, (HEADS, NX)); at += HEADS * NX
    assert NX * HEADS % 8 == 0
    x_h = place("x_h", at, (HEADS, NX), F32R); at += HEADS * NX
    x_l = place("x_l", at, (HEADS, NX), F32R); at += HEADS * NX
    assert at <= M_YM, (at, M_YM)
    SCALE = float(np.float32(1.0) / np.sqrt(np.float32(QK)))
    mx = con["lam_t"].rearrange("p a b -> p (a b)")
    mx_a, mx_b, rl, x_o = mx[:, 0:NT], mx[:, NT:2 * NT], mx[:, 24:24 + XT], mx[:, 32:48]
    x_rl = con["stat"].rearrange("p a b -> p (a b)")[:, 0:16]
    ident = con["ident"]

    def s_ps(g):
        return bank(2 * (g % 2), 2)

    o_ps, side = bank(4, 2), bank(6, 2)

    def slot_jobs(h, s):
        prep = {0: [("tq", 0), ("tk", 0)], 1: [("tm", 0)], 2: [("a", 0), ("a", 1)], 3: [("a", 2), ("a", 3)],
                4: [("a", 4), ("a", 5)], 5: [("a", 6), ("a", 7)], 6: [("am", 0), ("ax", 0)], 7: [("r", 0), ("rm", 0)]}
        fin = {1: [("l", 0)], 2: [("rt", 0)], 3: [("b", 0)]}
        jobs = []
        if h + 1 < HEADS:
            jobs += [(kind, h + 1, i) for kind, i in prep.get(s, [])]
        if h >= 1:
            jobs += [(kind, h - 1, i) for kind, i in fin.get(s, [])]
        if 0 <= h < HEADS and s == 8:
            jobs.append(("x", h, 0))
        return jobs

    steps = [(h, s) for h in range(-1, HEADS + 1) for s in range(SLOTS)]
    jobs = [j for h, s in steps for j in slot_jobs(h, s)]
    by_act = {"r", "rm", "x"}
    number = {j: n for n, j in enumerate(jobs)}

    def wait_read(eng, j):
        same = [i for i in jobs[:number[j] + 1] if (i[0] in by_act) == (j[0] in by_act)]
        eng.wait_ge(sem["side_read_act" if j[0] in by_act else "side_read_dve"], len(same))

    def attend(h, s):
        return 0 <= h < HEADS

    with nc.Block() as block:
        @block.sync
        def _(sp):
            sp.dma_start(sel, dram["sel"]).then_inc(sem["sel_in"], 16)

        @block.gpsimd
        def _(pool):
            sets = [0]

            def settle(ins):
                sets[0] += 1
                ins.then_inc(sem["b_set"], 1)
                pool.wait_ge(sem["b_set"], sets[0])

            for b in range(2):
                settle(nc.gpsimd.memset(f32(k_h[b][:, T:]), 0.0))
                settle(nc.gpsimd.memset(f32(k_l[b][:, T:]), 0.0))
                settle(nc.gpsimd.memset(f32(k_h[b][QK:QK + 1, 0:T]), 1.0))
            settle(nc.gpsimd.memset(f32(rl_r), 0.0))
            settle(nc.gpsimd.tensor_copy(ones_r, con["ones"][:, 0:VD]))
            pool.wait_ge(sem["sel_in"], 16)
            settle(nc.gpsimd.tensor_copy(sel_r, sel[0:40]))
            for h in range(HEADS):
                for s in range(SLOTS):
                    g = SLOTS * h + s
                    n = P if s < XT else META
                    pool.wait_ge(sem["e_full"], g + 1)
                    if s == 0:
                        if h:
                            pool.wait_ge(sem["es_lo"], h)
                        nc.gpsimd.tensor_copy(es, e_f[g % 2]).then_inc(sem["e_summed"], 1)
                    else:
                        pool.wait_ge(sem["e_summed"], g)
                        nc.gpsimd.tensor_tensor(es[0:n], es[0:n], e_f[g % 2][0:n], ALU.add).then_inc(sem["e_summed"], 1)

        @block.scalar
        def _(act):
            def job(j):
                kind, h, i = j
                b = h % 2
                if kind in ("tq", "tk", "tm", "rt"):
                    act.wait_ge(sem["side_done"], number[j] + 1)
                    if kind == "tq":
                        if h >= 2:
                            act.wait_ge(sem["side_done"], number[("x", h - 2, 0)] + 1)
                        ins = nc.scalar.activation(q_h[b][0:QK, 0:SEQ], side[0:QK], ACT.Copy)
                    elif kind == "tk":
                        ins = nc.scalar.activation(k_h[b][0:QK, 0:SEQ], side[0:QK], ACT.Copy)
                    elif kind == "tm":
                        nc.scalar.activation(q_h[b][0:QK, SEQ:T], side[0:QK, 0:META], ACT.Copy).then_inc(sem["side_hi"], 1)
                        ins = nc.scalar.activation(k_h[b][0:QK, SEQ:T], side[0:QK, META:2 * META], ACT.Copy)
                    else:
                        ins = nc.scalar.activation(rl_r[0:XT], side[0:XT, 0:P], ACT.Copy)
                    ins.then_inc(sem["side_hi"], 1)
                elif kind == "r":
                    act.wait_ge(sem["side_done"], number[j] + 1)
                    nc.scalar.activation(q_h[b][QK:QK + 1, 0:SEQ], side[0:1], ACT.Copy, scale=-1.0)\
                      .then_inc(sem["side_read_act"], 1)
                elif kind == "rm":
                    act.wait_ge(sem["side_done"], number[j] + 1)
                    nc.scalar.activation(q_h[b][QK:QK + 1, SEQ:T], side[0:1, 0:META], ACT.Copy, scale=-1.0)\
                      .then_inc(sem["side_read_act"], 1)
                elif kind == "x":
                    act.wait_ge(sem["side_done"], number[j] + 1)
                    nc.scalar.activation(x_f[:, h, :], side[:, 0:NX], ACT.Exp, scale=SCALE).then_inc(sem["x_exp"], 1)
                    nc.scalar.activation(x_h[:, h, :], side[:, 0:NX], ACT.Exp, scale=SCALE).then_inc(sem["side_read_act"], 1)

            act.wait_ge(sem["b_set"], 9)
            for h, s in steps:
                js = slot_jobs(h, s)
                for j in js[:1]:
                    job(j)
                if attend(h, s):
                    g = SLOTS * h + s
                    n = P if s < XT else META
                    act.wait_ge(sem["s_done"], g + 1)
                    if g >= 2:
                        act.wait_ge(sem["e_summed"], g - 1)
                        act.wait_ge(sem["e_lo"], g - 1)
                        act.wait_ge(sem["pv_done"], g - 1)
                    nc.scalar.activation(e_f[g % 2][0:n], s_ps(g)[0:n], ACT.Exp, scale=SCALE).then_inc(sem["e_full"], 1)
                    nc.scalar.activation(e_h[g % 2][0:n], s_ps(g)[0:n], ACT.Exp, scale=SCALE).then_inc(sem["e_hi"], 1)
                if h >= 1 and s == 0:
                    act.wait_ge(sem["pv_done"], SLOTS * h)
                    if h >= 2:
                        wait_read(act, ("b", h - 2, 0))
                    nc.scalar.activation(osum, o_ps[VD:P], ACT.Copy).then_inc(sem["o_low"], 1)
                    act.wait_ge(sem["e_summed"], SLOTS * h)
                    if h >= 2:
                        act.wait_ge(sem["side_done"], number[("l", h - 2, 0)] + 1)
                    nc.scalar.activation(es_h, es, ACT.Copy).then_inc(sem["es_hi"], 1)
                for j in js[1:]:
                    job(j)
            act.wait_ge(sem["xo_mm"], 1)
            nc.scalar.activation(x_o[0:VD], bank(4)[VD:P, 0:16], ACT.Copy).then_inc(sem["xo_low"], 1)

        @block.vector
        def _(dve):
            link = chain(dve, sem["dve_link3"])
            n_hi = [0]

            def job(j):
                kind, h, i = j
                b = h % 2
                if kind in ("tq", "tk", "tm", "rt"):
                    n_hi[0] += 2 if kind == "tm" else 1
                    dve.wait_ge(sem["side_hi"], n_hi[0])
                elif kind in ("l", "b", "a", "ax", "am"):
                    dve.wait_ge(sem["side_done"], number[j] + 1)
                if kind == "tq":
                    ins = nc.vector.tensor_tensor(q_l[b][:, 0:SEQ], side[0:QK], f32(q_h[b][0:QK, 0:SEQ]), ALU.subtract)
                elif kind == "tk":
                    ins = nc.vector.tensor_tensor(k_l[b][:, 0:SEQ], side[0:QK], f32(k_h[b][0:QK, 0:SEQ]), ALU.subtract)
                elif kind == "tm":
                    nc.vector.tensor_tensor(q_l[b][:, SEQ:T], side[0:QK, 0:META], f32(q_h[b][0:QK, SEQ:T]), ALU.subtract)\
                      .then_inc(sem["q_low_meta"], 1)
                    ins = nc.vector.tensor_tensor(k_l[b][:, SEQ:T], side[0:QK, META:2 * META], f32(k_h[b][0:QK, SEQ:T]),
                                                  ALU.subtract)
                elif kind == "a":
                    ins = nc.vector.tensor_reduce(mx_a[:, i:i + 1], side, AX.X, ALU.max)
                elif kind == "ax":
                    link(nc.vector.tensor_reduce(mx_a[0:META, XT:NT], side[0:META], AX.X, ALU.max))
                    ins = nc.vector.tensor_tensor(mx_a[0:META, XT:NT], mx_a[0:META, XT:NT], mx_b[0:META, XT:NT], ALU.max)
                elif kind == "am":
                    s3 = side[:, 0:XT * META].rearrange("p (i n) -> p i n", n=META)
                    link(nc.vector.tensor_reduce(mx_b[:, 0:XT], s3, AX.X, ALU.max))
                    link(nc.vector.tensor_reduce(mx_b[0:META, XT:NT], side[0:META, XT * META:NT * META], AX.X, ALU.max))
                    wait_read(dve, ("a", h, 7))
                    ins = nc.vector.tensor_tensor(mx_a[:, 0:XT], mx_a[:, 0:XT], mx_b[:, 0:XT], ALU.max)
                elif kind == "l":
                    ins = nc.vector.reciprocal(rl, side[:, 0:2 * XT].rearrange("p (i t) -> p i t", t=2)[:, :, 0])
                elif kind == "rt":
                    ins = nc.vector.tensor_tensor(rl_r[32:32 + XT], side[0:XT, 0:P], f32(rl_r[0:XT]), ALU.subtract)
                elif kind == "b":
                    dve.wait_ge(sem["o_sum"], h + 1)
                    o = VD * (h % 2)
                    ins = nc.vector.tensor_tensor(ym[o:o + VD, h // 2, 0:SEQ], side[0:VD], osum, ALU.mult)
                else:
                    return
                ins.then_inc(sem["side_read_dve"], 1)

            dve.wait_ge(sem["b_set"], 9)
            for h, s in steps:
                js = slot_jobs(h, s)
                for j in js[:1]:
                    job(j)
                if h >= 1 and s == 0:
                    dve.wait_ge(sem["o_low"], h)
                    nc.vector.tensor_tensor(osum, o_ps[0:VD], osum, ALU.add).then_inc(sem["o_sum"], 1)
                    dve.wait_ge(sem["es_hi"], h)
                    nc.vector.tensor_tensor(es_l, es, f32(es_h), ALU.subtract).then_inc(sem["es_lo"], 1)
                if attend(h, s):
                    g = SLOTS * h + s
                    n = P if s < XT else META
                    dve.wait_ge(sem["e_hi"], g + 1)
                    if g >= 2:
                        dve.wait_ge(sem["pv_done"], g - 1)
                    nc.vector.tensor_tensor(e_l[g % 2][0:n], e_f[g % 2][0:n], f32(e_h[g % 2][0:n]), ALU.subtract)\
                      .then_inc(sem["e_lo"], 1)
                for j in js[1:]:
                    job(j)
                if h == HEADS and s == 0:
                    wait_read(dve, ("x", HEADS - 1, 0))
                    nc.vector.tensor_tensor(x_l, x_f, f32(x_h), ALU.subtract).then_inc(sem["x_lo2"], 1)
            dve.wait_ge(sem["xo_mm"], 2)
            link(nc.vector.reciprocal(x_rl[0:VD], bank(0)[0:VD, 0:16]))
            dve.wait_ge(sem["xo_low"], 1)
            link(nc.vector.tensor_tensor(x_o[0:VD], bank(4)[0:VD, 0:16], x_o[0:VD], ALU.add))
            xo3 = x_o[0:VD].rearrange("p (h c) -> p h c", c=2)
            xr3 = x_rl[0:VD].rearrange("p (h c) -> p h c", c=2)
            for o in range(2):
                ins = nc.vector.tensor_tensor(ym[VD * o:VD * o + VD, :, SEQ:SEQ + 2], xo3[:, o::2], xr3[:, o::2], ALU.mult)
            ins.then_inc(sem["x_y"], 1)

        @block.tensor
        def _(pe):
            def tile_of(i):
                return slice(P * i, P * i + P) if i < XT else slice(SEQ, T)

            def job(j):
                kind, h, i = j
                b = h % 2
                n = number[j]
                if n:
                    wait_read(pe, jobs[n - 1])
                if kind in ("tq", "tk"):
                    c0 = QK * (h + (HEADS if kind == "tk" else 0))
                    for t in range(XT):
                        ins = nc.tensor.transpose(side[0:QK, P * t:P * t + P], qk[:, t, c0:c0 + QK], ident)
                elif kind == "tm":
                    for w in range(2):
                        c0 = QK * (h + HEADS * w)
                        ins = nc.tensor.transpose(side[0:QK, META * w:META * w + META], qk[0:META, XT, c0:c0 + QK],
                                                  ident[0:META, 0:META])
                elif kind in ("a", "ax"):
                    t = i if kind == "a" else XT
                    m = P if kind == "a" else META
                    for c in range(2):
                        ins = nc.tensor.matmul(side[0:m, 512 * c:512 * c + 512], q_h[b][0:QK, tile_of(t)],
                                               k_h[b][0:QK, 512 * c:512 * c + 512], start=True, stop=True)
                elif kind == "am":
                    for t in range(NT):
                        m = P if t < XT else META
                        ins = nc.tensor.matmul(side[0:m, META * t:META * t + META], q_h[b][0:QK, tile_of(t)],
                                               k_h[b][0:QK, SEQ:T], start=True, stop=True)
                elif kind == "r":
                    wait_read(pe, ("ax", h, 0))
                    for t in range(XT):
                        ins = nc.tensor.transpose(side[0:1, P * t:P * t + P], mx_a[:, t:t + 1], ident)
                elif kind == "rm":
                    ins = nc.tensor.transpose(side[0:1, 0:META], mx_a[0:META, XT:NT], ident[0:META, 0:META])
                elif kind == "l":
                    pe.wait_ge(sem["es_lo"], h + 1)
                    for t in range(XT):
                        nc.tensor.matmul(side[:, 2 * t:2 * t + 2], es_h[:, tile_of(t)], ones_r[:, 0:2], start=True, stop=False)
                        ins = nc.tensor.matmul(side[:, 2 * t:2 * t + 2], es_l[:, tile_of(t)], ones_r[:, 0:2],
                                               start=False, stop=True)
                elif kind == "rt":
                    wait_read(pe, ("l", h, 0))
                    ins = nc.tensor.transpose(side[0:XT, 0:P], rl, ident)
                elif kind == "b":
                    wait_read(pe, ("rt", h, 0))
                    for t in range(XT):
                        ins = nc.tensor.matmul(side[0:VD, tile_of(t)], sel_r[:, t, :], rl_r, start=True, stop=True)
                elif kind == "x":
                    for t in range(NT):
                        ks = slice(P * t, P * t + P)
                        ins = scores(side[:, 2 * t:2 * t + 2], b, ks, slice(T - 2, T))
                ins.then_inc(sem["side_done"], 1)

            def scores(out, b, ks, qs):
                nc.tensor.matmul(out, k_h[b][:, ks], q_h[b][:, qs], start=True, stop=False)
                nc.tensor.matmul(out, k_h[b][0:QK, ks], q_l[b][:, qs], start=False, stop=False)
                return nc.tensor.matmul(out, k_l[b][:, ks], q_h[b][0:QK, qs], start=False, stop=True)

            def pv(g):
                h, s = divmod(g, SLOTS)
                n = P if s < XT else META
                pe.wait_ge(sem["e_lo"], g + 1)
                if s == 0 and h:
                    pe.wait_ge(sem["o_sum"], h)
                vt = v[0:n, s, 2 * VD * h:2 * VD * (h + 1)]
                for c in range(2):
                    cs = slice(512 * c, 512 * c + 512)
                    nc.tensor.matmul(o_ps[:, cs], vt, e_h[g % 2][0:n, cs], start=s == 0, stop=False)
                    ins = nc.tensor.matmul(o_ps[:, cs], vt, e_l[g % 2][0:n, cs], start=False, stop=s == XT)
                ins.then_inc(sem["pv_done"], 1)

            pe.wait_ge(sem["b_set"], 9)
            for h, s in steps:
                js = slot_jobs(h, s)
                g = SLOTS * h + s
                if attend(h, s):
                    b = h % 2
                    if s == 0:
                        wait_read(pe, ("rm", h, 0))
                    n = P if s < XT else META
                    if g >= 2:
                        pe.wait_ge(sem["e_hi"], g - 1)
                    ks = slice(P * s, P * s + n)
                    for c in range(2):
                        ins = scores(s_ps(g)[0:n, 512 * c:512 * c + 512], b, ks, slice(512 * c, 512 * c + 512))
                    ins.then_inc(sem["s_done"], 1)
                for j in js[:1]:
                    job(j)
                if 1 <= g <= HEADS * SLOTS:
                    pv(g - 1)
                for j in js[1:]:
                    job(j)
            pe.wait_ge(sem["x_lo2"], 1)
            pe.wait_ge(sem["o_sum"], HEADS)
            for h in range(HEADS):
                for t in range(NT):
                    n = P if t < XT else META
                    vt = v[0:n, t, 2 * VD * h:2 * VD * (h + 1)]
                    cs = slice(2 * t, 2 * t + 2)
                    nc.tensor.matmul(bank(4)[:, 2 * h:2 * h + 2], vt, x_h[0:n, h, cs], start=t == 0, stop=False)
                    ins = nc.tensor.matmul(bank(4)[:, 2 * h:2 * h + 2], vt, x_l[0:n, h, cs], start=False, stop=t == XT)
            ins.then_inc(sem["xo_mm"], 1)
            for h in range(HEADS):
                for t in range(NT):
                    n = P if t < XT else META
                    cs = slice(2 * t, 2 * t + 2)
                    nc.tensor.matmul(bank(0)[0:VD, 2 * h:2 * h + 2], ones_r[0:n], x_h[0:n, h, cs], start=t == 0, stop=False)
                    ins = nc.tensor.matmul(bank(0)[0:VD, 2 * h:2 * h + 2], ones_r[0:n], x_l[0:n, h, cs],
                                           start=False, stop=t == XT)
            ins.then_inc(sem["xo_mm"], 1)


Q2 = SEQ + 2
M_H = M_A
M_HN = M_H + XT * D
M_HNL = M_HN + KD * Q2
M_3 = M_HNL + KD * Q2


def out_phase(nc, place, con, yl, ym, h, hn_h, hn_l, bank, dram, sem):
    half = D // 2
    at = M_3
    wo_h = [place("wo_h0", M_HN, (KD, half), F32R), place("wo_h1", at, (KD, half), F32R)]; at += KD * half
    wo_l = [place("wo_l0", M_HN + KD * half, (KD, half), F32R), place("wo_l1", at, (KD, half), F32R)]; at += KD * half
    ys_at = M_HN + 2 * KD * half
    ysum = [place(f"ysum{w}", ys_at + (Q2 + 6) * w, (Q2,)) for w in range(2)]
    ysq = [place(f"ysq{w}", ys_at + (Q2 + 6) * (2 + w), (Q2,)) for w in range(2)]
    assert ys_at + 4 * (Q2 + 6) <= M_3
    y_h = [place(f"y_h{b}", at + 2048 * b, (KD, P), F32R) for b in range(2)]
    y_l = [place(f"y_l{b}", at + 2048 * b + 1024, (KD, P), F32R) for b in range(2)]; at += 4096
    raw = [place(f"wo_raw{b}", at + half * b, (half,)) for b in range(4)]; at += 4 * half
    hn = place("hn", at, (D,)); at += D
    fg = place("ffn_g", at, (D,)); at += D
    hm = place("h_meta", at, (D,), parts=2); at += D
    junk = place("h_sq", at, (D,)); at += D
    assert at <= M_YM, (at, M_YM)
    par, ident, ones = con["par"], con["ident"], con["ones"]
    stat = con["stat"].rearrange("p a b -> p (a b)")
    r_y, ss2, r2 = stat[:, 0:2 * NT], stat[:, 32:32 + NT], stat[:, 48:48 + NT]
    side = bank(6, 2)

    def rows(i):
        return P if i < XT else 2

    def cols(i):
        return slice(2 + P * i, 2 + P * i + P) if i < XT else slice(0, 2)

    def yl_cols(i):
        return slice(META + P * i, META + P * i + P) if i < XT else slice(META - 2, META)

    def ym_cols(i):
        return slice(P * i, P * i + P) if i < XT else slice(SEQ, Q2)

    units = [(c, i) for c in range(2) for i in [XT] + list(range(XT))]

    def res(i):
        return h[:, i, :] if i < XT else hm

    with nc.Block() as block:
        @block.sync
        def _(sp):
            for c in range(2):
                for k in range(KD):
                    m = KD * c + k
                    if m >= 4:
                        sp.wait_ge(sem["wo_lo"], m - 3)
                    sp.dma_start(raw[m % 4], dram["w_out"][P * k:P * k + P, half * c:half * c + half])\
                      .then_inc(sem["wo_in"][m % 4], 16)
                if c == 0:
                    sp.dma_start(hm, dram["meta_tm"][META - 2:META, :]).then_inc(sem["res_in"], 16)
                    sp.dma_start(fg, dram["ffn_g"]).then_inc(sem["res_in"], 16)
                    for i in range(XT):
                        sp.dma_start(h[:, i, :], dram["x_tm"][P * i:P * i + P, :]).then_inc(sem["res_in"], 16)

        @block.gpsimd
        def _(pool):
            for u, (c, i) in enumerate(units):
                n = rows(i)
                pool.wait_ge(sem["y_hi"], 2 * u + 1)
                nc.gpsimd.tensor_tensor(y_l[u % 2][:, 0:LF, 0:n], yl[:, :, yl_cols(i)], f32(y_h[u % 2][:, 0:LF, 0:n]),
                                        ALU.subtract).then_inc(sem["y_lo"], 1)
                pool.wait_ge(sem["y_hi"], 2 * u + 2)
                nc.gpsimd.tensor_tensor(y_l[u % 2][:, LF:, 0:n], ym[:, :, ym_cols(i)], f32(y_h[u % 2][:, LF:, 0:n]),
                                        ALU.subtract).then_inc(sem["y_lo"], 1)

        @block.scalar
        def _(act):
            def split_y(u):
                c, i = units[u]
                n = rows(i)
                if u >= 2:
                    act.wait_ge(sem["wo_mm"], u - 1)
                nc.scalar.activation(y_h[u % 2][:, 0:LF, 0:n], yl[:, :, yl_cols(i)], ACT.Copy).then_inc(sem["y_hi"], 1)
                nc.scalar.activation(y_h[u % 2][:, LF:, 0:n], ym[:, :, ym_cols(i)], ACT.Copy).then_inc(sem["y_hi"], 1)

            def split_w(m):
                k = m % KD
                act.wait_ge(sem["wo_in"][m % 4], 16 * (m // 4 + 1))
                g = par[:, COLS["out_g"] + k:COLS["out_g"] + k + 1]
                nc.scalar.activation(wo_h[m // KD][:, k, :], raw[m % 4], ACT.Copy, scale=g).then_inc(sem["wo_hi"], 1)

            split_y(0)
            split_y(1)
            for k in range(KD):
                split_w(k)
            for k in range(KD):
                w = k // LF
                if k >= 2:
                    act.wait_ge(sem["ysum"], k - 1)
                if w == 0:
                    nc.scalar.activation(ysq[k % 2][:, 0:2], yl[:, k, META - 2:META], ACT.Square).then_inc(sem["ysq"], 1)
                    nc.scalar.activation(ysq[k % 2][:, 2:], yl[:, k, META:], ACT.Square).then_inc(sem["ysq"], 1)
                else:
                    nc.scalar.activation(ysq[k % 2][:, 0:2], ym[:, k - LF, SEQ:], ACT.Square).then_inc(sem["ysq"], 1)
                    nc.scalar.activation(ysq[k % 2][:, 2:], ym[:, k - LF, 0:SEQ], ACT.Square).then_inc(sem["ysq"], 1)
            act.wait_ge(sem["y_var"], 2)
            nc.scalar.activation(r_y[:, 0:2 * XT], r_y[:, 0:2 * XT], ACT.Sqrt).then_inc(sem["y_std"], 1)
            nc.scalar.activation(r_y[0:2, 2 * XT:], r_y[0:2, 2 * XT:], ACT.Sqrt).then_inc(sem["y_std"], 1)

            def square_h(t):
                i = units[NT + t][1]
                n = rows(i)
                act.wait_ge(sem["h_done"], 2 * (NT + t) + 2)
                nc.scalar.activation(junk[0:n], res(i)[0:n], ACT.Square, accum_out=ss2[0:n, t:t + 1]).then_inc(sem["h_sq"], 1)

            def std_h(t):
                n = rows(units[NT + t][1])
                act.wait_ge(sem["h_var"], t + 1)
                nc.scalar.activation(ss2[0:n, t:t + 1], ss2[0:n, t:t + 1], ACT.Sqrt).then_inc(sem["h_std"], 1)

            def high_h(t):
                i = units[NT + t][1]
                n = rows(i)
                act.wait_ge(sem["hn_t"], t + 1)
                if t == 0:
                    act.wait_ge(sem["wo_mm"], NT)
                nc.scalar.activation(hn_h[:, :, cols(i)], side.rearrange("p (k n) -> p k n", k=KD)[:, :, 0:n], ACT.Copy)\
                  .then_inc(sem["hn_hi"], 1)

            for u in range(2, 2 * NT):
                split_y(u)
                if u - 2 < KD:
                    split_w(KD + u - 2)
                t = u - NT - 1
                if t >= 0:
                    square_h(t)
                    std_h(t)
                if t >= 1:
                    high_h(t - 1)
            square_h(NT - 1)
            std_h(NT - 1)
            high_h(NT - 2)
            high_h(NT - 1)

        @block.vector
        def _(dve):
            link = chain(dve, sem["dve_link4"])

            def split_w(m):
                k = m % KD
                g = par[:, COLS["out_g"] + k:COLS["out_g"] + k + 1]
                dve.wait_ge(sem["wo_hi"], m + 1)
                nc.vector.scalar_tensor_tensor(out=wo_l[m // KD][:, k, :], in0=raw[m % 4], scalar=g,
                                               in1=f32(wo_h[m // KD][:, k, :]), op0=ALU.mult, op1=ALU.subtract)\
                  .then_inc(sem["wo_lo"], 1)

            for k in range(KD):
                split_w(k)
            for k in range(KD):
                w = k // LF
                dve.wait_ge(sem["ysq"], 2 * k + 2)
                if k % LF == 0:
                    nc.vector.tensor_copy(ysum[w], ysq[k % 2]).then_inc(sem["ysum"], 1)
                else:
                    dve.wait_ge(sem["ysum"], k)
                    nc.vector.tensor_tensor(ysum[w], ysum[w], ysq[k % 2], ALU.add).then_inc(sem["ysum"], 1)
            dve.wait_ge(sem["yss_mm"], 1)
            ss = side[:, 0:4 * NT].rearrange("p (i t) -> p i t", t=2)[:, :, 0]
            nc.vector.tensor_scalar(r_y[:, 0:2 * XT], ss[:, 0:2 * XT], 1.0 / LRU, EPS, ALU.mult, ALU.add)\
              .then_inc(sem["y_var"], 1)
            nc.vector.tensor_scalar(r_y[0:2, 2 * XT:], ss[0:2, 2 * XT:], 1.0 / LRU, EPS, ALU.mult, ALU.add)\
              .then_inc(sem["y_var"], 1)
            dve.wait_ge(sem["y_std"], 2)
            link(nc.vector.reciprocal(r_y[:, 0:2 * XT], r_y[:, 0:2 * XT]))
            link(nc.vector.reciprocal(r_y[0:2, 2 * XT:], r_y[0:2, 2 * XT:]))
            dve.wait_ge(sem["res_in"], 16 * (2 + XT))

            def add_groups(u):
                c, i = units[u]
                n = rows(i)
                cs = slice(half * c, half * c + half)
                dve.wait_ge(sem["wo_mm"], u + 1)
                for w in range(2):
                    r = r_y[0:n, 2 * i + w:2 * i + w + 1]
                    nc.vector.scalar_tensor_tensor(out=res(i)[0:n, cs], in0=bank(2 * (u % 3) + w)[0:n], scalar=r,
                                                   in1=res(i)[0:n, cs], op0=ALU.mult, op1=ALU.add)\
                      .then_inc(sem["h_done"], 1)
                    dve.wait_ge(sem["h_done"], 2 * u + w + 1)

            def normalise(t):
                i = units[NT + t][1]
                n = rows(i)
                dve.wait_ge(sem["h_sq"], t + 1)
                nc.vector.tensor_scalar(ss2[0:n, t:t + 1], ss2[0:n, t:t + 1], 1.0 / D, EPS, ALU.mult, ALU.add)\
                  .then_inc(sem["h_var"], 1)
                dve.wait_ge(sem["h_std"], t + 1)
                link(nc.vector.reciprocal(r2[0:n, t:t + 1], ss2[0:n, t:t + 1]))
                if t:
                    dve.wait_ge(sem["hn_t"], t)
                nc.vector.scalar_tensor_tensor(out=hn[0:n], in0=res(i)[0:n], scalar=r2[0:n, t:t + 1], in1=fg[0:n],
                                               op0=ALU.mult, op1=ALU.mult).then_inc(sem["hn"], 1)

            def low_h(t):
                i = units[NT + t][1]
                n = rows(i)
                dve.wait_ge(sem["hn_hi"], t + 1)
                nc.vector.tensor_tensor(hn_l[:, :, cols(i)], side.rearrange("p (k n) -> p k n", k=KD)[:, :, 0:n],
                                        f32(hn_h[:, :, cols(i)]), ALU.subtract).then_inc(sem["hn_lo"], 1)

            for u in range(2 * NT):
                add_groups(u)
                if u < KD:
                    split_w(KD + u)
                t = u - NT
                if t >= 0:
                    normalise(t)
                if t >= 1:
                    low_h(t - 1)
            low_h(NT - 1)

        @block.tensor
        def _(pe):
            def transpose_h(t):
                n = rows(units[NT + t][1])
                pe.wait_ge(sem["hn"], t + 1)
                if t:
                    pe.wait_ge(sem["hn_lo"], t)
                for k in range(KD):
                    ins = nc.tensor.transpose(side[:, P * k:P * k + n], hn[0:n, P * k:P * k + P], ident[0:n, 0:n])
                ins.then_inc(sem["hn_t"], 1)

            for u, (c, i) in enumerate(units):
                n = rows(i)
                pe.wait_ge(sem["y_lo"], 2 * u + 2)
                if u >= 3:
                    pe.wait_ge(sem["h_done"], 2 * (u - 2))
                for k in range(KD):
                    if u == 0 or (c == 1 and u == NT):
                        pe.wait_ge(sem["wo_lo"], KD * c + k + 1)
                    w = k // LF
                    ins = split_products(nc, bank(2 * (u % 3) + w)[0:n], y_h[u % 2][:, k, 0:n], y_l[u % 2][:, k, 0:n],
                                         wo_h[c][:, k, :], wo_l[c][:, k, :], k % LF == 0, k % LF == LF - 1)
                ins.then_inc(sem["wo_mm"], 1)
                if u == 1:
                    pe.wait_ge(sem["ysum"], KD)
                    for j in range(NT):
                        m = rows(j)
                        for w in range(2):
                            o = side[0:m, 2 * (2 * j + w):2 * (2 * j + w) + 2]
                            ins = nc.tensor.matmul(o, ysum[w][:, cols(j)], ones[:, 0:2], start=True, stop=True)
                    ins.then_inc(sem["yss_mm"], 1)
                t = u - NT - 1
                if t >= 0:
                    if t == 0:
                        pe.wait_ge(sem["y_var"], 2)
                    transpose_h(t)
            transpose_h(NT - 1)


def ffn_phase(nc, place, con, h, hn_h, hn_l, bank, dram, out, sem):
    at = M_3
    up_raw = place("up_raw", at, (2 * KD, P)); at += 2 * KD * P
    up_h, up_l, dn_h, dn_l, a_h, a_l, dn_raw = [], [], [], [], [], [], []
    for e in range(2):
        up_h.append(place(f"up_h{e}", at, (2 * KD, P), F32R)); at += 2 * KD * P
        up_l.append(place(f"up_l{e}", at, (2 * KD, P), F32R)); at += 2 * KD * P
        dn_h.append(place(f"dn_h{e}", at, (D,), F32R)); at += D
        dn_l.append(place(f"dn_l{e}", at, (D,), F32R)); at += D
        a_h.append(place(f"a_h{e}", at, (SEQ,), F32R)); at += SEQ
        a_l.append(place(f"a_l{e}", at, (SEQ,), F32R)); at += SEQ
        dn_raw.append(place(f"dn_raw{e}", at, (D,))); at += D
    assert at <= 53208, at
    at = M_YL
    gs = place("gate", at, (Q2 + 2,)); at += Q2 + 6
    cv = place("gate_conv", at, (SEQ,)); at += SEQ
    pr = place("ffn_act", at, (SEQ,)); at += SEQ
    par = con["par"]
    third = Q2 // 3
    assert third * 3 == Q2 and third % 2 == 0
    GROUPS = NFF // 2
    NU = 2 * XT

    g_ps = bank(0, 3).rearrange("p (c n) -> p c n", c=3)[:, :, 0:third]
    u_ps = bank(3, 2)

    def over_groups(eng, first, steady, last):
        first(0)
        with eng.Fori(1, GROUPS - 1) as g:
            steady(g)
        last(GROUPS - 1)

    with nc.Block() as block:
        @block.sync
        def _(sp):
            def load(g, wait=True):
                for e in range(2):
                    t = 2 * g + e
                    if wait or e:
                        sp.wait_ge(sem["up_lo"], t)
                    sp.dma_start(up_raw, dram["w_up"][bass.ds(t, 1)].rearrange("o p a k n -> p (o a k) n"))\
                      .then_inc(sem["up_in"], 16)
                    if wait:
                        sp.wait_ge(sem["dn_lo"], t - 1)
                    sp.dma_start(dn_raw[e], dram["w_down"].rearrange("(t p) n -> t p n", p=P)[bass.ds(t, 1)]
                                 .rearrange("o p n -> p (o n)")).then_inc(sem["dn_in"][e], 16)

            load(0, False)
            with sp.Fori(1, GROUPS) as g:
                load(g)
            for u in range(NU):
                i, c = divmod(u, 2)
                sp.wait_ge(sem["dn_read"], NU * (GROUPS - 1) + u + 1)
                sp.dma_start(out[P * i:P * i + P, 512 * c:512 * c + 512], h[:, i, 512 * c:512 * c + 512])\
                  .then_inc(sem["stored"], 16)
            sp.wait_ge(sem["stored"], 16 * NU)

        @block.gpsimd
        def _(pool):
            def low_up(t, e, first=False):
                pool.wait_ge(sem["up_hi"], t + 1)
                nc.gpsimd.tensor_tensor(up_l[e], up_raw, f32(up_h[e]), ALU.subtract).then_inc(sem["up_lo"], 1)

            def low_dn(t, e):
                pool.wait_ge(sem["dn_hi"], t + 1)
                nc.gpsimd.tensor_tensor(dn_l[e], dn_raw[e], f32(dn_h[e]), ALU.subtract).then_inc(sem["dn_lo"], 1)

            low_up(0, 0)
            low_up(1, 1)

            def group(g, more=True):
                for e in range(2):
                    low_dn(2 * g + e, e)
                    if more:
                        low_up(2 * g + 2 + e, e)

            over_groups(pool, group, group, lambda g: group(g, False))

        @block.scalar
        def _(act):
            def high_up(t, e):
                act.wait_ge(sem["up_in"], 16 * t + 16)
                nc.scalar.activation(up_h[e], up_raw, ACT.Copy).then_inc(sem["up_hi"], 1)

            high_up(0, 0)
            high_up(1, 1)

            def group(g, down=True, more=True):
                for e in range(2):
                    t = 2 * g + e
                    act.wait_ge(sem["gate_mm"], t + 1)
                    if down or e:
                        act.wait_ge(sem["conv2"], t)
                    nc.scalar.activation(gs[:, 0:Q2].rearrange("p (c n) -> p c n", c=3), g_ps, ACT.Copy)\
                      .then_inc(sem["gate_read"], 1)
                    act.wait_ge(sem["conv2"], t + 1)
                    nc.scalar.activation(cv, cv, ACT.Silu).then_inc(sem["silu"], 1)
                    act.wait_ge(sem["prod"], t + 1)
                    if down:
                        act.wait_ge(sem["dn_mm"], NU * g)
                    nc.scalar.activation(a_h[e], pr, ACT.Copy).then_inc(sem["a_hi"], 1)
                    act.wait_ge(sem["dn_in"][e], 16 * g + 16)
                    nc.scalar.activation(dn_h[e], dn_raw[e], ACT.Copy).then_inc(sem["dn_hi"], 1)
                    if more:
                        act.wait_ge(sem["up_mm"], t + 1)
                        high_up(t + 2, e)

            over_groups(act, lambda g: group(g, down=False), group, lambda g: group(g, more=False))

        @block.vector
        def _(dve):
            link = chain(dve, sem["dve_link5"])
            link(nc.vector.memset(gs[:, Q2:Q2 + 2], 0.0))

            def col(name, i):
                return par[:, bass.ds(COLS[name] + i, 1)]

            def group(g, down=True):
                for e in range(2):
                    t = 2 * g + e
                    dve.wait_ge(sem["gate_read"], t + 1)
                    if down or e:
                        dve.wait_ge(sem["prod"], t)
                    nc.vector.tensor_scalar(cv, gs[:, 1:1 + SEQ], col("ffn_w", 3 * t), col("ffn_b", t),
                                            ALU.mult, ALU.add).then_inc(sem["conv_a"], 1)
                    dve.wait_ge(sem["conv_a"], 2 * t + 1)
                    nc.vector.scalar_tensor_tensor(out=cv, in0=gs[:, 2:2 + SEQ], scalar=col("ffn_w", 3 * t + 1), in1=cv,
                                                   op0=ALU.mult, op1=ALU.add).then_inc(sem["conv_a"], 1)
                    dve.wait_ge(sem["conv_a"], 2 * t + 2)
                    nc.vector.scalar_tensor_tensor(out=cv, in0=gs[:, 3:3 + SEQ], scalar=col("ffn_w", 3 * t + 2), in1=cv,
                                                   op0=ALU.mult, op1=ALU.add).then_inc(sem["conv2"], 1)
                    dve.wait_ge(sem["silu"], t + 1)
                    dve.wait_ge(sem["up_mm"], t + 1)
                    if down or e:
                        dve.wait_ge(sem["a_lo"], t)
                    nc.vector.tensor_tensor(pr, u_ps, cv, ALU.mult).then_inc(sem["prod"], 1)
                    if e == 0 and down:
                        add_down(g - 1)
                    dve.wait_ge(sem["a_hi"], t + 1)
                    nc.vector.tensor_tensor(a_l[e], pr, f32(a_h[e]), ALU.subtract).then_inc(sem["a_lo"], 1)

            def add_down(g):
                for u in range(NU):
                    i, c = divmod(u, 2)
                    r = h[:, i, 512 * c:512 * c + 512]
                    if u == 0:
                        dve.wait_ge(sem["dn_read"], NU * g)
                    dve.wait_ge(sem["dn_mm"], NU * g + u + 1)
                    nc.vector.tensor_tensor(r, bank(5 + u % 3), r, ALU.add).then_inc(sem["dn_read"], 1)

            over_groups(dve, lambda g: group(g, down=False), group, group)
            add_down(GROUPS - 1)

        @block.tensor
        def _(pe):
            def up(g, e, first):
                t = 2 * g + e
                pe.wait_ge(sem["up_lo"], t + 1)
                if not first:
                    pe.wait_ge(sem["gate_read"], t)
                for k in range(KD):
                    for c in range(3):
                        cs = slice(third * c, third * c + third)
                        ins = split_products(nc, g_ps[:, c], up_h[e][:, k, :], up_l[e][:, k, :], hn_h[:, k, cs],
                                             hn_l[:, k, cs], k == 0, k == KD - 1)
                ins.then_inc(sem["gate_mm"], 1)
                if not first:
                    pe.wait_ge(sem["prod"], t)
                for k in range(KD):
                    for c in range(2):
                        cs = slice(2 + 512 * c, 2 + 512 * c + 512)
                        ins = split_products(nc, u_ps[:, 512 * c:512 * c + 512], up_h[e][:, KD + k, :],
                                             up_l[e][:, KD + k, :], hn_h[:, k, cs], hn_l[:, k, cs], k == 0, k == KD - 1)
                ins.then_inc(sem["up_mm"], 1)

            def down(g):
                pe.wait_ge(sem["a_lo"], 2 * g + 2)
                pe.wait_ge(sem["dn_lo"], 2 * g + 2)
                pe.wait_ge(sem["dn_read"], NU * g)
                for u in range(NU):
                    i, c = divmod(u, 2)
                    ts, cs = slice(P * i, P * i + P), slice(512 * c, 512 * c + 512)
                    if u >= 3:
                        pe.wait_ge(sem["dn_read"], NU * g + u - 2)
                    for e in range(2):
                        ins = split_products(nc, bank(5 + u % 3), a_h[e][:, ts], a_l[e][:, ts], dn_h[e][:, cs],
                                             dn_l[e][:, cs], e == 0, e == 1)
                    ins.then_inc(sem["dn_mm"], 1)

            def group(g):
                up(g, 0, False)
                down(g - 1)
                up(g, 1, False)

            def first(g):
                up(g, 0, True)
                up(g, 1, False)

            over_groups(pe, first, group, group)
            down(GROUPS - 1)


SEMS = """par_in gw_in con_in x_hi x_sq x_lo x_acc ones pads w_split gw_split xc_hi xc_lo a_ready a_sq scanned gelu y_lru
lam_e lam_done var std conv gate_in unit_done unit_read_act unit_read_dve var_lru sqrt_lru pool_link act_link dve_link
uq_in ukv_in csq uq_hi ukv_hi uq_lo v_hi v_lo gained roped c_hi c_lo kv_var kv_std kv_rstd q_mm kv_mm st_mm squares
summed kvs k_scaled q_scaled head_var head_std dve_link2
sel_in b_set e_summed e_full e_hi e_lo es_lo es_hi side_done side_hi side_read_act side_read_dve s_done pv_done o_low
o_sum y_mla xo_mm xo_low x_lo2 x_y x_exp q_low_meta dve_link3
wo_lo wo_hi res_in y_hi y_lo ysq ysum y_var y_std yss_mm wo_mm h_done h_sq h_var h_std hn hn_t hn_hi hn_lo dve_link4
up_in up_hi up_lo dn_hi dn_lo gate_mm up_mm gate_read conv_a conv2 silu prod a_hi a_lo dn_mm dn_read stored
dve_link5""".split()


def build(nc, dram, out):
    with ExitStack() as ctx:
        place = Place(nc)
        con = constants(place)
        sem = {n: ctx.enter_context(nc.semaphore(n)) for n in SEMS}
        sem["xt_in"] = [ctx.enter_context(nc.semaphore(f"xt_in{b}")) for b in range(4)]
        sem["wo_in"] = [ctx.enter_context(nc.semaphore(f"wo_in{b}")) for b in range(4)]
        sem["dn_in"] = [ctx.enter_context(nc.semaphore(f"dn_in{b}")) for b in range(2)]
        sem["w_in"] = [ctx.enter_context(nc.semaphore(f"w_in{b}")) for b in range(2)]
        all_banks = ctx.enter_context(nc.psum_tensor("banks", [P, 8 * 512], F32))

        def bank(b, n=1):
            return all_banks[:, 512 * b:512 * (b + n)]

        yl = place("y_lru", M_YL, (LF, T))
        cq = place("cq", M_CQ, (3, T))
        kpe = place("kpe_fm", M_KPE, (T,), parts=ROPE)
        xpad = place("xpad", M_KPE, (T + 3,))
        mix_phase(nc, place, con, yl, cq, (kpe, xpad), [bank(b) for b in range(8)], dram, sem)
        qk = place("qk", M_QK, (NT, 2 * HEADS * QK))
        v = place("v", M_V, (NT, HEADS * 2 * VD), F32R)
        qkv_phase(nc, place, con, cq, kpe, qk, v, bank, dram, sem)
        ym = place("y_mla", M_YM, (KD // 2, SEQ + 2))
        attention_phase(nc, place, con, qk, v, ym, bank, dram, sem)
        h = place("h", M_H, (XT, D))
        hn_h = place("hn_h", M_HN, (KD, Q2), F32R)
        hn_l = place("hn_l", M_HNL, (KD, Q2), F32R)
        out_phase(nc, place, con, yl, ym, h, hn_h, hn_l, bank, dram, sem)
        ffn_phase(nc, place, con, h, hn_h, hn_l, bank, dram, out, sem)


def _pack(inputs):
    a = {k: np.ascontiguousarray(np.asarray(v)) for k, v in inputs.items()}
    h0 = np.concatenate([a["meta_tokens"], a["x"][0]], axis=0)

    def cols(v):
        v = v.reshape(-1, v.shape[-1] // P, P)
        return v.transpose(1, 0, 2).reshape(-1, P).T

    par = np.zeros((P, NCOL), np.float32)
    gate_b = np.stack([a["lru_b_a"][0], a["lru_b_x"][0]], 1).reshape(4, LRU)
    for name, v in [("mix_g", a["norm_mix_g"][0]), ("conv_w", a["conv_lru_w"][0]), ("conv_b", a["conv_lru_b"][0]),
                    ("gate_b", gate_b), ("lam", a["lru_lambda"][0]), ("q_g", a["q_latent_g"][0]),
                    ("kv_g", a["kv_latent_g"][0]),
                    ("out_g", np.concatenate([a["lru_gate_g"][0], a["mla_out_g"][0]])),
                    ("ffn_w", a["conv_ffn_w"][0]), ("ffn_b", a["conv_ffn_b"][0])]:
        c = cols(v)
        par[:, COLS[name]:COLS[name] + c.shape[1]] = c
    gw = np.zeros((P, LF, 2, 2, P), np.float32)
    for d in range(2):
        for w, name in enumerate(["lru_w_a", "lru_w_x"]):
            for h in range(8):
                o = 64 * (h % 2)
                gw[o:o + 64, h // 2, d, w, o:o + 64] = a[name][0, d, h]
    inv = (10000.0 ** (-np.arange(0, ROPE, 2, dtype=np.float32) / ROPE)).astype(np.float32)
    ang = np.arange(T, dtype=np.float32)[:, None] * inv[None, :]
    cos, sin = np.cos(ang), np.sin(ang)
    rc, rs = np.zeros((P, NT, ROPE), np.float32), np.zeros((P, NT, ROPE), np.float32)
    for i in range(NT):
        n, t0 = token_rows(i)
        rc[:n, i] = np.concatenate([cos[t0:t0 + n], cos[t0:t0 + n]], 1)
        rs[:n, i] = np.concatenate([-sin[t0:t0 + n], sin[t0:t0 + n]], 1)
    gqk = np.broadcast_to(np.stack([a["q_norm_g"][0], a["k_norm_g"][0]])[None], (P, 2, QK))
    up = a["w_ffn_up"][0].reshape(KD, P, 2, NFF, P).transpose(3, 1, 2, 0, 4)
    return {
        "x_tm": a["x"][0], "meta_tm": a["meta_tokens"],
        "x_fm": np.ascontiguousarray(h0.T.reshape(KD, P, T)),
        "par": par, "gate_w": gw.reshape(P, 4 * LF, P), "w_in": a["w_in"][0],
        "ident": np.eye(P, dtype=np.float32), "gqk": np.ascontiguousarray(gqk), "rope_c": rc, "rope_s": rs,
        "w_uq": a["w_uq"][0], "w_ukv": a["w_ukv"][0], "w_out": a["w_out"][0],
        "ffn_g": np.ascontiguousarray(np.broadcast_to(a["norm_ffn_g"][0][None], (P, D))),
        "w_up": np.ascontiguousarray(up), "w_down": a["w_ffn_down"][0],
        "sel": _selectors(),
    }


def _selectors():
    s = np.zeros((P, XT, VD), np.float32)
    for i in range(XT):
        s[i, i] = 1.0
        s[32 + i, i] = 1.0
    return s


def kernel(**inputs):
    import concourse.bacc as _bacc
    from concourse.bass_utils import run_bass_kernel_spmd as _run

    nc = _bacc.Bacc("TRN2", target_bir_lowering=False, num_devices=1)
    arrays, dram = {}, {}
    for name, a in _pack(inputs).items():
        arrays[f"in_{name}"] = a
        dram[name] = nc.dram_tensor(f"in_{name}", a.shape, mybir.dt.from_np(a.dtype), kind="ExternalInput").ap()
    out = nc.dram_tensor("out_0", (SEQ, D), F32, kind="ExternalOutput").ap()
    build(nc, dram, out)
    r = _run(nc, [arrays], core_ids=[0])
    return r.results[0]["out_0"].reshape(1, SEQ, D)
```

```python
from contextlib import ExitStack

import numpy as np

import concourse.bass as bass
from concourse import mybir

F32 = mybir.dt.float32
F32R = mybir.dt.float32r
ACT = mybir.ActivationFunctionType
ALU = mybir.AluOpType
AX = mybir.AxisListType

P = 128
D = 1024
KD = D // P
META = 16
SEQ = 1024
T = META + SEQ
XT = SEQ // P
NT = XT + 1
LRU = 512
LF = LRU // P
TAPS = 4
LRU_C = 8.0
HEADS = 8
NOPE, ROPE = 64, 32
QK = NOPE + ROPE
VD = 64
QL, KVL = 256, 128
FF = 2816
NFF = FF // P
EPS = 1e-6
CH = [(0, 348), (348, 346), (694, 346)]
WORD = 4


def token_rows(i):
    return (P, META + P * i) if i < XT else (META, 0)


COLS = {}
_at = 0
for _name, _n in [("mix_g", KD), ("conv_w", LF * TAPS), ("conv_b", LF), ("gate_b", LF * 4), ("lam", LF * 2),
                  ("q_g", QL // P), ("kv_g", KVL // P), ("out_g", KD), ("ffn_w", NFF * 3), ("ffn_b", NFF)]:
    COLS[_name] = _at
    _at += _n
NCOL = _at


class Place:

    BASE = 16512

    def __init__(self, nc):
        self.nc = nc

    def __call__(self, name, at, shape, dtype=F32, parts=P):
        words = int(np.prod(shape))
        t = self.nc.alloc_sbuf_tensor_at(name, [parts, words], dtype, offset=self.BASE + WORD * at)
        ap = t[:, :]
        if len(shape) == 2:
            ap = ap.rearrange("p (a b) -> p a b", a=shape[0])
        if len(shape) == 3:
            ap = ap.rearrange("p (a b c) -> p a b c", a=shape[0], b=shape[1])
        return ap


def f32(ap):
    return ap.bitcast(F32)


def chain(eng, sem):
    n = [0]

    def link(ins):
        n[0] += 1
        ins.then_inc(sem, 1)
        eng.wait_ge(sem, n[0])

    return link


def split_products(nc, out, w_h, w_l, x_h, x_l, first, last):
    nc.tensor.matmul(out, w_h, x_h, start=first, stop=False)
    nc.tensor.matmul(out, w_h, x_l, start=False, stop=False)
    return nc.tensor.matmul(out, w_l, x_h, start=False, stop=last)


M_SMALL = 0
M_YL = 1400
M_A = M_YL + LF * T


def constants(place):
    c = {}
    at = M_SMALL
    for name, shape in [("ident", (P,)), ("par", (NCOL,)), ("sp4", (LF * 2,)), ("sp4n", (LF * 2,)), ("hb", (LF * 4,)),
                        ("ones", (P,)), ("gqk", (2, QK)), ("rope_c", (NT, ROPE)), ("rope_s", (NT, ROPE)),
                        ("lam_t", (6, LF * 2)), ("stat", (2, 64))]:
        c[name] = place(name, at, shape)
        if name == "gqk":
            c["late"] = at
        at += -(-int(np.prod(shape)) // 8) * 8
    assert at <= M_YL, at
    return c


def mix_phase(nc, place, con, yl, cq, kpe_fm, psum, dram, sem):
    at = M_A
    xn_h = place("xn_h", at, (KD, T), F32R); at += KD * T
    xn_l = place("xn_l", at, (KD, T), F32R); at += KD * T
    w_h = [place(f"win_h{b}", at + 2048 * b, (KD, P), F32R) for b in range(2)]
    w_l = [place(f"win_l{b}", at + 2048 * b + 1024, (KD, P), F32R) for b in range(2)]; at += 4096
    gw_h = place("gw_h", at, (4 * LF, P), F32R); at += 2048
    gw_l = place("gw_l", at, (4 * LF, P), F32R); at += 2048
    xc_h = place("xc_h", at, (T,), F32R); at += T
    xc_l = place("xc_l", at, (T,), F32R); at += T
    w_raw = [place(f"win_raw{b}", at + 1024 * b, (KD, P)) for b in range(2)]; at += 2048
    xpad = kpe_fm[1]
    xc = [place(f"xc{b}", at + T * b, (T,)) for b in range(2)]; at += 2 * T
    gel = [place(f"gelu{b}", at + T * b, (T,)) for b in range(2)]; at += 2 * T
    rb = place("rb", at, (T,)); at += T
    A = [place(f"lru_a{d}", at + T * d, (T,)) for d in range(2)]
    W = [place(f"lru_w{d}", at + T * (2 + d), (T,)) for d in range(2)]
    X = [place(f"lru_x{d}", at + T * (4 + d), (T,)) for d in range(2)]
    S = [place(f"lru_s{d}", at + T * (6 + d), (T,)) for d in range(2)]
    xt = [place(f"xt{b}", at + T * b, (T,)) for b in range(4)]
    sq = [place(f"xsq{b}", at + T * (4 + b), (T,)) for b in range(2)]
    acc = place("xacc", at + T * 6, (T,)); at += 8 * T
    assert at <= M_CQ, (at, M_CQ)
    gw_raw = place("gw_raw", M_YL, (4 * LF, P))
    par = con["par"]

    def col(name, i):
        return par[:, COLS[name] + i:COLS[name] + i + 1]

    tiles = [("x", 0), ("x", 1), ("g", 0), ("g", 1), ("x", 2), ("g", 2), ("x", 3), ("g", 3),
             ("c", 0), ("c", 1), ("c", 2), ("k", 0)]
    first_col = {"x": 0, "g": LRU, "c": 2 * LRU, "k": 2 * LRU + QL + KVL}
    order = [("x", 0), ("x", 1), ("s", 0), ("g", 0), ("G", 0), ("g", 1), ("G", 1), ("x", 2), ("g", 2), ("G", 2),
             ("x", 3), ("g", 3), ("G", 3), ("c", 0), ("c", 1), ("c", 2), ("k", 0)]
    units = []
    for kind, f in order:
        if kind == "G":
            units += [(kind, f, d, w, c) for d in range(2) for w in range(2) for c in range(3)]
        else:
            units += [(kind, f, c) for c in range(3)]
    at_unit = {u: n for n, u in enumerate(units)}
    dve_reads = [("s", 0, 0), ("s", 0, 1), ("x", 0, 0), ("x", 0, 1), ("s", 0, 2), ("x", 0, 2)]
    dve_reads += [u for u in units if u[0] != "G" and u not in dve_reads]
    act_reads = [u for u in units if u[0] == "G"]

    def bank(u):
        return psum[at_unit[u] % 8]

    def wait_unit(eng, u):
        eng.wait_ge(sem["unit_done"], at_unit[u] + 1)

    def wait_bank(eng, u):
        n = at_unit[u] - 8
        if n >= 0:
            v = units[n]
            if v[0] == "G":
                eng.wait_ge(sem["unit_read_act"], act_reads.index(v) + 1)
            else:
                eng.wait_ge(sem["unit_read_dve"], dve_reads.index(v) + 1)

    def wait_tile(eng, n):
        kind, f = tiles[n]
        eng.wait_ge(sem["unit_done"], at_unit[(kind, f, 2)] + 1)

    with nc.Block() as block:
        @block.sync
        def _(sp):
            sp.dma_start(par, dram["par"]).then_inc(sem["par_in"], 16)

            def load_x(k):
                if k >= 4:
                    sp.wait_ge(sem["x_sq"], k - 3)
                    sp.wait_ge(sem["x_lo"], k - 3)
                sp.dma_start(xt[k % 4], dram["x_fm"][k]).then_inc(sem["xt_in"][k % 4], 16)

            def load_w(n):
                if n >= 2:
                    sp.wait_ge(sem["w_split"], n - 1)
                cols = ROPE if tiles[n][0] == "k" else P
                c0 = first_col[tiles[n][0]] + P * tiles[n][1]
                sp.dma_start(w_raw[n % 2][:, :, 0:cols],
                             dram["w_in"].rearrange("(k p) n -> p k n", p=P)[:, :, c0:c0 + cols])\
                  .then_inc(sem["w_in"][n % 2], 16)

            load_x(0)
            load_w(0)
            load_x(1)
            load_w(1)
            for k in range(2, KD):
                load_x(k)
            sp.dma_start(gw_raw, dram["gate_w"]).then_inc(sem["gw_in"], 16)
            for n, name in enumerate(["ident", "gqk", "rope_c", "rope_s"]):
                sp.dma_start(con[name], dram[name]).then_inc(sem["con_in"], 16)
            for n in range(2, len(tiles)):
                load_w(n)

        @block.gpsimd
        def _(pool):
            link = chain(pool, sem["pool_link"])
            nc.gpsimd.memset(con["ones"], 1.0).then_inc(sem["ones"], 1)
            nc.gpsimd.memset(xpad[:, 0:2], 0.0).then_inc(sem["pads"], 1)
            nc.gpsimd.memset(xpad[:, T + 2:T + 3], 0.0).then_inc(sem["pads"], 1)

            def split_w(n):
                cols = ROPE if tiles[n][0] == "k" else P
                pool.wait_ge(sem["w_in"][n % 2], 16 * (n // 2 + 1))
                if n >= 2:
                    wait_tile(pool, n - 2)
                raw = w_raw[n % 2][:, :, 0:cols]
                link(nc.gpsimd.tensor_copy(w_h[n % 2][:, :, 0:cols], raw))
                nc.gpsimd.tensor_tensor(w_l[n % 2][:, :, 0:cols], raw, f32(w_h[n % 2][:, :, 0:cols]),
                                        ALU.subtract).then_inc(sem["w_split"], 1)

            def split_gates():
                pool.wait_ge(sem["gw_in"], 16)
                link(nc.gpsimd.tensor_copy(gw_h, gw_raw))
                nc.gpsimd.tensor_tensor(gw_l, gw_raw, f32(gw_h), ALU.subtract).then_inc(sem["gw_split"], 1)

            def low_xc(f):
                pool.wait_ge(sem["xc_hi"], f + 1)
                nc.gpsimd.tensor_tensor(xc_l, xc[f % 2], f32(xc_h), ALU.subtract).then_inc(sem["xc_lo"], 1)

            def square_a(f):
                if f:
                    pool.wait_ge(sem["y_lru"], f)
                for d in range(2):
                    pool.wait_ge(sem["a_ready"], 2 * f + d + 1)
                    nc.gpsimd.tensor_tensor(S[d], A[d], A[d], ALU.mult).then_inc(sem["a_sq"], 1)

            def join(f):
                pool.wait_ge(sem["scanned"], 2 * f + 2)
                link(nc.gpsimd.tensor_tensor(S[0], S[0], S[1], ALU.add))
                pool.wait_ge(sem["gelu"], f + 1)
                if f == 0:
                    pool.wait_ge(sem["gw_split"], 1)
                nc.gpsimd.tensor_tensor(yl[:, f, :], S[0], gel[f % 2], ALU.mult).then_inc(sem["y_lru"], 1)

            split_w(0)
            split_w(1)
            split_gates()
            split_w(2)
            low_xc(0)
            split_w(3)
            square_a(0)
            low_xc(1)
            for f in range(LF):
                if f < LF:
                    split_w(4 + 2 * f)
                    split_w(5 + 2 * f)
                join(f)
                if f + 1 < LF:
                    square_a(f + 1)
                if f + 2 < LF:
                    low_xc(f + 2)

        @block.scalar
        def _(act):
            link = chain(act, sem["act_link"])
            act.wait_ge(sem["par_in"], 16)
            for k in range(KD):
                act.wait_ge(sem["xt_in"][k % 4], 16 * (k // 4 + 1))
                nc.scalar.activation(xn_h[:, k, :], xt[k % 4], ACT.Copy, scale=col("mix_g", k)).then_inc(sem["x_hi"], 1)
                if k >= 2:
                    act.wait_ge(sem["x_acc"], k - 1)
                nc.scalar.activation(sq[k % 2], xt[k % 4], ACT.Square).then_inc(sem["x_sq"], 1)
            lam = par[:, COLS["lam"]:COLS["lam"] + 2 * LF]
            link(nc.scalar.activation(con["lam_t"][:, 0, :], lam, ACT.Abs))
            nc.scalar.activation(con["lam_t"][:, 1, :], con["lam_t"][:, 0, :], ACT.Exp, scale=-1.0).then_inc(sem["lam_e"], 1)
            for c, (c0, cn) in enumerate(CH):
                act.wait_ge(sem["unit_read_dve"], dve_reads.index(("s", 0, c)) + 1)
                nc.scalar.activation(rb[:, c0:c0 + cn], rb[:, c0:c0 + cn], ACT.Sqrt).then_inc(sem["std"], 1)
            for f in range(LF):
                act.wait_ge(sem["conv"], f + 1)
                if f:
                    act.wait_ge(sem["unit_done"], at_unit[("G", f - 1, 1, 1, 2)] + 1)
                nc.scalar.activation(xc_h, xc[f % 2], ACT.Copy).then_inc(sem["xc_hi"], 1)
                act.wait_ge(sem["unit_read_dve"], dve_reads.index(("g", f, 2)) + 1)
                nc.scalar.activation(gel[f % 2], gel[f % 2], ACT.Gelu_apprx_tanh).then_inc(sem["gelu"], 1)
                if f == 0:
                    act.wait_ge(sem["lam_done"], 1)
                for d in range(2):
                    if f:
                        act.wait_ge(sem["scanned"], 2 * (f - 1) + d + 1)
                    for w, out in ((0, A[d]), (1, X[d])):
                        hb = con["hb"][:, 4 * f + 2 * d + w:4 * f + 2 * d + w + 1]
                        for c, (c0, cn) in enumerate(CH):
                            wait_unit(act, ("G", f, d, w, c))
                            nc.scalar.activation(out[:, c0:c0 + cn], bank(("G", f, d, w, c))[:, 0:cn], ACT.Tanh,
                                                 bias=hb, scale=0.5).then_inc(sem["unit_read_act"], 1)
                    act.wait_ge(sem["unit_read_act"], 12 * f + 6 * d + 6)
                    p4 = con["sp4"][:, 2 * f + d:2 * f + d + 1]
                    n4 = con["sp4n"][:, 2 * f + d:2 * f + d + 1]
                    link(nc.scalar.activation(W[d], A[d], ACT.Tanh, bias=p4, scale=p4))
                    nc.scalar.activation(A[d], A[d], ACT.Exp, bias=n4, scale=n4).then_inc(sem["a_ready"], 1)
                for d in range(2):
                    act.wait_ge(sem["var_lru"], 2 * f + d + 1)
                    nc.scalar.activation(W[d], W[d], ACT.Sqrt).then_inc(sem["sqrt_lru"], 1)

        @block.vector
        def _(dve):
            link = chain(dve, sem["dve_link"])
            dve.wait_ge(sem["par_in"], 16)
            for k in range(KD):
                dve.wait_ge(sem["x_hi"], k + 1)
                nc.vector.scalar_tensor_tensor(out=xn_l[:, k, :], in0=xt[k % 4], scalar=col("mix_g", k),
                                               in1=f32(xn_h[:, k, :]), op0=ALU.mult, op1=ALU.subtract)\
                  .then_inc(sem["x_lo"], 1)
                dve.wait_ge(sem["x_sq"], k + 1)
                if k == 0:
                    nc.vector.tensor_copy(acc, sq[0]).then_inc(sem["x_acc"], 1)
                else:
                    dve.wait_ge(sem["x_acc"], k)
                    nc.vector.tensor_tensor(acc, acc, sq[k % 2], ALU.add).then_inc(sem["x_acc"], 1)

            link(nc.vector.tensor_scalar(con["hb"], par[:, COLS["gate_b"]:COLS["gate_b"] + 4 * LF], 0.5, None, ALU.mult))
            lt = con["lam_t"]
            z, e, w, w2, s, m = (lt[:, i, :] for i in (0, 1, 2, 3, 4, 5))
            dve.wait_ge(sem["lam_e"], 1)
            lam = par[:, COLS["lam"]:COLS["lam"] + 2 * LF]
            link(nc.vector.tensor_scalar(m, lam, -1.0, 0.0, ALU.mult, ALU.max))
            link(nc.vector.tensor_scalar(w2, e, 2.0, None, ALU.add))
            link(nc.vector.reciprocal(w, w2))
            link(nc.vector.tensor_tensor(w, w, e, ALU.mult))
            link(nc.vector.tensor_tensor(w2, w, w, ALU.mult))
            n_terms = 10
            link(nc.vector.tensor_scalar(s, w2, 1.0 / (2 * n_terms + 1), 1.0 / (2 * n_terms - 1), ALU.mult, ALU.add))
            for j in range(n_terms - 2, -1, -1):
                link(nc.vector.tensor_tensor(s, s, w2, ALU.mult))
                link(nc.vector.tensor_scalar(s, s, 1.0 / (2 * j + 1), None, ALU.add))
            link(nc.vector.tensor_tensor(s, s, w, ALU.mult))
            link(nc.vector.scalar_tensor_tensor(out=s, in0=s, scalar=2.0, in1=m, op0=ALU.mult, op1=ALU.add))
            link(nc.vector.tensor_scalar(con["sp4"], s, LRU_C / 2, None, ALU.mult))
            nc.vector.tensor_scalar(con["sp4n"], s, -LRU_C / 2, None, ALU.mult).then_inc(sem["lam_done"], 1)

            def variance(c):
                c0, cn = CH[c]
                wait_unit(dve, ("s", 0, c))
                nc.vector.tensor_scalar(rb[:, c0:c0 + cn], bank(("s", 0, c))[:, 0:cn], 1.0 / D, EPS,
                                        ALU.mult, ALU.add).then_inc(sem["unit_read_dve"], 1)

            def scale_rows(c):
                c0, cn = CH[c]
                dve.wait_ge(sem["std"], c + 1)
                link(nc.vector.reciprocal(rb[:, c0:c0 + cn], rb[:, c0:c0 + cn]))

            def read(u, out, m=P):
                c0, cn = CH[u[-1]]
                wait_unit(dve, u)
                nc.vector.tensor_tensor(out[:, c0:c0 + cn], bank(u)[0:m, 0:cn], rb[0:m, c0:c0 + cn], ALU.mult)\
                  .then_inc(sem["unit_read_dve"], 1)

            def done_reading(u):
                dve.wait_ge(sem["unit_read_dve"], dve_reads.index(u) + 1)

            def conv(f):
                done_reading(("x", f, 2))
                if f >= 2:
                    dve.wait_ge(sem["xc_lo"], f - 1)
                taps = [col("conv_w", TAPS * f + k) for k in range(TAPS)]
                link(nc.vector.tensor_scalar(xc[f % 2], xpad[:, 0:T], taps[0], col("conv_b", f), ALU.mult, ALU.add))
                for k in range(1, TAPS):
                    ins = nc.vector.scalar_tensor_tensor(out=xc[f % 2], in0=xpad[:, k:k + T], scalar=taps[k],
                                                         in1=xc[f % 2], op0=ALU.mult, op1=ALU.add)
                    if k < TAPS - 1:
                        link(ins)
                ins.then_inc(sem["conv"], 1)
                dve.wait_ge(sem["conv"], f + 1)

            def read_gate(f):
                if f >= 2:
                    dve.wait_ge(sem["y_lru"], f - 1)
                for c in range(3):
                    read(("g", f, c), gel[f % 2])

            def recurrence(f):
                for d in range(2):
                    dve.wait_ge(sem["a_sq"], 2 * f + d + 1)
                    nc.vector.scalar_tensor_tensor(out=W[d], in0=S[d], scalar=1.0, in1=W[d], op0=ALU.add, op1=ALU.mult)\
                      .then_inc(sem["var_lru"], 1)
                    link(nc.vector.scalar_tensor_tensor(out=X[d], in0=X[d], scalar=1.0, in1=xc[f % 2],
                                                        op0=ALU.add, op1=ALU.mult))
                for d in range(2):
                    dve.wait_ge(sem["sqrt_lru"], 2 * f + d + 1)
                    link(nc.vector.scalar_tensor_tensor(out=X[d], in0=W[d], scalar=0.5, in1=X[d],
                                                        op0=ALU.mult, op1=ALU.mult))
                    if d == 0:
                        nc.vector.tensor_tensor_scan(S[0], A[0], X[0], 0.0, ALU.mult, ALU.add).then_inc(sem["scanned"], 1)
                    else:
                        nc.vector.tensor_tensor_scan(S[1][:, ::-1], A[1][:, ::-1], X[1][:, ::-1], 0.0,
                                                     ALU.mult, ALU.add).then_inc(sem["scanned"], 1)

            variance(0)
            variance(1)
            scale_rows(0)
            dve.wait_ge(sem["pads"], 2)
            read(("x", 0, 0), xpad[:, 2:])
            scale_rows(1)
            read(("x", 0, 1), xpad[:, 2:])
            variance(2)
            scale_rows(2)
            read(("x", 0, 2), xpad[:, 2:])
            conv(0)
            for f in range(LF):
                if f < LF - 1 and f != 1:
                    pass
                if f == 0:
                    for c in range(3):
                        read(("x", 1, c), xpad[:, 2:])
                    conv(1)
                if f >= 2:
                    for c in range(3):
                        read(("x", f, c), xpad[:, 2:])
                    conv(f)
                read_gate(f)
                recurrence(f)
            for n in range(3):
                for c in range(3):
                    read(("c", n, c), cq[:, n, :])
            for c in range(3):
                read(("k", 0, c), kpe_fm[0], ROPE)

        @block.tensor
        def _(pe):
            def project(kinds, n0):
                for n, _ in enumerate(kinds):
                    pe.wait_ge(sem["w_split"], n0 + n + 1)
                us = [(kind, f, c) for kind, f in kinds for c in range(3)]
                for u in us:
                    wait_bank(pe, u)
                for k in range(KD):
                    if n0 == 0:
                        pe.wait_ge(sem["x_lo"], k + 1)
                    for u in us:
                        n = tiles.index(u[:2])
                        m = ROPE if u[0] == "k" else P
                        c0, cn = CH[u[2]]
                        ins = split_products(nc, bank(u)[0:m, 0:cn], w_h[n % 2][:, k, 0:m], w_l[n % 2][:, k, 0:m],
                                             xn_h[:, k, c0:c0 + cn], xn_l[:, k, c0:c0 + cn], k == 0, k == KD - 1)
                        if k == KD - 1:
                            ins.then_inc(sem["unit_done"], 1)

            for kind, f in order:
                if kind == "x" and f == 1:
                    continue
                if kind == "x" and f == 0:
                    project([("x", 0), ("x", 1)], 0)
                elif kind == "s":
                    pe.wait_ge(sem["ones"], 1)
                    pe.wait_ge(sem["x_acc"], KD)
                    for c, (c0, cn) in enumerate(CH):
                        wait_bank(pe, ("s", 0, c))
                        nc.tensor.matmul(bank(("s", 0, c))[:, 0:cn], con["ones"], acc[:, c0:c0 + cn],
                                         start=True, stop=True).then_inc(sem["unit_done"], 1)
                elif kind == "G":
                    pe.wait_ge(sem["gw_split"], 1)
                    pe.wait_ge(sem["xc_lo"], f + 1)
                    for u in units:
                        if u[:2] != ("G", f):
                            continue
                        _, _, d, w, c = u
                        c0, cn = CH[c]
                        m = 4 * f + 2 * d + w
                        wait_bank(pe, u)
                        split_products(nc, bank(u)[:, 0:cn], gw_h[:, m, :], gw_l[:, m, :], xc_h[:, c0:c0 + cn],
                                       xc_l[:, c0:c0 + cn], True, True).then_inc(sem["unit_done"], 1)
                else:
                    project([(kind, f)], tiles.index((kind, f)))


M_KPE = 53208 - (T + 8)
M_CQ = M_KPE - 3 * T


M_QK = M_A
M_V = M_QK + NT * 2 * HEADS * QK
M_2 = M_V + NT * HEADS * 2 * VD


def qkv_phase(nc, place, con, cq, kpe_fm, qk, v, bank, dram, sem):
    at = M_2
    c_h = place("c_h", at, (3, T), F32R); at += 3 * T
    c_l = place("c_l", at, (3, T), F32R); at += 3 * T
    NQ, NKV = HEADS * QK, HEADS * (NOPE + VD)
    uq_h = place("uq_h", at, (2, NQ), F32R); at += 2 * NQ
    uq_l = place("uq_l", at, (2, NQ), F32R); at += 2 * NQ
    ukv_h = place("ukv_h", at, (NKV,), F32R); at += NKV
    ukv_l = place("ukv_l", at, (NKV,), F32R); at += NKV
    csq = place("csq", at, (3, T)); at += 3 * T
    uq_raw = place("uq_raw", at, (2, NQ))
    kv1 = place("kvs1", at, (HEADS, NOPE + VD)); at += 2 * NQ
    ukv_raw = place("ukv_raw", at, (NKV,)); at += NKV
    sqs = place("squares", at, (1344,)); at += 1344
    kvs = [place("kvs0", at, (HEADS, NOPE + VD)), kv1]; at += NKV
    ra = place("rope_a", at, (2 * HEADS, ROPE)); at += 512
    rp = place("rope_b", at, (2 * HEADS, ROPE)); at += 512
    assert at <= M_CQ, (at, M_CQ)
    qsq = sqs[:, 0:NQ].rearrange("p (h d) -> p h d", h=HEADS)
    ksq = sqs[:, NQ:NQ + HEADS * NOPE].rearrange("p (h d) -> p h d", h=HEADS)
    psq = sqs[:, 1280:1280 + ROPE]
    par, ident, ones, stat = con["par"], con["ident"], con["ones"], con["stat"]
    half = ROPE // 2

    q_ps = bank(0, 2).rearrange("p (b n) -> p b n", b=2)[:, :, 0:NQ // 2]

    def kv_ps(i):
        return bank(2 if i % 2 == 0 else 6, 2)

    def st_ps(i):
        return bank(4 + i % 2, 1)

    def tok(i):
        n, t0 = token_rows(i)
        return slice(t0, t0 + n)

    with nc.Block() as block:
        @block.sync
        def _(sp):
            sp.dma_start(uq_raw, dram["w_uq"].rearrange("(k p) n -> p k n", p=P)).then_inc(sem["uq_in"], 16)
            sp.dma_start(ukv_raw, dram["w_ukv"]).then_inc(sem["ukv_in"], 16)

        @block.gpsimd
        def _(pool):
            for k in range(3):
                nc.gpsimd.tensor_tensor(csq[:, k, :], cq[:, k, :], cq[:, k, :], ALU.mult).then_inc(sem["csq"], 1)
            pool.wait_ge(sem["uq_hi"], 1)
            nc.gpsimd.tensor_tensor(uq_l, uq_raw, f32(uq_h), ALU.subtract).then_inc(sem["uq_lo"], 1)
            pool.wait_ge(sem["ukv_hi"], 1)
            nc.gpsimd.tensor_tensor(ukv_l, ukv_raw, f32(ukv_h), ALU.subtract).then_inc(sem["uq_lo"], 1)
            for i in range(NT):
                n, _ = token_rows(i)
                pool.wait_ge(sem["v_hi"], i + 1)
                vt = v[0:n, i, :].rearrange("p (h d) -> p h d", h=HEADS)
                nc.gpsimd.tensor_tensor(vt[:, :, VD:], kvs[i % 2][0:n, :, NOPE:], f32(vt[:, :, 0:VD]), ALU.subtract)\
                  .then_inc(sem["v_lo"], 1)
                pool.wait_ge(sem["gained"], i + 1)
                if i:
                    pool.wait_ge(sem["roped"], 4 * i)
                x = qk[0:n, i, :].rearrange("p (h d) -> p h d", d=QK)[:, :, NOPE:QK]
                cs = con["rope_c"][0:n, i, :].unsqueeze(1).broadcast_to((n, 2 * HEADS, ROPE))
                sn = con["rope_s"][0:n, i, :].unsqueeze(1).broadcast_to((n, 2 * HEADS, ROPE))
                nc.gpsimd.tensor_tensor(ra[0:n], x, cs, ALU.mult).then_inc(sem["roped"], 1)
                nc.gpsimd.tensor_tensor(rp[0:n, :, 0:half], x[:, :, half:], sn[:, :, 0:half], ALU.mult)\
                  .then_inc(sem["roped"], 1)
                nc.gpsimd.tensor_tensor(rp[0:n, :, half:], x[:, :, 0:half], sn[:, :, half:], ALU.mult)\
                  .then_inc(sem["roped"], 1)
                pool.wait_ge(sem["roped"], 4 * i + 3)
                nc.gpsimd.tensor_tensor(x, ra[0:n], rp[0:n], ALU.add).then_inc(sem["roped"], 1)

        @block.scalar
        def _(act):
            for k in range(3):
                g = par[:, COLS["q_g"] + k:COLS["q_g"] + k + 1]
                nc.scalar.activation(c_h[:, k, :], cq[:, k, :], ACT.Copy, scale=g).then_inc(sem["c_hi"], 1)
            act.wait_ge(sem["uq_in"], 16)
            nc.scalar.activation(uq_h, uq_raw, ACT.Copy).then_inc(sem["uq_hi"], 1)
            act.wait_ge(sem["ukv_in"], 16)
            nc.scalar.activation(ukv_h, ukv_raw, ACT.Copy).then_inc(sem["ukv_hi"], 1)

            def kv_std(i):
                n, _ = token_rows(i)
                act.wait_ge(sem["kv_var"], i + 1)
                nc.scalar.activation(stat[0:n, i % 2, 1:2], stat[0:n, i % 2, 1:2], ACT.Sqrt).then_inc(sem["kv_std"], 1)

            kv_std(0)
            for i in range(NT):
                n, _ = token_rows(i)
                st = stat[0:n, i % 2]
                act.wait_ge(sem["q_mm"], i + 1)
                if i:
                    act.wait_ge(sem["summed"], 3 * i)
                nc.scalar.activation(qsq[0:n].rearrange("p (b h) d -> p b (h d)", b=2), q_ps[0:n], ACT.Square)\
                  .then_inc(sem["squares"], 1)
                act.wait_ge(sem["kv_mm"], i + 1)
                act.wait_ge(sem["kv_rstd"], i + 1)
                if i == 1:
                    act.wait_ge(sem["uq_lo"], 2)
                if i >= 2:
                    act.wait_ge(sem["v_lo"], i - 1)
                    act.wait_ge(sem["k_scaled"], i - 1)
                nc.scalar.activation(kvs[i % 2][0:n].rearrange("p h d -> p (h d)"), kv_ps(i)[0:n], ACT.Copy,
                                     scale=st[:, 2:3]).then_inc(sem["kvs"], 1)
                act.wait_ge(sem["kvs"], i + 1)
                nc.scalar.activation(ksq[0:n], kvs[i % 2][0:n, :, 0:NOPE], ACT.Square).then_inc(sem["squares"], 1)
                nc.scalar.activation(psq[0:n], st_ps(i)[0:n, 32:32 + ROPE], ACT.Square).then_inc(sem["squares"], 1)
                vt = v[0:n, i, :].rearrange("p (h d) -> p h d", h=HEADS)
                nc.scalar.activation(vt[:, :, 0:VD], kvs[i % 2][0:n, :, NOPE:], ACT.Copy).then_inc(sem["v_hi"], 1)
                if i + 1 < NT:
                    kv_std(i + 1)
                act.wait_ge(sem["head_var"], i + 1)
                nc.scalar.activation(st[:, 16:32], st[:, 16:32], ACT.Sqrt).then_inc(sem["head_std"], 1)

        @block.vector
        def _(dve):
            link = chain(dve, sem["dve_link2"])
            for k in range(3):
                g = par[:, COLS["q_g"] + k:COLS["q_g"] + k + 1]
                dve.wait_ge(sem["c_hi"], k + 1)
                nc.vector.scalar_tensor_tensor(out=c_l[:, k, :], in0=cq[:, k, :], scalar=g, in1=f32(c_h[:, k, :]),
                                               op0=ALU.mult, op1=ALU.subtract).then_inc(sem["c_lo"], 1)

            def latent_stats(i):
                n, _ = token_rows(i)
                dve.wait_ge(sem["st_mm"], i + 1)
                link(nc.vector.tensor_scalar(stat[0:n, i % 2, 0:1], st_ps(i)[0:n, 0:1], EPS / QL, EPS * EPS,
                                             ALU.mult, ALU.add))
                nc.vector.tensor_scalar(stat[0:n, i % 2, 1:2], st_ps(i)[0:n, 2:3], 1.0 / KVL, EPS, ALU.mult, ALU.add)\
                  .then_inc(sem["kv_var"], 1)

            def kv_rstd(i):
                n, _ = token_rows(i)
                dve.wait_ge(sem["kv_std"], i + 1)
                nc.vector.reciprocal(stat[0:n, i % 2, 2:3], stat[0:n, i % 2, 1:2]).then_inc(sem["kv_rstd"], 1)

            latent_stats(0)
            kv_rstd(0)
            for i in range(NT):
                n, _ = token_rows(i)
                st = stat[0:n, i % 2]
                if i + 1 < NT:
                    latent_stats(i + 1)
                dve.wait_ge(sem["squares"], 3 * i + 1)
                nc.vector.tensor_reduce(st[:, 16:24], qsq[0:n], AX.X, ALU.add).then_inc(sem["summed"], 1)
                dve.wait_ge(sem["squares"], 3 * i + 3)
                nc.vector.tensor_reduce(st[:, 24:32], ksq[0:n], AX.X, ALU.add).then_inc(sem["summed"], 1)
                nc.vector.tensor_reduce(st[:, 3:4], psq[0:n], AX.X, ALU.add).then_inc(sem["summed"], 1)
                if i + 1 < NT:
                    kv_rstd(i + 1)
                dve.wait_ge(sem["summed"], 3 * i + 3)
                link(nc.vector.tensor_scalar(st[:, 4:5], st[:, 3:4], QK * EPS, None, ALU.add))
                link(nc.vector.tensor_scalar(st[:, 16:24], st[:, 16:24], 1.0 / QK, st[:, 0:1], ALU.mult, ALU.add))
                nc.vector.tensor_scalar(st[:, 24:32], st[:, 24:32], st[:, 4:5], 1.0 / QK, ALU.add, ALU.mult)\
                  .then_inc(sem["head_var"], 1)
                dve.wait_ge(sem["head_std"], i + 1)
                link(nc.vector.reciprocal(st[:, 32:48], st[:, 16:32]))
                x = qk[0:n, i, :].rearrange("p (h d) -> p h d", d=QK)
                xq = x[:, 0:HEADS].rearrange("p (b h) d -> p b h d", b=2)
                for b in range(2):
                    rq = st[:, 32 + 4 * b:36 + 4 * b].unsqueeze(2).broadcast_to((n, 4, QK))
                    ins = nc.vector.tensor_tensor(xq[:, b], q_ps[0:n, b].rearrange("p (h d) -> p h d", h=4), rq, ALU.mult)
                    ins.then_inc(sem["q_scaled"], 1)
                rk = st[:, 40:48].unsqueeze(2)
                link(nc.vector.tensor_tensor(x[:, HEADS:, 0:NOPE], kvs[i % 2][0:n, :, 0:NOPE],
                                             rk.broadcast_to((n, HEADS, NOPE)), ALU.mult))
                kp = st_ps(i)[0:n, 32:32 + ROPE].unsqueeze(1).broadcast_to((n, HEADS, ROPE))
                nc.vector.tensor_tensor(x[:, HEADS:, NOPE:QK], kp, rk.broadcast_to((n, HEADS, ROPE)), ALU.mult)\
                  .then_inc(sem["k_scaled"], 1)
                dve.wait_ge(sem["k_scaled"], i + 1)
                dve.wait_ge(sem["q_scaled"], 2 * i + 2)
                x4 = qk[0:n, i, :].rearrange("p (g h d) -> p g h d", g=2, h=HEADS)
                gg = con["gqk"][0:n].unsqueeze(2).broadcast_to((n, 2, HEADS, QK))
                nc.vector.tensor_tensor(x4, x4, gg, ALU.mult).then_inc(sem["gained"], 1)

        @block.tensor
        def _(pe):
            pe.wait_ge(sem["con_in"], 64)
            for i in range(NT):
                n, _ = token_rows(i)
                if i == 0:
                    pe.wait_ge(sem["csq"], 3)
                if i >= 2:
                    pe.wait_ge(sem["k_scaled"], i - 1)
                st = st_ps(i)[0:n]
                for k in range(2):
                    nc.tensor.matmul(st[:, 0:2], csq[:, k, tok(i)], ones[:, 0:2], start=k == 0, stop=k == 1)
                nc.tensor.matmul(st[:, 2:4], csq[:, 2, tok(i)], ones[:, 0:2], start=True, stop=True)
                nc.tensor.transpose(st[:, 32:32 + ROPE], kpe_fm[:, tok(i)], ident[0:ROPE, 0:ROPE]).then_inc(sem["st_mm"], 1)
                if i == 0:
                    pe.wait_ge(sem["c_lo"], 3)
                    pe.wait_ge(sem["uq_lo"], 2)
                if i:
                    pe.wait_ge(sem["q_scaled"], 2 * i)
                for b in range(2):
                    cols = slice(b * NQ // 2, (b + 1) * NQ // 2)
                    for k in range(2):
                        ins = split_products(nc, q_ps[0:n, b], c_h[:, k, tok(i)], c_l[:, k, tok(i)],
                                             uq_h[:, k, cols], uq_l[:, k, cols], k == 0, k == 1)
                ins.then_inc(sem["q_mm"], 1)
                if i >= 2:
                    pe.wait_ge(sem["kvs"], i - 1)
                for b in range(2):
                    cols = slice(b * NKV // 2, (b + 1) * NKV // 2)
                    ins = split_products(nc, kv_ps(i)[0:n, cols], c_h[:, 2, tok(i)], c_l[:, 2, tok(i)],
                                         ukv_h[:, cols], ukv_l[:, cols], True, True)
                ins.then_inc(sem["kv_mm"], 1)


M_YM = 53208 - (KD // 2) * (SEQ + 2) - 8
M_YM -= M_YM % 8
SLOTS = NT


def attention_phase(nc, place, con, qk, v, ym, bank, dram, sem):
    at = M_2
    q_h = [place(f"q_h{b}", at + T * b, (T,), F32R, QK + 1) for b in range(2)]; at += 2 * T
    q_l = [place(f"q_l{b}", at + T * b, (T,), F32R, QK) for b in range(2)]; at += 2 * T
    k_h = [place(f"k_h{b}", at + T * b, (T,), F32R, QK + 1) for b in range(2)]; at += 2 * T
    k_l = [place(f"k_l{b}", at + T * b, (T,), F32R, QK) for b in range(2)]; at += 2 * T
    e_h = [place(f"e_h{b}", at + SEQ * b, (SEQ,), F32R) for b in range(3)]; at += 3 * SEQ
    e_l = [place(f"e_l{b}", at + SEQ * b, (SEQ,), F32R) for b in range(2)]; at += 2 * SEQ
    e_f = [place(f"e_f{b}", at + SEQ * b, (SEQ,)) for b in range(3)]; at += 3 * SEQ
    sel = place("sel", at, (XT, VD))
    es = [place(f"esum{b}", at + SEQ * b, (SEQ,)) for b in range(2)]; at += 2 * SEQ
    o_lo = place("o_lo", at, (SEQ,)); at += SEQ
    sel_r = place("sel_r", con["late"], (XT, VD), F32R, 40)
    rl_r = place("rl_r", at, (P,), F32R, 40); at += P
    NX = 2 * HEADS
    x_e = place("x_e", at, (NT, HEADS, 4), F32R); at += 2 * NT * NX
    x_v = place("x_v", at, (4, 2 * NX)); at += 8 * NX
    r_row = place("r_row", at, (P,), F32R, XT); at += P
    x_one = place("x_one", M_2 + 2 * T, (T,))[QK:QK + 2]
    x_all = place("x_all", M_2 + 4 * T + 2 * T, (T,))[QK:QK + NX]
    x_row = place("x_row", M_2 + 2 * T, (T,), parts=NX)
    assert at <= M_YM, (at, M_YM)
    SCALE = float(np.float32(1.0) / np.sqrt(np.float32(QK)))
    mx = con["lam_t"].rearrange("p a b -> p (a b)")
    mx3, mx_all, rl = mx[:, 0:3 * XT], mx[:, 24:24 + XT], mx[:, 32:32 + XT]
    ident, ones = con["ident"], con["ones"]

    def s_ps(g):
        return bank(2 * (g % 2), 2)

    o_ps = bank(4, 2)

    PREPARE = {0: ("tq0", "tq1", "", "tk0"), 1: ("", "tk1", "", "a0"), 2: ("a1", "", "a2", ""), 3: ("a3", "a4", "a5", "tm"),
               4: ("", "a6", "", "a7"), 5: ("a8", "a9", "a10", ""), 6: ("a11", "a12", "a13", ""),
               7: ("a14", "a15", "am", "r"), 8: ("", "", "", "")}
    CURRENT = {0: ("", "", "x0", ""), 1: ("x1", "", "x2", "")}
    FINISH = {2: ("", "l", "", "rt"), 4: ("b0", "", "b1", "")}
    META_QUERIES = {5: ("xt", "", "", ""), 7: ("", "", "", "xo")}
    NONE = ("", "", "", "")

    def side_jobs(h, s):
        places = [None] * 4
        for plan, head in [(PREPARE, h + 1), (CURRENT, h), (FINISH, h - 1), (META_QUERIES, h)]:
            if 0 <= head < HEADS and not (plan is META_QUERIES and h != HEADS - 1) and not (plan is CURRENT and h < 0):
                for i, kind in enumerate(plan.get(s, NONE)):
                    if kind:
                        assert places[i] is None
                        places[i] = (kind, head)
        return places

    steps = [(h, s) for h in range(-1, HEADS + 1) for s in range(SLOTS)]
    jobs = [j for h, s in steps for j in side_jobs(h, s) if j]
    number = {j: n for n, j in enumerate(jobs)}
    first = len([j for s in range(SLOTS) for j in side_jobs(-1, s) if j])
    BY_ACT = {"r", "x0", "x1", "x2"}
    HIGH = {"tq0": 1, "tq1": 1, "tk0": 1, "tk1": 1, "tm": 2, "rt": 1, "xt": 1, "xo": 1}

    def side_of(j):
        n = number[j]
        return bank([6, 7, 0, 1, 2, 3][n % 6] if n < first else 6 + (n - first) % 2, 1)

    def before(j):
        n = number[j]
        if n < first:
            return jobs[n - 6:n - 5] if n >= 6 else []
        return jobs[n - 2:n - 1] if n > first else jobs[n - 2:n]

    def hi_upto(j):
        return sum(HIGH.get(i[0], 0) for i in jobs[:number[j]])

    def wait_read(eng, j):
        same = [i for i in jobs[:number[j] + 1] if (i[0] in BY_ACT) == (j[0] in BY_ACT)]
        eng.wait_ge(sem["side_read_act" if j[0] in BY_ACT else "side_read_dve"], len(same))

    def half_of(h):
        return slice(VD * (h % 2), VD * (h % 2) + VD)

    def y_of(h):
        return ym[half_of(h), h // 2, 0:SEQ]

    def rows(g):
        return P if g % SLOTS < XT else META

    G = HEADS * SLOTS

    def summed(g):
        return XT * (g // SLOTS) + max(g % SLOTS, 1)

    with nc.Block() as block:
        @block.sync
        def _(sp):
            sp.dma_start(sel, dram["sel"]).then_inc(sem["sel_in"], 16)
            for h in range(HEADS):
                wait_read(sp, ("r", h))
                sp.dma_start(f32(q_h[h % 2][QK:QK + 1, 0:SEQ].rearrange("p (t n) -> p t n", n=P)), f32(r_row))\
                  .then_inc(sem["row_in"], 16)
                wait_read(sp, ("x2", h))
                sp.dma_start(x_all[2 * h:2 * h + 2], x_one).then_inc(sem["x_in"], 16)
            sp.wait_ge(sem["x_in"], 16 * HEADS)
            sp.wait_ge(sem["pv_done"], G - 3 * SLOTS)
            sp.dma_start(x_row, x_all).then_inc(sem["x_row_in"], 16)

        @block.gpsimd
        def _(pool):
            sets = [0]

            def settle(ins):
                sets[0] += 1
                ins.then_inc(sem["b_set"], 1)
                pool.wait_ge(sem["b_set"], sets[0])

            for b in range(2):
                settle(nc.gpsimd.memset(f32(k_h[b][QK:QK + 1, 0:T]), 1.0))
            settle(nc.gpsimd.memset(f32(rl_r), 0.0))
            pool.wait_ge(sem["sel_in"], 16)
            settle(nc.gpsimd.tensor_copy(sel_r, sel[0:40]))
            for h in range(HEADS + 1):
                for s in range(SLOTS):
                    g = SLOTS * h + s
                    n = rows(g)
                    if g < G:
                        pool.wait_ge(sem["e_full"], g + 1)
                        e = e_f[g % 3]
                        if s == 1:
                            if h >= 2:
                                pool.wait_ge(sem["side_done"], number[("l", h - 2)] + 1)
                            if h >= 1:
                                pool.wait_ge(sem["e_summed"], summed(g - 2))
                            nc.gpsimd.tensor_tensor(es[h % 2], e_f[(g - 1) % 3], e, ALU.add).then_inc(sem["e_summed"], 1)
                        elif s > 1:
                            if h >= 1 and s == 3:
                                pool.wait_ge(sem["o_sum"], h)
                            pool.wait_ge(sem["e_summed"], summed(g - 1))
                            nc.gpsimd.tensor_tensor(es[h % 2][0:n], es[h % 2][0:n], e[0:n], ALU.add)\
                              .then_inc(sem["e_summed"], 1)
                    if h >= 1 and s == 2:
                        pool.wait_ge(sem["o_hi"], h)
                        pool.wait_ge(sem["o_low"], h)
                        pool.wait_ge(sem["e_summed"], summed(min(g, G - 1)))
                        y = y_of(h - 1)
                        nc.gpsimd.tensor_tensor(y, y, o_lo[half_of(h - 1)], ALU.add).then_inc(sem["o_sum"], 1)

        @block.scalar
        def _(act):
            def job(j):
                kind, h = j
                b = h % 2
                side = side_of(j)
                if kind in HIGH or kind in BY_ACT:
                    act.wait_ge(sem["side_done"], number[j] + 1)
                if kind[:2] in ("tq", "tk"):
                    c = int(kind[2])
                    out = (q_h if kind[1] == "q" else k_h)[b]
                    ins = nc.scalar.activation(out[0:QK, 512 * c:512 * c + 512], side[0:QK], ACT.Copy)
                elif kind == "tm":
                    nc.scalar.activation(q_h[b][0:QK, SEQ:T], side[0:QK, 0:META], ACT.Copy).then_inc(sem["side_hi"], 1)
                    ins = nc.scalar.activation(k_h[b][0:QK, SEQ:T], side[0:QK, META:2 * META], ACT.Copy)
                elif kind == "rt":
                    ins = nc.scalar.activation(rl_r[0:XT], side[0:XT, 0:P], ACT.Copy)
                elif kind == "xt":
                    ins = nc.scalar.activation(x_e.rearrange("p t h c -> p (t h) c")[:, :, 0:2],
                                               side[:, 0:NT * NX].rearrange("p (n c) -> p n c", c=2), ACT.Copy)
                elif kind == "xo":
                    ins = nc.scalar.activation(x_v[0:VD, 0, :], side[VD:P, 0:2 * NX], ACT.Copy)
                elif kind == "r":
                    if h:
                        act.wait_ge(sem["row_in"], 16 * h)
                    nc.scalar.activation(r_row, side[0:XT, 0:P], ACT.Copy, scale=-1.0).then_inc(sem["side_read_act"], 1)
                    return
                elif kind[0] == "x":
                    c = int(kind[1])
                    w = 512 if c < 2 else META
                    if h and c == 0:
                        act.wait_ge(sem["x_in"], 16 * h)
                    nc.scalar.activation(x_one[:, 512 * c:512 * c + w], side[0:2, 0:w], ACT.Copy)\
                      .then_inc(sem["side_read_act"], 1)
                    return
                else:
                    return
                ins.then_inc(sem["side_hi"], 1)

            act.wait_ge(sem["b_set"], 4)
            for h, s in steps:
                g = SLOTS * h + s
                if h >= 1 and s == 2:
                    act.wait_ge(sem["pv_done"], SLOTS * h)
                    if h >= 2:
                        act.wait_ge(sem["o_sum"], h - 1)
                    nc.scalar.activation(o_lo[half_of(h - 1)], o_ps[VD:P], ACT.Copy).then_inc(sem["o_low"], 1)
                js = side_jobs(h, s)
                for j in js[0:2]:
                    if j:
                        job(j)
                if 0 <= g < G:
                    n = rows(g)
                    act.wait_ge(sem["s_done"], g + 1)
                    if g >= 3:
                        act.wait_ge(sem["e_summed"], summed(g - 3))
                        act.wait_ge(sem["e_lo"], 2 * (g - 2))
                        act.wait_ge(sem["pv_done"], g - 2)
                    nc.scalar.activation(e_f[g % 3][0:n], s_ps(g)[0:n], ACT.Exp, scale=SCALE).then_inc(sem["e_full"], 1)
                    nc.scalar.activation(e_h[g % 3][0:n], s_ps(g)[0:n], ACT.Exp, scale=SCALE).then_inc(sem["e_hi"], 1)
                if h == HEADS - 1 and s == 4:
                    act.wait_ge(sem["x_max"], 1)
                    nc.scalar.activation(x_row, x_row, ACT.Exp, bias=x_v[0:NX, 3, 0:1], scale=SCALE)\
                      .then_inc(sem["x_exp"], 1)
                for j in js[2:4]:
                    if j:
                        job(j)

        @block.vector
        def _(dve):
            link = chain(dve, sem["dve_link3"])
            n_hi = [0]

            def job(j):
                kind, h = j
                b = h % 2
                side = side_of(j)
                if kind in HIGH:
                    n_hi[0] += HIGH[kind]
                    dve.wait_ge(sem["side_hi"], n_hi[0])
                elif kind not in BY_ACT:
                    dve.wait_ge(sem["side_done"], number[j] + 1)
                if kind[:2] in ("tq", "tk"):
                    cs = slice(512 * int(kind[2]), 512 * int(kind[2]) + 512)
                    hi, lo = (q_h[b], q_l[b]) if kind[1] == "q" else (k_h[b], k_l[b])
                    ins = nc.vector.tensor_tensor(lo[:, cs], side[0:QK], f32(hi[0:QK, cs]), ALU.subtract)
                elif kind == "tm":
                    nc.vector.tensor_tensor(q_l[b][:, SEQ:T], side[0:QK, 0:META], f32(q_h[b][0:QK, SEQ:T]), ALU.subtract)\
                      .then_inc(sem["q_low_meta"], 1)
                    ins = nc.vector.tensor_tensor(k_l[b][:, SEQ:T], side[0:QK, META:2 * META], f32(k_h[b][0:QK, SEQ:T]),
                                                  ALU.subtract)
                elif kind[0] == "a" and kind != "am":
                    i = int(kind[1:])
                    ins = nc.vector.tensor_reduce(mx3[:, i:i + 1], side, AX.X, ALU.max)
                elif kind == "am":
                    s3 = side[:, 0:XT * META].rearrange("p (i n) -> p i n", n=META)
                    link(nc.vector.tensor_reduce(mx3[:, 2 * XT:3 * XT], s3, AX.X, ALU.max))
                    wait_read(dve, ("a15", h))
                    ins = nc.vector.tensor_reduce(mx_all, mx3.rearrange("p (c t) -> p t c", c=3), AX.X, ALU.max)
                elif kind == "l":
                    ins = nc.vector.reciprocal(rl, side[:, 0:2 * XT].rearrange("p (i t) -> p i t", t=2)[:, :, 0])
                elif kind == "rt":
                    ins = nc.vector.tensor_tensor(rl_r[32:32 + XT], side[0:XT, 0:P], f32(rl_r[0:XT]), ALU.subtract)
                elif kind in ("b0", "b1"):
                    c = int(kind[1])
                    y = y_of(h)[:, 512 * c:512 * c + 512]
                    dve.wait_ge(sem["o_sum"], h + 1)
                    ins = nc.vector.tensor_tensor(y, side[0:VD], y, ALU.mult)
                elif kind == "xt":
                    xe = x_e.rearrange("p t h c -> p (t h) c")
                    ins = nc.vector.tensor_tensor(xe[:, :, 2:4], side[:, 0:NT * NX].rearrange("p (n c) -> p n c", c=2),
                                                  f32(xe[:, :, 0:2]), ALU.subtract)
                elif kind == "xo":
                    link(nc.vector.tensor_tensor(x_v[0:VD, 1, :], side[0:VD, 0:2 * NX], x_v[0:VD, 0, :], ALU.add))
                    x4 = x_v[0:VD, 1, :].rearrange("p (h w c) -> p h w c", w=2, c=2)
                    for o in range(2):
                        ins = nc.vector.tensor_tensor(ym[VD * o:VD * o + VD, :, SEQ:SEQ + 2], x4[:, o::2, 0],
                                                      x4[:, o::2, 1], ALU.add)
                        ins.then_inc(sem["x_y" if o == 0 else "side_read_dve"], 1)
                    return
                else:
                    return
                ins.then_inc(sem["side_read_dve"], 1)

            dve.wait_ge(sem["b_set"], 4)
            for h, s in steps:
                g = SLOTS * h + s
                if h >= 1 and s == 2:
                    dve.wait_ge(sem["pv_done"], SLOTS * h)
                    nc.vector.tensor_copy(y_of(h - 1), o_ps[0:VD]).then_inc(sem["o_hi"], 1)
                js = side_jobs(h, s)
                split = 0 <= g - 1 < G
                n = rows(g - 1)

                def low_half(c):
                    cs = slice(512 * c, 512 * c + 512)
                    nc.vector.tensor_tensor(e_l[(g - 1) % 2][0:n, cs], e_f[(g - 1) % 3][0:n, cs],
                                            f32(e_h[(g - 1) % 3][0:n, cs]), ALU.subtract).then_inc(sem["e_lo"], 1)

                if js[0]:
                    job(js[0])
                if split:
                    dve.wait_ge(sem["e_hi"], g)
                    if g - 1 >= 2:
                        dve.wait_ge(sem["pv_done"], g - 2)
                    low_half(0)
                for j in js[1:3]:
                    if j:
                        job(j)
                if split:
                    low_half(1)
                if js[3]:
                    job(js[3])
                if h == HEADS - 1 and s == 3:
                    dve.wait_ge(sem["x_row_in"], 16)
                    link(nc.vector.tensor_reduce(x_v[0:NX, 3, 0:1], x_row, AX.X, ALU.max))
                    nc.vector.tensor_scalar(x_v[0:NX, 3, 0:1], x_v[0:NX, 3, 0:1], -SCALE, None, ALU.mult)\
                      .then_inc(sem["x_max"], 1)
                if h == HEADS - 1 and s == 4:
                    dve.wait_ge(sem["x_exp"], 1)
                    link(nc.vector.tensor_reduce(x_v[0:NX, 3, 1:2], x_row, AX.X, ALU.add))
                    link(nc.vector.reciprocal(x_v[0:NX, 3, 2:3], x_v[0:NX, 3, 1:2]))
                    nc.vector.tensor_scalar(x_row, x_row, x_v[0:NX, 3, 2:3], None, ALU.mult).then_inc(sem["x_prob"], 1)

        @block.tensor
        def _(pe):
            def tile_of(i):
                return slice(P * i, P * i + P) if i < XT else slice(SEQ, T)

            def job(j):
                kind, h = j
                b = h % 2
                side = side_of(j)
                for i in before(j):
                    wait_read(pe, i)
                if kind[:2] in ("tq", "tk"):
                    c0 = QK * (h + (HEADS if kind[1] == "k" else 0))
                    for t in range(4):
                        ins = nc.tensor.transpose(side[0:QK, P * t:P * t + P], qk[:, 4 * int(kind[2]) + t, c0:c0 + QK], ident)
                elif kind == "tm":
                    for w in range(2):
                        c0 = QK * (h + HEADS * w)
                        ins = nc.tensor.transpose(side[0:QK, META * w:META * w + META], qk[0:META, XT, c0:c0 + QK],
                                                  ident[0:META, 0:META])
                elif kind == "am":
                    pe.wait_ge(sem["side_hi"], hi_upto(j))
                    for t in range(XT):
                        ins = nc.tensor.matmul(side[:, META * t:META * t + META], q_h[b][0:QK, tile_of(t)],
                                               k_h[b][0:QK, SEQ:T], start=True, stop=True)
                elif kind[0] == "a":
                    pe.wait_ge(sem["side_hi"], hi_upto(j))
                    c, t = divmod(int(kind[1:]), XT)
                    ins = nc.tensor.matmul(side, q_h[b][0:QK, tile_of(t)], k_h[b][0:QK, 512 * c:512 * c + 512],
                                           start=True, stop=True)
                elif kind == "r":
                    wait_read(pe, ("am", h))
                    ins = nc.tensor.transpose(side[0:XT, 0:P], mx_all, ident)
                elif kind == "l":
                    pe.wait_ge(sem["e_summed"], XT * (h + 1))
                    for t in range(XT):
                        ins = nc.tensor.matmul(side[:, 2 * t:2 * t + 2], es[h % 2][:, tile_of(t)], ones[:, 0:2],
                                               start=True, stop=True)
                elif kind == "rt":
                    wait_read(pe, ("l", h))
                    ins = nc.tensor.transpose(side[0:XT, 0:P], rl, ident)
                elif kind in ("b0", "b1"):
                    wait_read(pe, ("rt", h))
                    for t in range(4):
                        ins = nc.tensor.matmul(side[0:VD, tile_of(t)], sel_r[:, 4 * int(kind[1]) + t, :], rl_r,
                                               start=True, stop=True)
                elif kind in ("x0", "x1", "x2"):
                    c = int(kind[1])
                    w = 512 if c < 2 else META
                    ks, qs = slice(512 * c, 512 * c + w), slice(T - 2, T)
                    if c == 0:
                        wait_read(pe, ("tm", h))
                    nc.tensor.matmul(side[0:2, 0:w], q_h[b][0:QK, qs], k_h[b][0:QK, ks], start=True, stop=False)
                    nc.tensor.matmul(side[0:2, 0:w], q_l[b][:, qs], k_h[b][0:QK, ks], start=False, stop=False)
                    ins = nc.tensor.matmul(side[0:2, 0:w], q_h[b][0:QK, qs], k_l[b][:, ks], start=False, stop=True)
                elif kind == "xt":
                    pe.wait_ge(sem["x_prob"], 1)
                    for t in range(NT):
                        n = rows(t)
                        ins = nc.tensor.transpose(side[0:n, NX * t:NX * t + NX], x_row[:, P * t:P * t + n],
                                                  ident[0:NX, 0:NX])
                elif kind == "xo":
                    ins = meta_pv(HEADS - 1)
                ins.then_inc(sem["side_done"], 1)

            def meta_pv(m):
                side = side_of(("xo", HEADS - 1))
                if m == 0:
                    wait_read(pe, ("xt", HEADS - 1))
                for t in range(NT):
                    n = rows(t)
                    ins = nc.tensor.matmul(side[:, 4 * m:4 * m + 4], v[0:n, t, 2 * VD * m:2 * VD * (m + 1)],
                                           x_e[0:n, t, m, :], start=t == 0, stop=t == XT)
                return ins

            def place_job(h, s, js, i):
                if js[i]:
                    job(js[i])
                elif h == HEADS - 1 and s in (6, 7):
                    meta_pv(4 * (s - 6) + i)

            def scores(g, c):
                h, s = divmod(g, SLOTS)
                b = h % 2
                ks = slice(P * s, P * s + rows(g))
                cs = slice(512 * c, 512 * c + 512)
                if c == 0:
                    if s == 0:
                        pe.wait_ge(sem["row_in"], 16 * (h + 1))
                    if g >= 2:
                        pe.wait_ge(sem["e_hi"], g - 1)
                out = s_ps(g)[0:rows(g), cs]
                nc.tensor.matmul(out, k_h[b][:, ks], q_h[b][:, cs], start=True, stop=False)
                nc.tensor.matmul(out, k_h[b][0:QK, ks], q_l[b][:, cs], start=False, stop=False)
                ins = nc.tensor.matmul(out, k_l[b][:, ks], q_h[b][0:QK, cs], start=False, stop=True)
                if c == 1:
                    ins.then_inc(sem["s_done"], 1)

            def pv(g, c):
                h, s = divmod(g, SLOTS)
                n = rows(g)
                pe.wait_ge(sem["e_lo"], 2 * g + 1 + c)
                if s == 0 and h and c == 0:
                    pe.wait_ge(sem["o_low"], h)
                    pe.wait_ge(sem["o_hi"], h)
                vt = v[0:n, s, 2 * VD * h:2 * VD * (h + 1)]
                cs = slice(512 * c, 512 * c + 512)
                nc.tensor.matmul(o_ps[:, cs], vt, e_h[g % 3][0:n, cs], start=s == 0, stop=False)
                ins = nc.tensor.matmul(o_ps[:, cs], vt, e_l[g % 2][0:n, cs], start=False, stop=s == XT)
                if c == 1:
                    ins.then_inc(sem["pv_done"], 1)

            pe.wait_ge(sem["b_set"], 4)
            for h, s in steps:
                js = side_jobs(h, s)
                g = SLOTS * h + s
                for c in range(2):
                    if 0 <= g < G:
                        scores(g, c)
                    place_job(h, s, js, c)
                for c in range(2):
                    if 0 <= g - 2 < G:
                        pv(g - 2, c)
                    place_job(h, s, js, 2 + c)


Q2 = SEQ + 2
M_H = M_A
M_HN = M_H + XT * D
M_HNL = M_HN + KD * Q2
M_3 = M_HNL + KD * Q2


def out_phase(nc, place, con, yl, ym, h, hn_h, hn_l, bank, dram, sem):
    half = D // 2
    at = M_3
    wo_h = [place("wo_h0", M_HN, (KD, half), F32R), place("wo_h1", at, (KD, half), F32R)]; at += KD * half
    wo_l = [place("wo_l0", M_HN + KD * half, (KD, half), F32R), place("wo_l1", at, (KD, half), F32R)]; at += KD * half
    ys_at = M_HN + 2 * KD * half
    ysum = [place(f"ysum{w}", ys_at + (Q2 + 6) * w, (Q2,)) for w in range(2)]
    ysq = [place(f"ysq{w}", ys_at + (Q2 + 6) * (2 + w), (Q2,)) for w in range(2)]
    assert ys_at + 4 * (Q2 + 6) <= M_3
    y_h = [place(f"y_h{b}", at + 2048 * b, (KD, P), F32R) for b in range(2)]
    y_l = [place(f"y_l{b}", at + 2048 * b + 1024, (KD, P), F32R) for b in range(2)]; at += 4096
    raw = [place(f"wo_raw{b}", at + half * b, (half,)) for b in range(4)]; at += 4 * half
    hn = place("hn", at, (D,)); at += D
    fg = place("ffn_g", at, (D,)); at += D
    hm = place("h_meta", at, (D,), parts=2); at += D
    junk = place("h_sq", at, (D,)); at += D
    assert at <= M_YM, (at, M_YM)
    par, ident, ones = con["par"], con["ident"], con["ones"]
    stat = con["stat"].rearrange("p a b -> p (a b)")
    r_y, ss2, r2 = stat[:, 0:2 * NT], stat[:, 32:32 + NT], stat[:, 48:48 + NT]
    side = bank(6, 2)

    def rows(i):
        return P if i < XT else 2

    def cols(i):
        return slice(2 + P * i, 2 + P * i + P) if i < XT else slice(0, 2)

    def yl_cols(i):
        return slice(META + P * i, META + P * i + P) if i < XT else slice(META - 2, META)

    def ym_cols(i):
        return slice(P * i, P * i + P) if i < XT else slice(SEQ, Q2)

    units = [(c, i) for c in range(2) for i in [XT] + list(range(XT))]

    def res(i):
        return h[:, i, :] if i < XT else hm

    with nc.Block() as block:
        @block.sync
        def _(sp):
            for c in range(2):
                for k in range(KD):
                    m = KD * c + k
                    if m >= 4:
                        sp.wait_ge(sem["wo_lo"], m - 3)
                    sp.dma_start(raw[m % 4], dram["w_out"][P * k:P * k + P, half * c:half * c + half])\
                      .then_inc(sem["wo_in"][m % 4], 16)
                if c == 0:
                    sp.dma_start(hm, dram["meta_tm"][META - 2:META, :]).then_inc(sem["res_in"], 16)
                    sp.dma_start(fg, dram["ffn_g"]).then_inc(sem["res_in"], 16)
                    for i in range(XT):
                        sp.dma_start(h[:, i, :], dram["x_tm"][P * i:P * i + P, :]).then_inc(sem["res_in"], 16)

        @block.gpsimd
        def _(pool):
            for u, (c, i) in enumerate(units):
                n = rows(i)
                pool.wait_ge(sem["y_hi"], 2 * u + 1)
                nc.gpsimd.tensor_tensor(y_l[u % 2][:, 0:LF, 0:n], yl[:, :, yl_cols(i)], f32(y_h[u % 2][:, 0:LF, 0:n]),
                                        ALU.subtract).then_inc(sem["y_lo"], 1)
                pool.wait_ge(sem["y_hi"], 2 * u + 2)
                nc.gpsimd.tensor_tensor(y_l[u % 2][:, LF:, 0:n], ym[:, :, ym_cols(i)], f32(y_h[u % 2][:, LF:, 0:n]),
                                        ALU.subtract).then_inc(sem["y_lo"], 1)

        @block.scalar
        def _(act):
            def split_y(u):
                c, i = units[u]
                n = rows(i)
                if u >= 2:
                    act.wait_ge(sem["wo_mm"], u - 1)
                nc.scalar.activation(y_h[u % 2][:, 0:LF, 0:n], yl[:, :, yl_cols(i)], ACT.Copy).then_inc(sem["y_hi"], 1)
                nc.scalar.activation(y_h[u % 2][:, LF:, 0:n], ym[:, :, ym_cols(i)], ACT.Copy).then_inc(sem["y_hi"], 1)

            def split_w(m):
                k = m % KD
                act.wait_ge(sem["wo_in"][m % 4], 16 * (m // 4 + 1))
                g = par[:, COLS["out_g"] + k:COLS["out_g"] + k + 1]
                nc.scalar.activation(wo_h[m // KD][:, k, :], raw[m % 4], ACT.Copy, scale=g).then_inc(sem["wo_hi"], 1)

            split_y(0)
            split_y(1)
            for k in range(KD):
                split_w(k)
            for k in range(KD):
                w = k // LF
                if k >= 2:
                    act.wait_ge(sem["ysum"], k - 1)
                if w == 0:
                    nc.scalar.activation(ysq[k % 2][:, 0:2], yl[:, k, META - 2:META], ACT.Square).then_inc(sem["ysq"], 1)
                    nc.scalar.activation(ysq[k % 2][:, 2:], yl[:, k, META:], ACT.Square).then_inc(sem["ysq"], 1)
                else:
                    nc.scalar.activation(ysq[k % 2][:, 0:2], ym[:, k - LF, SEQ:], ACT.Square).then_inc(sem["ysq"], 1)
                    nc.scalar.activation(ysq[k % 2][:, 2:], ym[:, k - LF, 0:SEQ], ACT.Square).then_inc(sem["ysq"], 1)
            act.wait_ge(sem["y_var"], 2)
            nc.scalar.activation(r_y[:, 0:2 * XT], r_y[:, 0:2 * XT], ACT.Sqrt).then_inc(sem["y_std"], 1)
            nc.scalar.activation(r_y[0:2, 2 * XT:], r_y[0:2, 2 * XT:], ACT.Sqrt).then_inc(sem["y_std"], 1)

            def square_h(t):
                i = units[NT + t][1]
                n = rows(i)
                act.wait_ge(sem["h_done"], 2 * (NT + t) + 2)
                nc.scalar.activation(junk[0:n], res(i)[0:n], ACT.Square, accum_out=ss2[0:n, t:t + 1]).then_inc(sem["h_sq"], 1)

            def std_h(t):
                n = rows(units[NT + t][1])
                act.wait_ge(sem["h_var"], t + 1)
                nc.scalar.activation(ss2[0:n, t:t + 1], ss2[0:n, t:t + 1], ACT.Sqrt).then_inc(sem["h_std"], 1)

            def high_h(t):
                i = units[NT + t][1]
                n = rows(i)
                act.wait_ge(sem["hn_t"], t + 1)
                if t == 0:
                    act.wait_ge(sem["wo_mm"], NT)
                nc.scalar.activation(hn_h[:, :, cols(i)], side.rearrange("p (k n) -> p k n", k=KD)[:, :, 0:n], ACT.Copy)\
                  .then_inc(sem["hn_hi"], 1)

            for u in range(2, 2 * NT):
                split_y(u)
                if u - 2 < KD:
                    split_w(KD + u - 2)
                t = u - NT - 1
                if t >= 0:
                    square_h(t)
                    std_h(t)
                if t >= 1:
                    high_h(t - 1)
            square_h(NT - 1)
            std_h(NT - 1)
            high_h(NT - 2)
            high_h(NT - 1)

        @block.vector
        def _(dve):
            link = chain(dve, sem["dve_link4"])

            def split_w(m):
                k = m % KD
                g = par[:, COLS["out_g"] + k:COLS["out_g"] + k + 1]
                dve.wait_ge(sem["wo_hi"], m + 1)
                nc.vector.scalar_tensor_tensor(out=wo_l[m // KD][:, k, :], in0=raw[m % 4], scalar=g,
                                               in1=f32(wo_h[m // KD][:, k, :]), op0=ALU.mult, op1=ALU.subtract)\
                  .then_inc(sem["wo_lo"], 1)

            for k in range(KD):
                split_w(k)
            for k in range(KD):
                w = k // LF
                dve.wait_ge(sem["ysq"], 2 * k + 2)
                if k % LF == 0:
                    nc.vector.tensor_copy(ysum[w], ysq[k % 2]).then_inc(sem["ysum"], 1)
                else:
                    dve.wait_ge(sem["ysum"], k)
                    nc.vector.tensor_tensor(ysum[w], ysum[w], ysq[k % 2], ALU.add).then_inc(sem["ysum"], 1)
            dve.wait_ge(sem["yss_mm"], 1)
            ss = side[:, 0:4 * NT].rearrange("p (i t) -> p i t", t=2)[:, :, 0]
            nc.vector.tensor_scalar(r_y[:, 0:2 * XT], ss[:, 0:2 * XT], 1.0 / LRU, EPS, ALU.mult, ALU.add)\
              .then_inc(sem["y_var"], 1)
            nc.vector.tensor_scalar(r_y[0:2, 2 * XT:], ss[0:2, 2 * XT:], 1.0 / LRU, EPS, ALU.mult, ALU.add)\
              .then_inc(sem["y_var"], 1)
            dve.wait_ge(sem["y_std"], 2)
            link(nc.vector.reciprocal(r_y[:, 0:2 * XT], r_y[:, 0:2 * XT]))
            link(nc.vector.reciprocal(r_y[0:2, 2 * XT:], r_y[0:2, 2 * XT:]))
            dve.wait_ge(sem["res_in"], 16 * (2 + XT))

            def add_groups(u):
                c, i = units[u]
                n = rows(i)
                cs = slice(half * c, half * c + half)
                dve.wait_ge(sem["wo_mm"], u + 1)
                for w in range(2):
                    r = r_y[0:n, 2 * i + w:2 * i + w + 1]
                    nc.vector.scalar_tensor_tensor(out=res(i)[0:n, cs], in0=bank(2 * (u % 3) + w)[0:n], scalar=r,
                                                   in1=res(i)[0:n, cs], op0=ALU.mult, op1=ALU.add)\
                      .then_inc(sem["h_done"], 1)
                    dve.wait_ge(sem["h_done"], 2 * u + w + 1)

            def normalise(t):
                i = units[NT + t][1]
                n = rows(i)
                dve.wait_ge(sem["h_sq"], t + 1)
                nc.vector.tensor_scalar(ss2[0:n, t:t + 1], ss2[0:n, t:t + 1], 1.0 / D, EPS, ALU.mult, ALU.add)\
                  .then_inc(sem["h_var"], 1)
                dve.wait_ge(sem["h_std"], t + 1)
                link(nc.vector.reciprocal(r2[0:n, t:t + 1], ss2[0:n, t:t + 1]))
                if t:
                    dve.wait_ge(sem["hn_t"], t)
                nc.vector.scalar_tensor_tensor(out=hn[0:n], in0=res(i)[0:n], scalar=r2[0:n, t:t + 1], in1=fg[0:n],
                                               op0=ALU.mult, op1=ALU.mult).then_inc(sem["hn"], 1)

            def low_h(t):
                i = units[NT + t][1]
                n = rows(i)
                dve.wait_ge(sem["hn_hi"], t + 1)
                nc.vector.tensor_tensor(hn_l[:, :, cols(i)], side.rearrange("p (k n) -> p k n", k=KD)[:, :, 0:n],
                                        f32(hn_h[:, :, cols(i)]), ALU.subtract).then_inc(sem["hn_lo"], 1)

            for u in range(2 * NT):
                add_groups(u)
                if u < KD:
                    split_w(KD + u)
                t = u - NT
                if t >= 0:
                    normalise(t)
                if t >= 1:
                    low_h(t - 1)
            low_h(NT - 1)

        @block.tensor
        def _(pe):
            def transpose_h(t):
                n = rows(units[NT + t][1])
                pe.wait_ge(sem["hn"], t + 1)
                if t:
                    pe.wait_ge(sem["hn_lo"], t)
                for k in range(KD):
                    ins = nc.tensor.transpose(side[:, P * k:P * k + n], hn[0:n, P * k:P * k + P], ident[0:n, 0:n])
                ins.then_inc(sem["hn_t"], 1)

            for u, (c, i) in enumerate(units):
                n = rows(i)
                pe.wait_ge(sem["y_lo"], 2 * u + 2)
                if u >= 3:
                    pe.wait_ge(sem["h_done"], 2 * (u - 2))
                for k in range(KD):
                    if u == 0 or (c == 1 and u == NT):
                        pe.wait_ge(sem["wo_lo"], KD * c + k + 1)
                    w = k // LF
                    ins = split_products(nc, bank(2 * (u % 3) + w)[0:n], y_h[u % 2][:, k, 0:n], y_l[u % 2][:, k, 0:n],
                                         wo_h[c][:, k, :], wo_l[c][:, k, :], k % LF == 0, k % LF == LF - 1)
                ins.then_inc(sem["wo_mm"], 1)
                if u == 1:
                    pe.wait_ge(sem["ysum"], KD)
                    for j in range(NT):
                        m = rows(j)
                        for w in range(2):
                            o = side[0:m, 2 * (2 * j + w):2 * (2 * j + w) + 2]
                            ins = nc.tensor.matmul(o, ysum[w][:, cols(j)], ones[:, 0:2], start=True, stop=True)
                    ins.then_inc(sem["yss_mm"], 1)
                t = u - NT - 1
                if t >= 0:
                    if t == 0:
                        pe.wait_ge(sem["y_var"], 2)
                    transpose_h(t)
            transpose_h(NT - 1)


def ffn_phase(nc, place, con, h, hn_h, hn_l, bank, dram, out, sem):
    at = M_3
    up_raw = place("up_raw", at, (2 * KD, P)); at += 2 * KD * P
    up_h, up_l, dn_h, dn_l, a_h, a_l, dn_raw = [], [], [], [], [], [], []
    for e in range(2):
        up_h.append(place(f"up_h{e}", at, (2 * KD, P), F32R)); at += 2 * KD * P
        up_l.append(place(f"up_l{e}", at, (2 * KD, P), F32R)); at += 2 * KD * P
        dn_h.append(place(f"dn_h{e}", at, (D,), F32R)); at += D
        dn_l.append(place(f"dn_l{e}", at, (D,), F32R)); at += D
        a_h.append(place(f"a_h{e}", at, (SEQ,), F32R)); at += SEQ
        a_l.append(place(f"a_l{e}", at, (SEQ,), F32R)); at += SEQ
        dn_raw.append(place(f"dn_raw{e}", at, (D,))); at += D
    assert at <= 53208, at
    at = M_YL
    gs = place("gate", at, (Q2 + 2,)); at += Q2 + 6
    cv = place("gate_conv", at, (SEQ,)); at += SEQ
    pr = place("ffn_act", at, (SEQ,)); at += SEQ
    par = con["par"]
    third = Q2 // 3
    assert third * 3 == Q2 and third % 2 == 0
    GROUPS = NFF // 2
    NU = 2 * XT

    g_ps = bank(0, 3).rearrange("p (c n) -> p c n", c=3)[:, :, 0:third]
    u_ps = bank(3, 2)

    def over_groups(eng, first, steady, last):
        first(0)
        with eng.Fori(1, GROUPS - 1) as g:
            steady(g)
        last(GROUPS - 1)

    with nc.Block() as block:
        @block.sync
        def _(sp):
            def load(g, wait=True):
                for e in range(2):
                    t = 2 * g + e
                    if wait or e:
                        sp.wait_ge(sem["up_lo"], t)
                    sp.dma_start(up_raw, dram["w_up"][bass.ds(t, 1)].rearrange("o p a k n -> p (o a k) n"))\
                      .then_inc(sem["up_in"], 16)
                    if wait:
                        sp.wait_ge(sem["dn_lo"], t - 1)
                    sp.dma_start(dn_raw[e], dram["w_down"].rearrange("(t p) n -> t p n", p=P)[bass.ds(t, 1)]
                                 .rearrange("o p n -> p (o n)")).then_inc(sem["dn_in"][e], 16)

            load(0, False)
            with sp.Fori(1, GROUPS) as g:
                load(g)
            for u in range(NU):
                i, c = divmod(u, 2)
                sp.wait_ge(sem["dn_read"], NU * (GROUPS - 1) + u + 1)
                sp.dma_start(out[P * i:P * i + P, 512 * c:512 * c + 512], h[:, i, 512 * c:512 * c + 512])\
                  .then_inc(sem["stored"], 16)
            sp.wait_ge(sem["stored"], 16 * NU)

        @block.gpsimd
        def _(pool):
            def low_up(t, e, first=False):
                pool.wait_ge(sem["up_hi"], t + 1)
                nc.gpsimd.tensor_tensor(up_l[e], up_raw, f32(up_h[e]), ALU.subtract).then_inc(sem["up_lo"], 1)

            def low_dn(t, e):
                pool.wait_ge(sem["dn_hi"], t + 1)
                nc.gpsimd.tensor_tensor(dn_l[e], dn_raw[e], f32(dn_h[e]), ALU.subtract).then_inc(sem["dn_lo"], 1)

            low_up(0, 0)
            low_up(1, 1)

            def group(g, more=True):
                for e in range(2):
                    low_dn(2 * g + e, e)
                    if more:
                        low_up(2 * g + 2 + e, e)

            over_groups(pool, group, group, lambda g: group(g, False))

        @block.scalar
        def _(act):
            def high_up(t, e):
                act.wait_ge(sem["up_in"], 16 * t + 16)
                nc.scalar.activation(up_h[e], up_raw, ACT.Copy).then_inc(sem["up_hi"], 1)

            high_up(0, 0)
            high_up(1, 1)

            def group(g, down=True, more=True):
                for e in range(2):
                    t = 2 * g + e
                    act.wait_ge(sem["gate_mm"], t + 1)
                    if down or e:
                        act.wait_ge(sem["conv2"], t)
                    nc.scalar.activation(gs[:, 0:Q2].rearrange("p (c n) -> p c n", c=3), g_ps, ACT.Copy)\
                      .then_inc(sem["gate_read"], 1)
                    act.wait_ge(sem["conv2"], t + 1)
                    nc.scalar.activation(cv, cv, ACT.Silu).then_inc(sem["silu"], 1)
                    act.wait_ge(sem["prod"], t + 1)
                    if down:
                        act.wait_ge(sem["dn_mm"], NU * g)
                    nc.scalar.activation(a_h[e], pr, ACT.Copy).then_inc(sem["a_hi"], 1)
                    act.wait_ge(sem["dn_in"][e], 16 * g + 16)
                    nc.scalar.activation(dn_h[e], dn_raw[e], ACT.Copy).then_inc(sem["dn_hi"], 1)
                    if more:
                        act.wait_ge(sem["up_mm"], t + 1)
                        high_up(t + 2, e)

            over_groups(act, lambda g: group(g, down=False), group, lambda g: group(g, more=False))

        @block.vector
        def _(dve):
            link = chain(dve, sem["dve_link5"])
            link(nc.vector.memset(gs[:, Q2:Q2 + 2], 0.0))

            def col(name, i):
                return par[:, bass.ds(COLS[name] + i, 1)]

            def group(g, down=True):
                for e in range(2):
                    t = 2 * g + e
                    dve.wait_ge(sem["gate_read"], t + 1)
                    if down or e:
                        dve.wait_ge(sem["prod"], t)
                    nc.vector.tensor_scalar(cv, gs[:, 1:1 + SEQ], col("ffn_w", 3 * t), col("ffn_b", t),
                                            ALU.mult, ALU.add).then_inc(sem["conv_a"], 1)
                    dve.wait_ge(sem["conv_a"], 2 * t + 1)
                    nc.vector.scalar_tensor_tensor(out=cv, in0=gs[:, 2:2 + SEQ], scalar=col("ffn_w", 3 * t + 1), in1=cv,
                                                   op0=ALU.mult, op1=ALU.add).then_inc(sem["conv_a"], 1)
                    dve.wait_ge(sem["conv_a"], 2 * t + 2)
                    nc.vector.scalar_tensor_tensor(out=cv, in0=gs[:, 3:3 + SEQ], scalar=col("ffn_w", 3 * t + 2), in1=cv,
                                                   op0=ALU.mult, op1=ALU.add).then_inc(sem["conv2"], 1)
                    dve.wait_ge(sem["silu"], t + 1)
                    dve.wait_ge(sem["up_mm"], t + 1)
                    if down or e:
                        dve.wait_ge(sem["a_lo"], t)
                    nc.vector.tensor_tensor(pr, u_ps, cv, ALU.mult).then_inc(sem["prod"], 1)
                    if e == 0 and down:
                        add_down(g - 1)
                    dve.wait_ge(sem["a_hi"], t + 1)
                    nc.vector.tensor_tensor(a_l[e], pr, f32(a_h[e]), ALU.subtract).then_inc(sem["a_lo"], 1)

            def add_down(g):
                for u in range(NU):
                    i, c = divmod(u, 2)
                    r = h[:, i, 512 * c:512 * c + 512]
                    if u == 0:
                        dve.wait_ge(sem["dn_read"], NU * g)
                    dve.wait_ge(sem["dn_mm"], NU * g + u + 1)
                    nc.vector.tensor_tensor(r, bank(5 + u % 3), r, ALU.add).then_inc(sem["dn_read"], 1)

            over_groups(dve, lambda g: group(g, down=False), group, group)
            add_down(GROUPS - 1)

        @block.tensor
        def _(pe):
            def up(g, e, first):
                t = 2 * g + e
                pe.wait_ge(sem["up_lo"], t + 1)
                if not first:
                    pe.wait_ge(sem["gate_read"], t)
                for k in range(KD):
                    for c in range(3):
                        cs = slice(third * c, third * c + third)
                        ins = split_products(nc, g_ps[:, c], up_h[e][:, k, :], up_l[e][:, k, :], hn_h[:, k, cs],
                                             hn_l[:, k, cs], k == 0, k == KD - 1)
                ins.then_inc(sem["gate_mm"], 1)
                if not first:
                    pe.wait_ge(sem["prod"], t)
                for k in range(KD):
                    for c in range(2):
                        cs = slice(2 + 512 * c, 2 + 512 * c + 512)
                        ins = split_products(nc, u_ps[:, 512 * c:512 * c + 512], up_h[e][:, KD + k, :],
                                             up_l[e][:, KD + k, :], hn_h[:, k, cs], hn_l[:, k, cs], k == 0, k == KD - 1)
                ins.then_inc(sem["up_mm"], 1)

            def down(g):
                pe.wait_ge(sem["a_lo"], 2 * g + 2)
                pe.wait_ge(sem["dn_lo"], 2 * g + 2)
                pe.wait_ge(sem["dn_read"], NU * g)
                for u in range(NU):
                    i, c = divmod(u, 2)
                    ts, cs = slice(P * i, P * i + P), slice(512 * c, 512 * c + 512)
                    if u >= 3:
                        pe.wait_ge(sem["dn_read"], NU * g + u - 2)
                    for e in range(2):
                        ins = split_products(nc, bank(5 + u % 3), a_h[e][:, ts], a_l[e][:, ts], dn_h[e][:, cs],
                                             dn_l[e][:, cs], e == 0, e == 1)
                    ins.then_inc(sem["dn_mm"], 1)

            def group(g):
                up(g, 0, False)
                down(g - 1)
                up(g, 1, False)

            def first(g):
                up(g, 0, True)
                up(g, 1, False)

            over_groups(pe, first, group, group)
            down(GROUPS - 1)


SEMS = """par_in gw_in con_in x_hi x_sq x_lo x_acc ones pads w_split gw_split xc_hi xc_lo a_ready a_sq scanned gelu y_lru
lam_e lam_done var std conv gate_in unit_done unit_read_act unit_read_dve var_lru sqrt_lru pool_link act_link dve_link
uq_in ukv_in csq uq_hi ukv_hi uq_lo v_hi v_lo gained roped c_hi c_lo kv_var kv_std kv_rstd q_mm kv_mm st_mm squares
summed kvs k_scaled q_scaled head_var head_std dve_link2
sel_in b_set e_summed e_full e_hi e_lo es_lo es_hi side_done side_hi side_read_act side_read_dve s_done pv_done o_low
o_sum y_mla xo_mm xo_low x_lo2 x_y x_exp q_low_meta dve_link3 o_hi x_max x_row_in x_in row_in x_prob
wo_lo wo_hi res_in y_hi y_lo ysq ysum y_var y_std yss_mm wo_mm h_done h_sq h_var h_std hn hn_t hn_hi hn_lo dve_link4
up_in up_hi up_lo dn_hi dn_lo gate_mm up_mm gate_read conv_a conv2 silu prod a_hi a_lo dn_mm dn_read stored
dve_link5""".split()


def build(nc, dram, out):
    with ExitStack() as ctx:
        place = Place(nc)
        con = constants(place)
        sem = {n: ctx.enter_context(nc.semaphore(n)) for n in SEMS}
        sem["xt_in"] = [ctx.enter_context(nc.semaphore(f"xt_in{b}")) for b in range(4)]
        sem["wo_in"] = [ctx.enter_context(nc.semaphore(f"wo_in{b}")) for b in range(4)]
        sem["dn_in"] = [ctx.enter_context(nc.semaphore(f"dn_in{b}")) for b in range(2)]
        sem["w_in"] = [ctx.enter_context(nc.semaphore(f"w_in{b}")) for b in range(2)]
        all_banks = ctx.enter_context(nc.psum_tensor("banks", [P, 8 * 512], F32))

        def bank(b, n=1):
            return all_banks[:, 512 * b:512 * (b + n)]

        yl = place("y_lru", M_YL, (LF, T))
        cq = place("cq", M_CQ, (3, T))
        kpe = place("kpe_fm", M_KPE, (T,), parts=ROPE)
        xpad = place("xpad", M_KPE, (T + 3,))
        mix_phase(nc, place, con, yl, cq, (kpe, xpad), [bank(b) for b in range(8)], dram, sem)
        qk = place("qk", M_QK, (NT, 2 * HEADS * QK))
        v = place("v", M_V, (NT, HEADS * 2 * VD), F32R)
        qkv_phase(nc, place, con, cq, kpe, qk, v, bank, dram, sem)
        ym = place("y_mla", M_YM, (KD // 2, SEQ + 2))
        attention_phase(nc, place, con, qk, v, ym, bank, dram, sem)
        h = place("h", M_H, (XT, D))
        hn_h = place("hn_h", M_HN, (KD, Q2), F32R)
        hn_l = place("hn_l", M_HNL, (KD, Q2), F32R)
        out_phase(nc, place, con, yl, ym, h, hn_h, hn_l, bank, dram, sem)
        ffn_phase(nc, place, con, h, hn_h, hn_l, bank, dram, out, sem)


def _pack(inputs):
    a = {k: np.ascontiguousarray(np.asarray(v)) for k, v in inputs.items()}
    h0 = np.concatenate([a["meta_tokens"], a["x"][0]], axis=0)

    def cols(v):
        v = v.reshape(-1, v.shape[-1] // P, P)
        return v.transpose(1, 0, 2).reshape(-1, P).T

    par = np.zeros((P, NCOL), np.float32)
    gate_b = np.stack([a["lru_b_a"][0], a["lru_b_x"][0]], 1).reshape(4, LRU)
    for name, v in [("mix_g", a["norm_mix_g"][0]), ("conv_w", a["conv_lru_w"][0]), ("conv_b", a["conv_lru_b"][0]),
                    ("gate_b", gate_b), ("lam", a["lru_lambda"][0]), ("q_g", a["q_latent_g"][0]),
                    ("kv_g", a["kv_latent_g"][0]),
                    ("out_g", np.concatenate([a["lru_gate_g"][0], a["mla_out_g"][0]])),
                    ("ffn_w", a["conv_ffn_w"][0]), ("ffn_b", a["conv_ffn_b"][0])]:
        c = cols(v)
        par[:, COLS[name]:COLS[name] + c.shape[1]] = c
    gw = np.zeros((P, LF, 2, 2, P), np.float32)
    for d in range(2):
        for w, name in enumerate(["lru_w_a", "lru_w_x"]):
            for h in range(8):
                o = 64 * (h % 2)
                gw[o:o + 64, h // 2, d, w, o:o + 64] = a[name][0, d, h]
    inv = (10000.0 ** (-np.arange(0, ROPE, 2, dtype=np.float32) / ROPE)).astype(np.float32)
    ang = np.arange(T, dtype=np.float32)[:, None] * inv[None, :]
    cos, sin = np.cos(ang), np.sin(ang)
    rc, rs = np.zeros((P, NT, ROPE), np.float32), np.zeros((P, NT, ROPE), np.float32)
    for i in range(NT):
        n, t0 = token_rows(i)
        rc[:n, i] = np.concatenate([cos[t0:t0 + n], cos[t0:t0 + n]], 1)
        rs[:n, i] = np.concatenate([-sin[t0:t0 + n], sin[t0:t0 + n]], 1)
    gqk = np.broadcast_to(np.stack([a["q_norm_g"][0], a["k_norm_g"][0]])[None], (P, 2, QK))
    up = a["w_ffn_up"][0].reshape(KD, P, 2, NFF, P).transpose(3, 1, 2, 0, 4)
    return {
        "x_tm": a["x"][0], "meta_tm": a["meta_tokens"],
        "x_fm": np.ascontiguousarray(h0.T.reshape(KD, P, T)),
        "par": par, "gate_w": gw.reshape(P, 4 * LF, P), "w_in": a["w_in"][0],
        "ident": np.eye(P, dtype=np.float32), "gqk": np.ascontiguousarray(gqk), "rope_c": rc, "rope_s": rs,
        "w_uq": a["w_uq"][0], "w_ukv": a["w_ukv"][0], "w_out": a["w_out"][0],
        "ffn_g": np.ascontiguousarray(np.broadcast_to(a["norm_ffn_g"][0][None], (P, D))),
        "w_up": np.ascontiguousarray(up), "w_down": a["w_ffn_down"][0],
        "sel": _selectors(),
    }


def _selectors():
    s = np.zeros((P, XT, VD), np.float32)
    for i in range(XT):
        s[i, i] = 1.0
        s[32 + i, i] = 1.0
    return s


def kernel(**inputs):
    import concourse.bacc as _bacc
    from concourse.bass_utils import run_bass_kernel_spmd as _run

    nc = _bacc.Bacc("TRN2", target_bir_lowering=False, num_devices=1)
    arrays, dram = {}, {}
    for name, a in _pack(inputs).items():
        arrays[f"in_{name}"] = a
        dram[name] = nc.dram_tensor(f"in_{name}", a.shape, mybir.dt.from_np(a.dtype), kind="ExternalInput").ap()
    out = nc.dram_tensor("out_0", (SEQ, D), F32, kind="ExternalOutput").ap()
    build(nc, dram, out)
    r = _run(nc, [arrays], core_ids=[0])
    return r.results[0]["out_0"].reshape(1, SEQ, D)
```

```python
from contextlib import ExitStack

import numpy as np

import concourse.bass as bass
from concourse import mybir

F32 = mybir.dt.float32
F32R = mybir.dt.float32r
ACT = mybir.ActivationFunctionType
ALU = mybir.AluOpType
AX = mybir.AxisListType

P = 128
D = 1024
KD = D // P
META = 16
SEQ = 1024
T = META + SEQ
XT = SEQ // P
NT = XT + 1
LRU = 512
LF = LRU // P
TAPS = 4
LRU_C = 8.0
HEADS = 8
NOPE, ROPE = 64, 32
QK = NOPE + ROPE
VD = 64
QL, KVL = 256, 128
FF = 2816
NFF = FF // P
EPS = 1e-6
CH = [(0, 348), (348, 346), (694, 346)]
WORD = 4


def token_rows(i):
    return (P, META + P * i) if i < XT else (META, 0)


COLS = {}
_at = 0
for _name, _n in [("mix_g", KD), ("conv_w", LF * TAPS), ("conv_b", LF), ("gate_b", LF * 4), ("lam", LF * 2),
                  ("q_g", QL // P), ("kv_g", KVL // P), ("qk_g", 2), ("out_g", KD), ("ffn_w", NFF * 3), ("ffn_b", NFF)]:
    COLS[_name] = _at
    _at += _n
NCOL = _at


class Place:

    BASE = 16512

    def __init__(self, nc):
        self.nc = nc

    def __call__(self, name, at, shape, dtype=F32, parts=P):
        words = int(np.prod(shape))
        t = self.nc.alloc_sbuf_tensor_at(name, [parts, words], dtype, offset=self.BASE + WORD * at)
        ap = t[:, :]
        if len(shape) == 2:
            ap = ap.rearrange("p (a b) -> p a b", a=shape[0])
        if len(shape) == 3:
            ap = ap.rearrange("p (a b c) -> p a b c", a=shape[0], b=shape[1])
        return ap


def f32(ap):
    return ap.bitcast(F32)


def chain(eng, sem):
    n = [0]

    def link(ins):
        n[0] += 1
        ins.then_inc(sem, 1)
        eng.wait_ge(sem, n[0])

    return link


def split_products(nc, out, w_h, w_l, x_h, x_l, first, last):
    nc.tensor.matmul(out, w_h, x_h, start=first, stop=False)
    nc.tensor.matmul(out, w_h, x_l, start=False, stop=False)
    return nc.tensor.matmul(out, w_l, x_h, start=False, stop=last)


M_SMALL = 0
M_YL = 1400
M_A = M_YL + LF * T
WORDS = 53208
M_KPE = WORDS - (T + 8)
M_CQ = M_KPE - 3 * T
M_UQ = M_CQ - 2 * HEADS * QK - HEADS * (NOPE + VD)
M_QK = M_A
M_V = M_QK + NT * 2 * HEADS * QK
M_2 = M_V + NT * HEADS * 2 * VD
M_CH = M_A + 2 * KD * T + 4096 + 4096 + 7 * T


def constants(place):
    c = {}
    at = M_SMALL
    for name, shape in [("ident", (P,)), ("par", (NCOL,)), ("sp4", (LF * 2,)), ("sp4n", (LF * 2,)), ("hb", (LF * 4,)),
                        ("ones", (P,)), ("gqk", (2, QK)), ("rope_c", (NT, ROPE)), ("rope_s", (NT, ROPE)),
                        ("lam_t", (6, LF * 2)), ("stat", (2, 64))]:
        c[name] = place(name, at, shape)
        if name == "gqk":
            c["late"] = at
        at += -(-int(np.prod(shape)) // 8) * 8
    assert at <= M_YL, at
    return c


def mix_phase(nc, place, con, yl, cq, kpe_fm, lat, psum, dram, sem):
    at = M_A
    xn_h = place("xn_h", at, (KD, T), F32R); at += KD * T
    xn_l = place("xn_l", at, (KD, T), F32R); at += KD * T
    w_h = [place(f"win_h{b}", at + 2048 * b, (KD, P), F32R) for b in range(2)]
    w_l = [place(f"win_l{b}", at + 2048 * b + 1024, (KD, P), F32R) for b in range(2)]; at += 4096
    gw_h = place("gw_h", at, (4 * LF, P), F32R); at += 2048
    gw_l = place("gw_l", at, (4 * LF, P), F32R); at += 2048
    xc_h = place("xc_h", at, (T,), F32R); at += T
    xc_l = place("xc_l", at, (T,), F32R); at += T
    xpad = kpe_fm[1]
    xc = [place(f"xc{b}", at + T * b, (T,)) for b in range(2)]; at += 2 * T
    gel = [place(f"gelu{b}", at + T * b, (T,)) for b in range(2)]; at += 2 * T
    rb = place("rb", at, (T,)); at += T
    assert M_2 + 2 * (2 * HEADS * QK + HEADS * (NOPE + VD)) + 3 * T <= at == M_CH
    A = [place(f"lru_a{d}", at + T * d, (T,)) for d in range(2)]
    W = [place(f"lru_w{d}", at + T * (2 + d), (T,)) for d in range(2)]
    X = [place(f"lru_x{d}", at + T * (4 + d), (T,)) for d in range(2)]
    S = [place(f"lru_s{d}", at + T * (6 + d), (T,)) for d in range(2)]
    xt = [place(f"xt{b}", at + T * b, (T,)) for b in range(4)]
    sq = [place(f"xsq{b}", at + T * (4 + b), (T,)) for b in range(2)]
    acc = place("xacc", at + T * 6, (T,)); at += 8 * T
    assert at <= M_UQ
    w_raw = [place(f"win_raw{b}", at + 1024 * b, (KD, P)) for b in range(2)]; at += 2048
    assert at <= M_CQ, (at, M_CQ)
    gw_raw = place("gw_raw", M_YL, (4 * LF, P))
    par = con["par"]

    def col(name, i):
        return par[:, COLS[name] + i:COLS[name] + i + 1]

    tiles = [("x", 0), ("x", 1), ("g", 0), ("c", 0), ("x", 2), ("g", 1), ("x", 3), ("g", 2), ("g", 3), ("c", 1),
             ("c", 2), ("k", 0)]
    first_col = {"x": 0, "g": LRU, "c": 2 * LRU, "k": 2 * LRU + QL + KVL}
    order = [("g", 0), ("c", 0), ("G", 0), ("x", 2), ("g", 1), ("G", 1), ("x", 3), ("g", 2), ("G", 2), ("g", 3), ("G", 3),
             ("c", 1), ("c", 2), ("k", 0)]
    units = [("s", 0, 0), ("s", 0, 1)] + [("x", f, c) for f in range(2) for c in range(3)] + [("s", 0, 2)]
    for kind, f in order:
        if kind == "G":
            units += [(kind, f, d, w, c) for d in range(2) for w in range(2) for c in range(3)]
        else:
            units += [(kind, f, c) for c in range(3)]
    at_unit = {u: n for n, u in enumerate(units)}
    dve_reads = [("s", 0, 0), ("s", 0, 1), ("x", 0, 0), ("x", 0, 1), ("s", 0, 2), ("x", 0, 2)]
    dve_reads += [u for u in units if u[0] != "G" and u not in dve_reads]
    act_reads = [u for u in units if u[0] == "G"]

    def bank(u):
        return psum[at_unit[u] % 8]

    def wait_unit(eng, u):
        eng.wait_ge(sem["unit_done"], at_unit[u] + 1)

    def wait_bank(eng, u):
        n = at_unit[u] - 8
        if n >= 0:
            v = units[n]
            if v[0] == "G":
                eng.wait_ge(sem["unit_read_act"], act_reads.index(v) + 1)
            else:
                eng.wait_ge(sem["unit_read_dve"], dve_reads.index(v) + 1)

    def wait_tile(eng, n):
        kind, f = tiles[n]
        eng.wait_ge(sem["unit_done"], at_unit[(kind, f, 2)] + 1)

    with nc.Block() as block:
        @block.sync
        def _(sp):
            sp.dma_start(par, dram["par"]).then_inc(sem["par_in"], 16)

            def load_x(k):
                if k >= 4:
                    sp.wait_ge(sem["x_sq"], k - 3)
                    sp.wait_ge(sem["x_lo"], k - 3)
                sp.dma_start(xt[k % 4], dram["x_fm"][k]).then_inc(sem["xt_in"][k % 4], 16)

            def load_w(n):
                if n >= 2:
                    if n == 3:
                        sp.wait_ge(sem["w1_split"], 1)
                    else:
                        sp.wait_ge(sem["w_split"], max(n - 2, 1))
                cols = ROPE if tiles[n][0] == "k" else P
                c0 = first_col[tiles[n][0]] + P * tiles[n][1]
                sp.dma_start(w_raw[n % 2][:, :, 0:cols],
                             dram["w_in"].rearrange("(k p) n -> p k n", p=P)[:, :, c0:c0 + cols])\
                  .then_inc(sem["w_in"][n % 2], 16)

            load_x(0)
            load_w(0)
            load_x(1)
            load_w(1)
            for k in range(2, KD):
                load_x(k)
            sp.dma_start(gw_raw, dram["gate_w"]).then_inc(sem["gw_in"], 16)
            for n, name in enumerate(["ident", "gqk", "rope_c", "rope_s"]):
                sp.dma_start(con[name], dram[name]).then_inc(sem["con_in"], 16)
            for n in range(2, len(tiles)):
                load_w(n)
            sp.wait_ge(sem["w_split"], len(tiles) - 1)
            sp.dma_start(lat["uq_raw"], dram["w_uq"].rearrange("(k p) n -> p k n", p=P)).then_inc(sem["uq_in"], 16)
            sp.dma_start(lat["ukv_raw"], dram["w_ukv"]).then_inc(sem["ukv_in"], 16)

        @block.gpsimd
        def _(pool):
            link = chain(pool, sem["pool_link"])
            nc.gpsimd.memset(con["ones"], 1.0).then_inc(sem["ones"], 1)
            nc.gpsimd.memset(xpad[:, 0:2], 0.0).then_inc(sem["pads"], 1)
            nc.gpsimd.memset(xpad[:, T + 2:T + 3], 0.0).then_inc(sem["pads"], 1)

            def low_w(n):
                cols = ROPE if tiles[n][0] == "k" else P
                pool.wait_ge(sem["w_hi"], n + 1)
                if n == 2:
                    pool.wait_ge(sem["w1_split"], 1)
                nc.gpsimd.tensor_tensor(w_l[n % 2][:, :, 0:cols], w_raw[n % 2][:, :, 0:cols],
                                        f32(w_h[n % 2][:, :, 0:cols]), ALU.subtract).then_inc(sem["w_split"], 1)

            def low_xc(f):
                pool.wait_ge(sem["xc_hi"], f + 1)
                nc.gpsimd.tensor_tensor(xc_l, xc[f % 2], f32(xc_h), ALU.subtract).then_inc(sem["xc_lo"], 1)

            def square_a(f):
                if f:
                    pool.wait_ge(sem["y_lru"], f)
                pool.wait_ge(sem["a_ready"], 2 * f + 2)
                nc.gpsimd.tensor_tensor(S[1], A[1], A[1], ALU.mult).then_inc(sem["a_sq"], 1)

            def join(f):
                pool.wait_ge(sem["scanned"], 2 * f + 2)
                link(nc.gpsimd.tensor_tensor(S[0], S[0], S[1], ALU.add))
                pool.wait_ge(sem["gelu"], f + 1)
                if f == 0:
                    pool.wait_ge(sem["gw_split"], 1)
                nc.gpsimd.tensor_tensor(yl[:, f, :], S[0], gel[f % 2], ALU.mult).then_inc(sem["y_lru"], 1)

            low_w(0)
            pool.wait_ge(sem["gw_hi"], 1)
            nc.gpsimd.tensor_tensor(gw_l, gw_raw, f32(gw_h), ALU.subtract).then_inc(sem["gw_split"], 1)
            low_w(2)
            low_w(3)
            low_xc(0)
            low_w(4)
            for f in range(LF):
                square_a(f)
                if f + 1 < LF:
                    low_xc(f + 1)
                for n in ([5, 6], [8], [10], [11])[f]:
                    low_w(n)
                join(f)
                for n in ([7], [9], [], [])[f]:
                    low_w(n)
            for k in range(2):
                pool.wait_ge(sem["unit_read_dve"], dve_reads.index(("c", k, 2)) + 1)
                if k == 0:
                    pool.wait_ge(sem["y_lru"], LF)
                nc.gpsimd.tensor_tensor(lat["csq"][:, k, :], cq[:, k, :], cq[:, k, :], ALU.mult).then_inc(sem["csq"], 1)

        @block.scalar
        def _(act):
            link = chain(act, sem["act_link"])
            act.wait_ge(sem["par_in"], 16)

            def high_w(n):
                cols = ROPE if tiles[n][0] == "k" else P
                act.wait_ge(sem["w_in"][n % 2], 16 * (n // 2 + 1))
                if n >= 2:
                    wait_tile(act, n - 2)
                nc.scalar.activation(w_h[n % 2][:, :, 0:cols], w_raw[n % 2][:, :, 0:cols], ACT.Copy)\
                  .then_inc(sem["w_hi"], 1)

            for k in range(KD):
                act.wait_ge(sem["xt_in"][k % 4], 16 * (k // 4 + 1))
                nc.scalar.activation(xn_h[:, k, :], xt[k % 4], ACT.Copy, scale=col("mix_g", k)).then_inc(sem["x_hi"], 1)
                if k >= 2:
                    act.wait_ge(sem["x_acc"], k - 1)
                nc.scalar.activation(sq[k % 2], xt[k % 4], ACT.Square).then_inc(sem["x_sq"], 1)
                if k == 0:
                    high_w(0)
                    high_w(1)
            lam = par[:, COLS["lam"]:COLS["lam"] + 2 * LF]
            link(nc.scalar.activation(con["lam_t"][:, 0, :], lam, ACT.Abs))
            nc.scalar.activation(con["lam_t"][:, 1, :], con["lam_t"][:, 0, :], ACT.Exp, scale=-1.0).then_inc(sem["lam_e"], 1)
            act.wait_ge(sem["gw_in"], 16)
            nc.scalar.activation(gw_h, gw_raw, ACT.Copy).then_inc(sem["gw_hi"], 1)
            for c, (c0, cn) in enumerate(CH):
                act.wait_ge(sem["unit_read_dve"], dve_reads.index(("s", 0, c)) + 1)
                nc.scalar.activation(rb[:, c0:c0 + cn], rb[:, c0:c0 + cn], ACT.Sqrt).then_inc(sem["std"], 1)
                if c >= 1:
                    high_w(c + 1)

            def high_xc(f):
                act.wait_ge(sem["conv"], f + 1)
                if f:
                    act.wait_ge(sem["unit_done"], at_unit[("G", f - 1, 1, 1, 2)] + 1)
                    act.wait_ge(sem["xc_lo"], f)
                nc.scalar.activation(xc_h, xc[f % 2], ACT.Copy).then_inc(sem["xc_hi"], 1)

            high_xc(0)
            high_w(4)
            for f in range(LF):
                act.wait_ge(sem["unit_read_dve"], dve_reads.index(("g", f, 2)) + 1)
                nc.scalar.activation(gel[f % 2], gel[f % 2], ACT.Gelu_apprx_tanh).then_inc(sem["gelu"], 1)
                if f == 0:
                    act.wait_ge(sem["lam_done"], 1)
                for d in range(2):
                    if f:
                        act.wait_ge(sem["scanned"], 2 * (f - 1) + d + 1)
                    for w, out in ((0, A[d]), (1, X[d])):
                        hb = con["hb"][:, 4 * f + 2 * d + w:4 * f + 2 * d + w + 1]
                        for c, (c0, cn) in enumerate(CH):
                            wait_unit(act, ("G", f, d, w, c))
                            nc.scalar.activation(out[:, c0:c0 + cn], bank(("G", f, d, w, c))[:, 0:cn], ACT.Tanh,
                                                 bias=hb, scale=0.5).then_inc(sem["unit_read_act"], 1)
                act.wait_ge(sem["unit_read_act"], 12 * (f + 1))
                p4, n4 = ([con[name][:, 2 * f + d:2 * f + d + 1] for d in range(2)] for name in ("sp4", "sp4n"))
                for d in range(2):
                    nc.scalar.activation(W[d], A[d], ACT.Tanh, bias=p4[d], scale=p4[d]).then_inc(sem["w_tanh"], 1)
                for d in range(2):
                    act.wait_ge(sem["w_tanh"], 2 * f + d + 1)
                    nc.scalar.activation(A[d], A[d], ACT.Exp, bias=n4[d], scale=n4[d]).then_inc(sem["a_ready"], 1)
                if f + 1 < LF:
                    high_xc(f + 1)
                for n in ([5], [], [], [11])[f]:
                    high_w(n)
                for d in range(2):
                    act.wait_ge(sem["var_lru"], 2 * f + d + 1)
                    nc.scalar.activation(W[d], W[d], ACT.Sqrt).then_inc(sem["sqrt_lru"], 1)
                for n in ([6, 7], [8, 9], [10], [])[f]:
                    high_w(n)
            act.wait_ge(sem["scanned"], 2 * LF)
            for k in range(2):
                act.wait_ge(sem["unit_read_dve"], dve_reads.index(("c", k, 2)) + 1)
                nc.scalar.activation(lat["c_h"][:, k, :], cq[:, k, :], ACT.Copy, scale=col("q_g", k)).then_inc(sem["c_hi"], 1)
            act.wait_ge(sem["unit_done"], at_unit[("G", LF - 1, 1, 1, 2)] + 1)
            act.wait_ge(sem["uq_in"], 16)
            nc.scalar.activation(lat["uq_h"], lat["uq_raw"], ACT.Copy).then_inc(sem["uq_hi"], 1)
            act.wait_ge(sem["ukv_in"], 16)
            nc.scalar.activation(lat["ukv_h"], lat["ukv_raw"], ACT.Copy).then_inc(sem["ukv_hi"], 1)

        @block.vector
        def _(dve):
            link = chain(dve, sem["dve_link"])
            dve.wait_ge(sem["par_in"], 16)
            for k in range(KD):
                dve.wait_ge(sem["x_hi"], k + 1)
                nc.vector.scalar_tensor_tensor(out=xn_l[:, k, :], in0=xt[k % 4], scalar=col("mix_g", k),
                                               in1=f32(xn_h[:, k, :]), op0=ALU.mult, op1=ALU.subtract)\
                  .then_inc(sem["x_lo"], 1)
                if k == 0:
                    dve.wait_ge(sem["w_hi"], 2)
                    nc.vector.tensor_tensor(w_l[1], w_raw[1], f32(w_h[1]), ALU.subtract).then_inc(sem["w1_split"], 1)
                dve.wait_ge(sem["x_sq"], k + 1)
                if k == 0:
                    nc.vector.tensor_copy(acc, sq[0]).then_inc(sem["x_acc"], 1)
                else:
                    dve.wait_ge(sem["x_acc"], k)
                    nc.vector.tensor_tensor(acc, acc, sq[k % 2], ALU.add).then_inc(sem["x_acc"], 1)

            def softplus():
                link(nc.vector.tensor_scalar(con["hb"], par[:, COLS["gate_b"]:COLS["gate_b"] + 4 * LF], 0.5, None, ALU.mult))
                lt = con["lam_t"]
                z, e, w, w2, s, m = (lt[:, i, :] for i in (0, 1, 2, 3, 4, 5))
                dve.wait_ge(sem["lam_e"], 1)
                lam = par[:, COLS["lam"]:COLS["lam"] + 2 * LF]
                link(nc.vector.tensor_scalar(m, lam, -1.0, 0.0, ALU.mult, ALU.max))
                link(nc.vector.tensor_scalar(w2, e, 2.0, None, ALU.add))
                link(nc.vector.reciprocal(w, w2))
                link(nc.vector.tensor_tensor(w, w, e, ALU.mult))
                link(nc.vector.tensor_tensor(w2, w, w, ALU.mult))
                n_terms = 10
                link(nc.vector.tensor_scalar(s, w2, 1.0 / (2 * n_terms + 1), 1.0 / (2 * n_terms - 1), ALU.mult, ALU.add))
                for j in range(n_terms - 2, -1, -1):
                    link(nc.vector.tensor_tensor(s, s, w2, ALU.mult))
                    link(nc.vector.tensor_scalar(s, s, 1.0 / (2 * j + 1), None, ALU.add))
                link(nc.vector.tensor_tensor(s, s, w, ALU.mult))
                link(nc.vector.scalar_tensor_tensor(out=s, in0=s, scalar=2.0, in1=m, op0=ALU.mult, op1=ALU.add))
                link(nc.vector.tensor_scalar(con["sp4"], s, LRU_C / 2, None, ALU.mult))
                nc.vector.tensor_scalar(con["sp4n"], s, -LRU_C / 2, None, ALU.mult).then_inc(sem["lam_done"], 1)

            def variance(c):
                c0, cn = CH[c]
                wait_unit(dve, ("s", 0, c))
                nc.vector.tensor_scalar(rb[:, c0:c0 + cn], bank(("s", 0, c))[:, 0:cn], 1.0 / D, EPS,
                                        ALU.mult, ALU.add).then_inc(sem["unit_read_dve"], 1)

            def scale_rows(c):
                c0, cn = CH[c]
                dve.wait_ge(sem["std"], c + 1)
                link(nc.vector.reciprocal(rb[:, c0:c0 + cn], rb[:, c0:c0 + cn]))

            def read(u, out, m=P):
                c0, cn = CH[u[-1]]
                wait_unit(dve, u)
                nc.vector.tensor_tensor(out[:, c0:c0 + cn], bank(u)[0:m, 0:cn], rb[0:m, c0:c0 + cn], ALU.mult)\
                  .then_inc(sem["unit_read_dve"], 1)

            def done_reading(u):
                dve.wait_ge(sem["unit_read_dve"], dve_reads.index(u) + 1)

            def conv(f):
                done_reading(("x", f, 2))
                if f >= 2:
                    dve.wait_ge(sem["xc_lo"], f - 1)
                taps = [col("conv_w", TAPS * f + k) for k in range(TAPS)]
                link(nc.vector.tensor_scalar(xc[f % 2], xpad[:, 0:T], taps[0], col("conv_b", f), ALU.mult, ALU.add))
                for k in range(1, TAPS):
                    ins = nc.vector.scalar_tensor_tensor(out=xc[f % 2], in0=xpad[:, k:k + T], scalar=taps[k],
                                                         in1=xc[f % 2], op0=ALU.mult, op1=ALU.add)
                    if k < TAPS - 1:
                        link(ins)
                ins.then_inc(sem["conv"], 1)
                dve.wait_ge(sem["conv"], f + 1)

            def read_gate(f):
                if f >= 2:
                    dve.wait_ge(sem["y_lru"], f - 1)
                for c in range(3):
                    read(("g", f, c), gel[f % 2])

            def recurrence(f):
                dve.wait_ge(sem["a_ready"], 2 * f + 1)
                if f:
                    dve.wait_ge(sem["y_lru"], f)
                link(nc.vector.tensor_tensor(S[0], A[0], A[0], ALU.mult))
                for d in range(2):
                    if d == 1:
                        dve.wait_ge(sem["a_sq"], f + 1)
                    nc.vector.scalar_tensor_tensor(out=W[d], in0=S[d], scalar=1.0, in1=W[d], op0=ALU.add, op1=ALU.mult)\
                      .then_inc(sem["var_lru"], 1)
                    link(nc.vector.scalar_tensor_tensor(out=X[d], in0=X[d], scalar=1.0, in1=xc[f % 2],
                                                        op0=ALU.add, op1=ALU.mult))
                for c in range(3):
                    if f < 2:
                        read(("x", f + 2, c), xpad[:, 2:])
                    if f == LF - 1:
                        read(("c", 1, c), cq[:, 1, :])
                for d in range(2):
                    dve.wait_ge(sem["sqrt_lru"], 2 * f + d + 1)
                    link(nc.vector.scalar_tensor_tensor(out=X[d], in0=W[d], scalar=0.5, in1=X[d],
                                                        op0=ALU.mult, op1=ALU.mult))
                    if d == 0:
                        nc.vector.tensor_tensor_scan(S[0], A[0], X[0], 0.0, ALU.mult, ALU.add).then_inc(sem["scanned"], 1)
                    else:
                        nc.vector.tensor_tensor_scan(S[1][:, ::-1], A[1][:, ::-1], X[1][:, ::-1], 0.0,
                                                     ALU.mult, ALU.add).then_inc(sem["scanned"], 1)

            variance(0)
            variance(1)
            scale_rows(0)
            dve.wait_ge(sem["pads"], 2)
            read(("x", 0, 0), xpad[:, 2:])
            scale_rows(1)
            read(("x", 0, 1), xpad[:, 2:])
            variance(2)
            scale_rows(2)
            read(("x", 0, 2), xpad[:, 2:])
            conv(0)
            for c in range(3):
                read(("x", 1, c), xpad[:, 2:])
            conv(1)
            softplus()
            for f in range(LF):
                read_gate(f)
                if f == 0:
                    for c in range(3):
                        read(("c", 0, c), cq[:, 0, :])
                recurrence(f)
                if f < 2:
                    conv(f + 2)
            dve.wait_ge(sem["y_lru"], LF)
            for k in range(2):
                dve.wait_ge(sem["c_hi"], k + 1)
                nc.vector.scalar_tensor_tensor(out=lat["c_l"][:, k, :], in0=cq[:, k, :], scalar=col("q_g", k),
                                               in1=f32(lat["c_h"][:, k, :]), op0=ALU.mult, op1=ALU.subtract)\
                  .then_inc(sem["c_lo"], 1)
            dve.wait_ge(sem["uq_hi"], 1)
            nc.vector.tensor_tensor(lat["uq_l"], lat["uq_raw"], f32(lat["uq_h"]), ALU.subtract).then_inc(sem["uq_lo"], 1)
            for c in range(3):
                read(("c", 2, c), cq[:, 2, :])
            for c in range(3):
                read(("k", 0, c), kpe_fm[0], ROPE)

        @block.tensor
        def _(pe):
            def project(kinds, n0):
                pe.wait_ge(sem["w_split"], max(n0, 1))
                if n0 == 0:
                    pe.wait_ge(sem["w1_split"], 1)
                us = [(kind, f, c) for kind, f in kinds for c in range(3)]
                for u in us:
                    wait_bank(pe, u)
                for k in range(KD):
                    if n0 == 0:
                        pe.wait_ge(sem["x_lo"], k + 1)
                        if k == KD - 1:
                            squares(0)
                            squares(1)
                    for u in us:
                        n = tiles.index(u[:2])
                        m = ROPE if u[0] == "k" else P
                        c0, cn = CH[u[2]]
                        ins = split_products(nc, bank(u)[0:m, 0:cn], w_h[n % 2][:, k, 0:m], w_l[n % 2][:, k, 0:m],
                                             xn_h[:, k, c0:c0 + cn], xn_l[:, k, c0:c0 + cn], k == 0, k == KD - 1)
                        if k == KD - 1:
                            ins.then_inc(sem["unit_done"], 1)

            def squares(c):
                pe.wait_ge(sem["ones"], 1)
                pe.wait_ge(sem["x_acc"], KD)
                wait_bank(pe, ("s", 0, c))
                c0, cn = CH[c]
                nc.tensor.matmul(bank(("s", 0, c))[:, 0:cn], con["ones"], acc[:, c0:c0 + cn],
                                 start=True, stop=True).then_inc(sem["unit_done"], 1)

            project([("x", 0), ("x", 1)], 0)
            squares(2)
            for kind, f in order:
                if kind == "G":
                    pe.wait_ge(sem["gw_split"], 1)
                    pe.wait_ge(sem["xc_lo"], f + 1)
                    for u in units:
                        if u[:2] != ("G", f):
                            continue
                        _, _, d, w, c = u
                        c0, cn = CH[c]
                        m = 4 * f + 2 * d + w
                        wait_bank(pe, u)
                        split_products(nc, bank(u)[:, 0:cn], gw_h[:, m, :], gw_l[:, m, :], xc_h[:, c0:c0 + cn],
                                       xc_l[:, c0:c0 + cn], True, True).then_inc(sem["unit_done"], 1)
                else:
                    project([(kind, f)], tiles.index((kind, f)))


def latent_map(place):
    NQ, NKV = HEADS * QK, HEADS * (NOPE + VD)
    at = M_2
    lat = {}
    lat["uq_h"] = place("uq_h", at, (2, NQ), F32R); at += 2 * NQ
    lat["uq_l"] = place("uq_l", at, (2, NQ), F32R); at += 2 * NQ
    lat["ukv_h"] = place("ukv_h", at, (NKV,), F32R); at += NKV
    lat["ukv_l"] = place("ukv_l", at, (NKV,), F32R); at += NKV
    lat["csq"] = place("csq", at, (3, T))
    lat["csq_at"] = at
    at = M_CH
    lat["c_h"] = place("c_h", at, (3, T), F32R); at += 3 * T
    lat["c_l"] = place("c_l", at, (3, T), F32R); at += 3 * T
    lat["end"] = at
    lat["uq_raw"] = place("uq_raw", M_UQ, (2, NQ))
    lat["ukv_raw"] = place("ukv_raw", M_UQ + 2 * NQ, (NKV,))
    return lat


def qkv_phase(nc, place, con, cq, kpe_fm, lat, qk, v, bank, sem):
    NQ, NKV = HEADS * QK, HEADS * (NOPE + VD)
    c_h, c_l, csq = lat["c_h"], lat["c_l"], lat["csq"]
    uq_h, uq_l, ukv_h, ukv_l, ukv_raw = (lat[name] for name in ("uq_h", "uq_l", "ukv_h", "ukv_l", "ukv_raw"))
    at = lat["csq_at"]
    kvs = [place(f"kvs{b}", at + NKV * b, (HEADS, NOPE + VD)) for b in range(2)]
    ra = place("rope_a", at + 2 * NKV, (2 * HEADS, ROPE))
    rp = place("rope_b", at + 2 * NKV + 512, (2 * HEADS, ROPE))
    at = lat["end"]
    sqs = place("squares", at, (1280,)); at += 1280
    psq = place("kpe_sq", at, (NT, ROPE)); at += NT * ROPE
    cg = place("rope_cg", at, (NT, 2, ROPE)); at += NT * 2 * ROPE
    sg = place("rope_sg", at, (NT, 2, ROPE)); at += NT * 2 * ROPE
    q_sb = [place(f"q_sb{b}", at + NQ * b, (NQ,)) for b in range(2)]; at += 2 * NQ
    assert at <= M_CQ, (at, M_CQ)
    qsq = sqs[:, 0:NQ].rearrange("p (h d) -> p h d", h=HEADS)
    ksq = sqs[:, NQ:NQ + HEADS * NOPE].rearrange("p (h d) -> p h d", h=HEADS)
    par, ident, ones, stat = con["par"], con["ident"], con["ones"], con["stat"]
    lt = con["lam_t"].rearrange("p a b -> p (a b)")
    v_q, r_kv, v_pe = lt[:, 0:NT], lt[:, 16:16 + NT], lt[:, 32:32 + NT]
    half = ROPE // 2
    ST = 48
    st_ps = [bank(4 + b, 1)[:, 0:NT * ST].rearrange("p (i n) -> p i n", n=ST) for b in range(2)]

    def st_of(i):
        return st_ps[0 if i < 2 else 1]

    def q_ps(i, b):
        return bank(b)[:, 0:NQ // 2]

    def kv_ps(i):
        return bank(2 if i % 2 == 0 else 6, 2)

    def tok(i):
        n, t0 = token_rows(i)
        return slice(t0, t0 + n)

    PARTS = [[(P, slice(0, 2))], [(P, slice(2, XT)), (META, slice(XT, NT))]]

    with nc.Block() as block:
        @block.gpsimd
        def _(pool):
            g = con["gqk"][:, :, NOPE:QK].unsqueeze(1).broadcast_to((P, NT, 2, ROPE))
            cs = con["rope_c"].unsqueeze(2).broadcast_to((P, NT, 2, ROPE))
            sn = con["rope_s"].unsqueeze(2).broadcast_to((P, NT, 2, ROPE))
            pool.wait_ge(sem["con_in"], 64)
            nc.gpsimd.tensor_tensor(cg, cs, g, ALU.mult).then_inc(sem["tables"], 1)
            nc.gpsimd.tensor_tensor(sg[:, :, :, 0:half], sn[:, :, :, 0:half], g[:, :, :, half:], ALU.mult)\
              .then_inc(sem["tables"], 1)
            nc.gpsimd.tensor_tensor(sg[:, :, :, half:], sn[:, :, :, half:], g[:, :, :, 0:half], ALU.mult)\
              .then_inc(sem["tables"], 1)
            pool.wait_ge(sem["tables"], 3)
            pool.wait_ge(sem["st_mm"], 2)
            for i in range(NT):
                n, _ = token_rows(i)
                pool.wait_ge(sem["v_hi"], i + 1)
                vt = v[0:n, i, :].rearrange("p (h d) -> p h d", h=HEADS)
                nc.gpsimd.tensor_tensor(vt[:, :, VD:], kvs[i % 2][0:n, :, NOPE:], f32(vt[:, :, 0:VD]), ALU.subtract)\
                  .then_inc(sem["v_lo"], 1)
                pool.wait_ge(sem["q_scaled"], i + 1)
                pool.wait_ge(sem["k_scaled"], i + 1)
                if i:
                    pool.wait_ge(sem["rope_done"], i)
                x = qk[0:n, i, :].rearrange("p (g h d) -> p g h d", g=2, d=QK)[:, :, :, NOPE:QK]
                ra4 = ra[0:n].rearrange("p (g h) d -> p g h d", g=2)
                rp4 = rp[0:n].rearrange("p (g h) d -> p g h d", g=2)
                ci = cg[0:n, i].unsqueeze(2).broadcast_to((n, 2, HEADS, ROPE))
                si = sg[0:n, i].unsqueeze(2).broadcast_to((n, 2, HEADS, ROPE))
                nc.gpsimd.tensor_tensor(ra4, x, ci, ALU.mult).then_inc(sem["roped"], 1)
                nc.gpsimd.tensor_tensor(rp4[:, :, :, 0:half], x[:, :, :, half:], si[:, :, :, 0:half], ALU.mult)\
                  .then_inc(sem["roped"], 1)
                nc.gpsimd.tensor_tensor(rp4[:, :, :, half:], x[:, :, :, 0:half], si[:, :, :, half:], ALU.mult)\
                  .then_inc(sem["roped"], 1)

        @block.scalar
        def _(act):
            nc.scalar.activation(csq[:, 2, :], cq[:, 2, :], ACT.Square).then_inc(sem["csq_act"], 1)
            g = par[:, COLS["kv_g"]:COLS["kv_g"] + 1]
            nc.scalar.activation(c_h[:, 2, :], cq[:, 2, :], ACT.Copy, scale=g).then_inc(sem["c_hi"], 1)

            def latent_std(p):
                st = st_ps[p]
                done = sum(len(PARTS[j]) for j in range(p + 1))
                act.wait_ge(sem["kv_var"], done)
                for n, ts in PARTS[p]:
                    nc.scalar.activation(r_kv[0:n, ts], r_kv[0:n, ts], ACT.Sqrt).then_inc(sem["kv_std"], 1)
                for n, ts in PARTS[p]:
                    nc.scalar.activation(psq[0:n, ts], st[0:n, ts, 16:16 + ROPE], ACT.Square).then_inc(sem["pe_sq"], 1)

            def head_std(i):
                n, _ = token_rows(i)
                st = stat[0:n, i % 2]
                act.wait_ge(sem["head_var"], 2 * i + 2)
                nc.scalar.activation(st[:, 16:32], st[:, 16:32], ACT.Sqrt).then_inc(sem["head_std"], 1)

            for i in range(NT):
                n, _ = token_rows(i)
                if i >= 2:
                    act.wait_ge(sem["q_scaled"], i - 1)
                if i == 0:
                    act.wait_ge(sem["ukv_lo"], 1)
                for b in range(2):
                    act.wait_ge(sem["q_mm"], 2 * i + b + 1)
                    nc.scalar.activation(q_sb[i % 2][0:n, b * NQ // 2:(b + 1) * NQ // 2], q_ps(i, b)[0:n], ACT.Copy)\
                      .then_inc(sem["q_read"], 1)
                if i == 0:
                    latent_std(0)
                if i:
                    act.wait_ge(sem["summed"], 2 * i)
                    head_std(i - 1)
                act.wait_ge(sem["q_read"], 2 * i + 2)
                nc.scalar.activation(qsq[0:n].rearrange("p h d -> p (h d)"), q_sb[i % 2][0:n], ACT.Square)\
                  .then_inc(sem["squares"], 1)
                act.wait_ge(sem["kv_mm"], i + 1)
                if i == 0:
                    act.wait_ge(sem["kv_rstd"], 1)
                    act.wait_ge(sem["st_mm"], 2)
                if i == 1:
                    latent_std(1)
                if i == 2:
                    act.wait_ge(sem["kv_rstd"], 3)
                if i >= 2:
                    act.wait_ge(sem["v_lo"], i - 1)
                    act.wait_ge(sem["k_scaled"], i - 1)
                nc.scalar.activation(kvs[i % 2][0:n].rearrange("p h d -> p (h d)"), kv_ps(i)[0:n], ACT.Copy,
                                     scale=r_kv[0:n, i:i + 1]).then_inc(sem["kvs"], 1)
                act.wait_ge(sem["kvs"], i + 1)
                nc.scalar.activation(ksq[0:n], kvs[i % 2][0:n, :, 0:NOPE], ACT.Square).then_inc(sem["squares"], 1)
                vt = v[0:n, i, :].rearrange("p (h d) -> p h d", h=HEADS)
                nc.scalar.activation(vt[:, :, 0:VD], kvs[i % 2][0:n, :, NOPE:], ACT.Copy).then_inc(sem["v_hi"], 1)
            head_std(NT - 1)

        @block.vector
        def _(dve):
            link = chain(dve, sem["dve_link2"])
            g = par[:, COLS["kv_g"]:COLS["kv_g"] + 1]
            dve.wait_ge(sem["ukv_hi"], 1)
            nc.vector.tensor_tensor(ukv_l, ukv_raw, f32(ukv_h), ALU.subtract).then_inc(sem["ukv_lo"], 1)
            dve.wait_ge(sem["c_hi"], 3)
            nc.vector.scalar_tensor_tensor(out=c_l[:, 2, :], in0=cq[:, 2, :], scalar=g, in1=f32(c_h[:, 2, :]),
                                           op0=ALU.mult, op1=ALU.subtract).then_inc(sem["c_lo"], 1)

            def latent_stats(p):
                st = st_ps[p]
                dve.wait_ge(sem["st_mm"], p + 1)
                for n, ts in PARTS[p]:
                    link(nc.vector.tensor_scalar(v_q[0:n, ts], st[0:n, ts, 0], EPS / QL, EPS * EPS, ALU.mult, ALU.add))
                for n, ts in PARTS[p]:
                    nc.vector.tensor_scalar(r_kv[0:n, ts], st[0:n, ts, 2], 1.0 / KVL, EPS, ALU.mult, ALU.add)\
                      .then_inc(sem["kv_var"], 1)

            def latent_rstd(p):
                done = sum(len(PARTS[j]) for j in range(p + 1))
                dve.wait_ge(sem["kv_std"], done)
                for n, ts in PARTS[p]:
                    nc.vector.reciprocal(r_kv[0:n, ts], r_kv[0:n, ts]).then_inc(sem["kv_rstd"], 1)
                dve.wait_ge(sem["pe_sq"], done)
                for n, ts in PARTS[p]:
                    link(nc.vector.tensor_reduce(v_pe[0:n, ts], psq[0:n, ts], AX.X, ALU.add))
                    link(nc.vector.tensor_scalar(v_pe[0:n, ts], v_pe[0:n, ts], QK * EPS, None, ALU.add))

            latent_stats(0)
            latent_rstd(0)

            def scale_q(i):
                n, _ = token_rows(i)
                st = stat[0:n, i % 2]
                dve.wait_ge(sem["head_std"], i + 1)
                link(nc.vector.reciprocal(st[:, 32:48], st[:, 16:32]))
                x = qk[0:n, i, 0:NQ].rearrange("p (h d) -> p h d", d=QK)
                nc.vector.tensor_tensor(x, q_sb[i % 2][0:n].rearrange("p (h d) -> p h d", d=QK),
                                        st[:, 32:40].unsqueeze(2).broadcast_to((n, HEADS, QK)), ALU.mult)\
                  .then_inc(sem["q_scaled"], 1)

            def scale_k(i):
                n, _ = token_rows(i)
                x = qk[0:n, i, NQ:].rearrange("p (h d) -> p h d", d=QK)
                rk = stat[0:n, i % 2, 40:48].unsqueeze(2)
                nc.vector.tensor_tensor(x[:, :, 0:NOPE], kvs[i % 2][0:n, :, 0:NOPE], rk.broadcast_to((n, HEADS, NOPE)),
                                        ALU.mult)
                kp = st_of(i)[0:n, i, 16:16 + ROPE].unsqueeze(1).broadcast_to((n, HEADS, ROPE))
                nc.vector.tensor_tensor(x[:, :, NOPE:QK], kp, rk.broadcast_to((n, HEADS, ROPE)), ALU.mult)\
                  .then_inc(sem["k_scaled"], 1)

            def rope_sum(i):
                n, _ = token_rows(i)
                dve.wait_ge(sem["roped"], 3 * i + 3)
                x = qk[0:n, i, :].rearrange("p (h d) -> p h d", d=QK)[:, :, NOPE:QK]
                nc.vector.tensor_tensor(x, ra[0:n], rp[0:n], ALU.add).then_inc(sem["rope_done"], 1)

            for i in range(NT + 2):
                if i < NT:
                    n, _ = token_rows(i)
                    st = stat[0:n, i % 2]
                    dve.wait_ge(sem["squares"], 2 * i + 1)
                    nc.vector.tensor_reduce(st[:, 16:24], qsq[0:n], AX.X, ALU.add).then_inc(sem["summed"], 1)
                if 1 <= i <= NT:
                    scale_q(i - 1)
                if i < NT:
                    dve.wait_ge(sem["squares"], 2 * i + 2)
                    nc.vector.tensor_reduce(st[:, 24:32], ksq[0:n], AX.X, ALU.add).then_inc(sem["summed"], 1)
                    dve.wait_ge(sem["summed"], 2 * i + 2)
                    nc.vector.tensor_scalar(st[:, 16:24], st[:, 16:24], 1.0 / QK, v_q[0:n, i:i + 1], ALU.mult, ALU.add)\
                      .then_inc(sem["head_var"], 1)
                    nc.vector.tensor_scalar(st[:, 24:32], st[:, 24:32], v_pe[0:n, i:i + 1], 1.0 / QK, ALU.add, ALU.mult)\
                      .then_inc(sem["head_var"], 1)
                if i == 0:
                    latent_stats(1)
                if i == 1:
                    latent_rstd(1)
                if 1 <= i <= NT:
                    scale_k(i - 1)
                if i >= 2:
                    rope_sum(i - 2)

        @block.tensor
        def _(pe):
            def statistics(tiles):
                for i in tiles:
                    n, _ = token_rows(i)
                    st = st_of(i)[0:n, i]
                    for k in range(2):
                        nc.tensor.matmul(st[:, 0:2], csq[:, k, tok(i)], ones[:, 0:2], start=k == 0, stop=k == 1)
                    nc.tensor.matmul(st[:, 2:4], csq[:, 2, tok(i)], ones[:, 0:2], start=True, stop=True)
                    ins = nc.tensor.transpose(st[:, 16:16 + ROPE], kpe_fm[:, tok(i)], ident[0:ROPE, 0:ROPE])
                ins.then_inc(sem["st_mm"], 1)

            pe.wait_ge(sem["c_lo"], 2)
            pe.wait_ge(sem["uq_lo"], 1)
            for i in range(NT):
                n, _ = token_rows(i)
                for b in range(2):
                    if i:
                        pe.wait_ge(sem["q_read"], 2 * (i - 1) + b + 1)
                    cols = slice(b * NQ // 2, (b + 1) * NQ // 2)
                    for k in range(2):
                        ins = split_products(nc, q_ps(i, b)[0:n], c_h[:, k, tok(i)], c_l[:, k, tok(i)],
                                             uq_h[:, k, cols], uq_l[:, k, cols], k == 0, k == 1)
                    ins.then_inc(sem["q_mm"], 1)
                if i == 0:
                    pe.wait_ge(sem["csq_act"], 1)
                    pe.wait_ge(sem["csq"], 2)
                    statistics([0, 1])
                    pe.wait_ge(sem["c_lo"], 3)
                    pe.wait_ge(sem["ukv_lo"], 1)
                    statistics(range(2, NT))
                if i >= 2:
                    pe.wait_ge(sem["kvs"], i - 1)
                for b in range(2):
                    cols = slice(b * NKV // 2, (b + 1) * NKV // 2)
                    ins = split_products(nc, kv_ps(i)[0:n, cols], c_h[:, 2, tok(i)], c_l[:, 2, tok(i)],
                                         ukv_h[:, cols], ukv_l[:, cols], True, True)
                ins.then_inc(sem["kv_mm"], 1)


M_YM = WORDS - (KD // 2) * (SEQ + 2) - 8
M_YM -= M_YM % 8
SLOTS = NT


def attention_phase(nc, place, con, qk, v, ym, h_res, wo_raw, bank, dram, sem):
    at = M_2
    q_h = [place(f"q_h{b}", at + T * b, (T,), F32R, QK + 1) for b in range(2)]; at += 2 * T
    q_l = [place(f"q_l{b}", at + T * b, (T,), F32R, QK) for b in range(2)]; at += 2 * T
    k_h = [place(f"k_h{b}", at + T * b, (T,), F32R, QK + 1) for b in range(2)]; at += 2 * T
    k_l = [place(f"k_l{b}", at + T * b, (T,), F32R, QK) for b in range(2)]; at += 2 * T
    e_h = [place(f"e_h{b}", at + SEQ * b, (SEQ,), F32R) for b in range(3)]; at += 3 * SEQ
    e_l = [place(f"e_l{b}", at + SEQ * b, (SEQ,), F32R) for b in range(2)]; at += 2 * SEQ
    e_f = [place(f"e_f{b}", at + SEQ * b, (SEQ,)) for b in range(3)]; at += 3 * SEQ
    sel = place("sel", at, (XT, VD))
    es = [place(f"esum{b}", at + SEQ * b, (SEQ,)) for b in range(2)]; at += 2 * SEQ
    o_lo = place("o_lo", at, (SEQ,)); at += SEQ
    sel_r = place("sel_r", con["late"], (XT, VD), F32R, 40)
    rl_r = place("rl_r", at, (P,), F32R, 40); at += P
    NX = 2 * HEADS
    x_e = place("x_e", at, (NT, HEADS, 4), F32R); at += 2 * NT * NX
    x_v = place("x_v", at, (4, 2 * NX)); at += 8 * NX
    r_row = place("r_row", at, (P,), F32R, XT); at += P
    x_one = place("x_one", M_2 + 2 * T, (T,))[QK:QK + 2]
    x_all = place("x_all", M_2 + 4 * T + 2 * T, (T,))[QK:QK + NX]
    x_row = place("x_row", M_2 + 2 * T, (T,), parts=NX)
    assert at <= M_YM, (at, M_YM)
    SCALE = float(np.float32(1.0) / np.sqrt(np.float32(QK)))
    mx = con["lam_t"].rearrange("p a b -> p (a b)")
    mx3, mx_all, rl = mx[:, 0:3 * XT], mx[:, 24:24 + XT], mx[:, 32:32 + XT]
    ident, ones = con["ident"], con["ones"]

    def s_ps(g):
        return bank(2 * (g % 2), 2)

    o_ps = bank(4, 2)

    PREPARE = {0: ("tq0", "tq1", "", "tk0"), 1: ("", "tk1", "", "a0"), 2: ("a1", "", "a2", ""), 3: ("a3", "a4", "a5", "tm"),
               4: ("", "a6", "", "a7"), 5: ("a8", "a9", "a10", ""), 6: ("a11", "a12", "a13", ""),
               7: ("a14", "a15", "am", "r"), 8: ("", "", "", "")}
    CURRENT = {0: ("", "", "x0", ""), 1: ("x1", "", "x2", "")}
    FINISH = {2: ("", "l", "", "rt"), 4: ("b0", "", "b1", "")}
    META_QUERIES = {5: ("xt", "", "", ""), 7: ("", "", "", "xo")}
    NONE = ("", "", "", "")

    def side_jobs(h, s):
        places = [None] * 4
        for plan, head in [(PREPARE, h + 1), (CURRENT, h), (FINISH, h - 1), (META_QUERIES, h)]:
            if 0 <= head < HEADS and not (plan is META_QUERIES and h != HEADS - 1) and not (plan is CURRENT and h < 0):
                for i, kind in enumerate(plan.get(s, NONE)):
                    if kind:
                        assert places[i] is None
                        places[i] = (kind, head)
        return places

    steps = [(h, s) for h in range(-1, HEADS + 1) for s in range(SLOTS)]
    jobs = [j for h, s in steps for j in side_jobs(h, s) if j]
    number = {j: n for n, j in enumerate(jobs)}
    first = len([j for s in range(SLOTS) for j in side_jobs(-1, s) if j])
    BY_ACT = {"r", "x0", "x1", "x2"}
    HIGH = {"tq0": 1, "tq1": 1, "tk0": 1, "tk1": 1, "tm": 2, "rt": 1, "xt": 1, "xo": 1}

    def side_of(j):
        n = number[j]
        return bank([6, 7, 0, 1, 2, 3][n % 6] if n < first else 6 + (n - first) % 2, 1)

    def before(j):
        n = number[j]
        if n < first:
            return jobs[n - 6:n - 5] if n >= 6 else []
        return jobs[n - 2:n - 1] if n > first else jobs[n - 2:n]

    def hi_upto(j):
        return sum(HIGH.get(i[0], 0) for i in jobs[:number[j]])

    def wait_read(eng, j):
        same = [i for i in jobs[:number[j] + 1] if (i[0] in BY_ACT) == (j[0] in BY_ACT)]
        eng.wait_ge(sem["side_read_act" if j[0] in BY_ACT else "side_read_dve"], len(same))

    gain = {w: con["par"][0:QK, COLS["qk_g"] + i:COLS["qk_g"] + i + 1] for i, w in enumerate("qk")}

    def low(out, x, g, high):
        return nc.vector.scalar_tensor_tensor(out=out, in0=x, scalar=g, in1=f32(high), op0=ALU.mult, op1=ALU.subtract)

    POOL_LOW = (4,)

    def pool_lows(g):
        h, s = divmod(g + 1, SLOTS)
        return len(POOL_LOW) * h + sum(s > i for i in POOL_LOW)

    def lows(g):
        return 2 * (g + 1 - pool_lows(g))

    def half_of(h):
        return slice(VD * (h % 2), VD * (h % 2) + VD)

    def y_of(h):
        return ym[half_of(h), h // 2, 0:SEQ]

    def rows(g):
        return P if g % SLOTS < XT else META

    G = HEADS * SLOTS

    def summed(g):
        return XT * (g // SLOTS) + max(g % SLOTS, 1)

    with nc.Block() as block:
        @block.sync
        def _(sp):
            sp.dma_start(sel, dram["sel"]).then_inc(sem["sel_in"], 16)
            for h in range(HEADS):
                wait_read(sp, ("r", h))
                sp.dma_start(f32(q_h[h % 2][QK:QK + 1, 0:SEQ].rearrange("p (t n) -> p t n", n=P)), f32(r_row))\
                  .then_inc(sem["row_in"], 16)
                wait_read(sp, ("x2", h))
                sp.dma_start(x_all[2 * h:2 * h + 2], x_one).then_inc(sem["x_in"], 16)
            sp.wait_ge(sem["x_in"], 16 * HEADS)
            sp.wait_ge(sem["pv_done"], G - 3 * SLOTS)
            sp.dma_start(x_row, x_all).then_inc(sem["x_row_in"], 16)
            sp.wait_ge(sem["side_done"], number[("tm", HEADS - 1)] + 1)
            for k in range(KD):
                sp.dma_start(wo_raw[k], dram["w_out"][P * k:P * k + P, 0:D // 2]).then_inc(sem["wo_first"], 16)
            for i in range(XT):
                sp.dma_start(h_res[:, i, :], dram["x_tm"][P * i:P * i + P, :]).then_inc(sem["res_in"], 16)

        @block.gpsimd
        def _(pool):
            sets = [0]

            def settle(ins):
                sets[0] += 1
                ins.then_inc(sem["b_set"], 1)
                pool.wait_ge(sem["b_set"], sets[0])

            for b in range(2):
                settle(nc.gpsimd.memset(f32(k_h[b][QK:QK + 1, 0:T]), 1.0))
            settle(nc.gpsimd.memset(f32(rl_r), 0.0))
            pool.wait_ge(sem["sel_in"], 16)
            settle(nc.gpsimd.tensor_copy(sel_r, sel[0:40]))
            for h in range(HEADS + 1):
                for s in range(SLOTS):
                    g = SLOTS * h + s
                    n = rows(g)
                    if g < G:
                        pool.wait_ge(sem["e_full"], g + 1)
                        e = e_f[g % 3]
                        if s == 1:
                            if h >= 2:
                                pool.wait_ge(sem["side_done"], number[("l", h - 2)] + 1)
                            if h >= 1:
                                pool.wait_ge(sem["e_summed"], summed(g - 2))
                            nc.gpsimd.tensor_tensor(es[h % 2], e_f[(g - 1) % 3], e, ALU.add).then_inc(sem["e_summed"], 1)
                        elif s > 1:
                            if h >= 1 and s == 3:
                                pool.wait_ge(sem["o_sum"], h)
                            pool.wait_ge(sem["e_summed"], summed(g - 1))
                            nc.gpsimd.tensor_tensor(es[h % 2][0:n], es[h % 2][0:n], e[0:n], ALU.add)\
                              .then_inc(sem["e_summed"], 1)
                    if s in POOL_LOW and h < HEADS:
                        pool.wait_ge(sem["e_hi"], g + 1)
                        if g >= 2:
                            pool.wait_ge(sem["pv_done"], g - 1)
                        nc.gpsimd.tensor_tensor(e_l[g % 2], e_f[g % 3], f32(e_h[g % 3]), ALU.subtract)\
                          .then_inc(sem["e_lo_pool"], 1)
                    if h >= 1 and s == 2:
                        pool.wait_ge(sem["o_hi"], h)
                        pool.wait_ge(sem["o_low"], h)
                        pool.wait_ge(sem["e_summed"], summed(min(g, G - 1)))
                        y = y_of(h - 1)
                        nc.gpsimd.tensor_tensor(y, y, o_lo[half_of(h - 1)], ALU.add).then_inc(sem["o_sum"], 1)

        @block.scalar
        def _(act):
            def job(j):
                kind, h = j
                b = h % 2
                side = side_of(j)
                if kind in HIGH or kind in BY_ACT:
                    act.wait_ge(sem["side_done"], number[j] + 1)
                if kind[:2] in ("tq", "tk"):
                    c = int(kind[2])
                    out = (q_h if kind[1] == "q" else k_h)[b]
                    ins = nc.scalar.activation(out[0:QK, 512 * c:512 * c + 512], side[0:QK], ACT.Copy,
                                               scale=gain[kind[1]])
                elif kind == "tm":
                    nc.scalar.activation(q_h[b][0:QK, SEQ:T], side[0:QK, 0:META], ACT.Copy, scale=gain["q"])\
                      .then_inc(sem["side_hi"], 1)
                    ins = nc.scalar.activation(k_h[b][0:QK, SEQ:T], side[0:QK, META:2 * META], ACT.Copy, scale=gain["k"])
                elif kind == "rt":
                    act.wait_ge(sem["b_set"], 4)
                    ins = nc.scalar.activation(rl_r[0:XT], side[0:XT, 0:P], ACT.Copy)
                elif kind == "xt":
                    ins = nc.scalar.activation(x_e.rearrange("p t h c -> p (t h) c")[:, :, 0:2],
                                               side[:, 0:NT * NX].rearrange("p (n c) -> p n c", c=2), ACT.Copy)
                elif kind == "xo":
                    ins = nc.scalar.activation(x_v[0:VD, 0, :], side[VD:P, 0:2 * NX], ACT.Copy)
                elif kind == "r":
                    if h:
                        act.wait_ge(sem["row_in"], 16 * h)
                    nc.scalar.activation(r_row, side[0:XT, 0:P], ACT.Copy, scale=-1.0).then_inc(sem["side_read_act"], 1)
                    return
                elif kind[0] == "x":
                    c = int(kind[1])
                    w = 512 if c < 2 else META
                    if h and c == 0:
                        act.wait_ge(sem["x_in"], 16 * h)
                    nc.scalar.activation(x_one[:, 512 * c:512 * c + w], side[0:2, 0:w], ACT.Copy)\
                      .then_inc(sem["side_read_act"], 1)
                    return
                else:
                    return
                ins.then_inc(sem["side_hi"], 1)

            for h, s in steps:
                g = SLOTS * h + s
                if h >= 1 and s == 2:
                    act.wait_ge(sem["pv_done"], SLOTS * h)
                    if h >= 2:
                        act.wait_ge(sem["o_sum"], h - 1)
                    nc.scalar.activation(y_of(h - 1), o_ps[0:VD], ACT.Copy).then_inc(sem["o_hi"], 1)
                    nc.scalar.activation(o_lo[half_of(h - 1)], o_ps[VD:P], ACT.Copy).then_inc(sem["o_low"], 1)
                js = side_jobs(h, s)
                for j in js[0:2]:
                    if j:
                        job(j)
                if 0 <= g < G:
                    n = rows(g)
                    act.wait_ge(sem["s_done"], g + 1)
                    if g >= 3:
                        act.wait_ge(sem["e_summed"], summed(g - 3))
                        act.wait_ge(sem["e_lo"], lows(g - 3))
                        if (g - 3) % SLOTS in POOL_LOW:
                            act.wait_ge(sem["e_lo_pool"], pool_lows(g - 3))
                        act.wait_ge(sem["pv_done"], g - 2)
                    nc.scalar.activation(e_f[g % 3][0:n], s_ps(g)[0:n], ACT.Exp, scale=SCALE).then_inc(sem["e_full"], 1)
                    nc.scalar.activation(e_h[g % 3][0:n], s_ps(g)[0:n], ACT.Exp, scale=SCALE).then_inc(sem["e_hi"], 1)
                if h == HEADS - 1 and s == 4:
                    act.wait_ge(sem["x_max"], 1)
                    nc.scalar.activation(x_row, x_row, ACT.Exp, bias=x_v[0:NX, 3, 0:1], scale=SCALE)\
                      .then_inc(sem["x_exp"], 1)
                for j in js[2:4]:
                    if j:
                        job(j)

        @block.vector
        def _(dve):
            link = chain(dve, sem["dve_link3"])
            n_hi = [0]

            def job(j):
                kind, h = j
                b = h % 2
                side = side_of(j)
                if kind in HIGH:
                    n_hi[0] += HIGH[kind]
                    dve.wait_ge(sem["side_hi"], n_hi[0])
                elif kind not in BY_ACT:
                    dve.wait_ge(sem["side_done"], number[j] + 1)
                if kind[:2] in ("tq", "tk"):
                    cs = slice(512 * int(kind[2]), 512 * int(kind[2]) + 512)
                    hi, lo = (q_h[b], q_l[b]) if kind[1] == "q" else (k_h[b], k_l[b])
                    ins = low(lo[:, cs], side[0:QK], gain[kind[1]], hi[0:QK, cs])
                elif kind == "tm":
                    low(q_l[b][:, SEQ:T], side[0:QK, 0:META], gain["q"], q_h[b][0:QK, SEQ:T])
                    ins = low(k_l[b][:, SEQ:T], side[0:QK, META:2 * META], gain["k"], k_h[b][0:QK, SEQ:T])
                elif kind[0] == "a" and kind != "am":
                    i = int(kind[1:])
                    ins = nc.vector.tensor_reduce(mx3[:, i:i + 1], side, AX.X, ALU.max)
                elif kind == "am":
                    s3 = side[:, 0:XT * META].rearrange("p (i n) -> p i n", n=META)
                    link(nc.vector.tensor_reduce(mx3[:, 2 * XT:3 * XT], s3, AX.X, ALU.max))
                    wait_read(dve, ("a15", h))
                    ins = nc.vector.tensor_reduce(mx_all, mx3.rearrange("p (c t) -> p t c", c=3), AX.X, ALU.max)
                elif kind == "l":
                    ins = nc.vector.reciprocal(rl, side[:, 0:2 * XT].rearrange("p (i t) -> p i t", t=2)[:, :, 0])
                elif kind == "rt":
                    ins = nc.vector.tensor_tensor(rl_r[32:32 + XT], side[0:XT, 0:P], f32(rl_r[0:XT]), ALU.subtract)
                elif kind in ("b0", "b1"):
                    c = int(kind[1])
                    y = y_of(h)[:, 512 * c:512 * c + 512]
                    dve.wait_ge(sem["o_sum"], h + 1)
                    ins = nc.vector.tensor_tensor(y, side[0:VD], y, ALU.mult)
                elif kind == "xt":
                    xe = x_e.rearrange("p t h c -> p (t h) c")
                    ins = nc.vector.tensor_tensor(xe[:, :, 2:4], side[:, 0:NT * NX].rearrange("p (n c) -> p n c", c=2),
                                                  f32(xe[:, :, 0:2]), ALU.subtract)
                elif kind == "xo":
                    link(nc.vector.tensor_tensor(x_v[0:VD, 1, :], side[0:VD, 0:2 * NX], x_v[0:VD, 0, :], ALU.add))
                    x4 = x_v[0:VD, 1, :].rearrange("p (h w c) -> p h w c", w=2, c=2)
                    for o in range(2):
                        ins = nc.vector.tensor_tensor(ym[VD * o:VD * o + VD, :, SEQ:SEQ + 2], x4[:, o::2, 0],
                                                      x4[:, o::2, 1], ALU.add)
                        ins.then_inc(sem["x_y" if o == 0 else "side_read_dve"], 1)
                    return
                else:
                    return
                ins.then_inc(sem["side_read_dve"], 1)

            for h, s in steps:
                g = SLOTS * h + s
                js = side_jobs(h, s)
                split = 0 <= g - 1 < G and (g - 1) % SLOTS not in POOL_LOW
                n = rows(g - 1)

                def low_half(c):
                    cs = slice(512 * c, 512 * c + 512)
                    nc.vector.tensor_tensor(e_l[(g - 1) % 2][0:n, cs], e_f[(g - 1) % 3][0:n, cs],
                                            f32(e_h[(g - 1) % 3][0:n, cs]), ALU.subtract).then_inc(sem["e_lo"], 1)

                if js[0]:
                    job(js[0])
                if split:
                    dve.wait_ge(sem["e_hi"], g)
                    if g - 1 >= 2:
                        dve.wait_ge(sem["pv_done"], g - 2)
                    low_half(0)
                for j in js[1:3]:
                    if j:
                        job(j)
                if split:
                    low_half(1)
                if js[3]:
                    job(js[3])
                if h == HEADS - 1 and s == 3:
                    dve.wait_ge(sem["x_row_in"], 16)
                    link(nc.vector.tensor_reduce(x_v[0:NX, 3, 0:1], x_row, AX.X, ALU.max))
                    nc.vector.tensor_scalar(x_v[0:NX, 3, 0:1], x_v[0:NX, 3, 0:1], -SCALE, None, ALU.mult)\
                      .then_inc(sem["x_max"], 1)
                if h == HEADS - 1 and s == 4:
                    dve.wait_ge(sem["x_exp"], 1)
                    link(nc.vector.tensor_reduce(x_v[0:NX, 3, 1:2], x_row, AX.X, ALU.add))
                    link(nc.vector.reciprocal(x_v[0:NX, 3, 2:3], x_v[0:NX, 3, 1:2]))
                    nc.vector.tensor_scalar(x_row, x_row, x_v[0:NX, 3, 2:3], None, ALU.mult).then_inc(sem["x_prob"], 1)

        @block.tensor
        def _(pe):
            def tile_of(i):
                return slice(P * i, P * i + P) if i < XT else slice(SEQ, T)

            def job(j):
                kind, h = j
                b = h % 2
                side = side_of(j)
                for i in before(j):
                    wait_read(pe, i)
                if kind[:2] in ("tq", "tk"):
                    c0 = QK * (h + (HEADS if kind[1] == "k" else 0))
                    for t in range(4):
                        ins = nc.tensor.transpose(side[0:QK, P * t:P * t + P], qk[:, 4 * int(kind[2]) + t, c0:c0 + QK], ident)
                elif kind == "tm":
                    for w in range(2):
                        c0 = QK * (h + HEADS * w)
                        ins = nc.tensor.transpose(side[0:QK, META * w:META * w + META], qk[0:META, XT, c0:c0 + QK],
                                                  ident[0:META, 0:META])
                elif kind == "am":
                    pe.wait_ge(sem["side_hi"], hi_upto(j))
                    for t in range(XT):
                        ins = nc.tensor.matmul(side[:, META * t:META * t + META], q_h[b][0:QK, tile_of(t)],
                                               k_h[b][0:QK, SEQ:T], start=True, stop=True)
                elif kind[0] == "a":
                    pe.wait_ge(sem["side_hi"], hi_upto(j))
                    c, t = divmod(int(kind[1:]), XT)
                    ins = nc.tensor.matmul(side, q_h[b][0:QK, tile_of(t)], k_h[b][0:QK, 512 * c:512 * c + 512],
                                           start=True, stop=True)
                elif kind == "r":
                    wait_read(pe, ("am", h))
                    ins = nc.tensor.transpose(side[0:XT, 0:P], mx_all, ident)
                elif kind == "l":
                    pe.wait_ge(sem["e_summed"], XT * (h + 1))
                    for t in range(XT):
                        ins = nc.tensor.matmul(side[:, 2 * t:2 * t + 2], es[h % 2][:, tile_of(t)], ones[:, 0:2],
                                               start=True, stop=True)
                elif kind == "rt":
                    wait_read(pe, ("l", h))
                    ins = nc.tensor.transpose(side[0:XT, 0:P], rl, ident)
                elif kind in ("b0", "b1"):
                    wait_read(pe, ("rt", h))
                    for t in range(4):
                        ins = nc.tensor.matmul(side[0:VD, tile_of(t)], sel_r[:, 4 * int(kind[1]) + t, :], rl_r,
                                               start=True, stop=True)
                elif kind in ("x0", "x1", "x2"):
                    c = int(kind[1])
                    w = 512 if c < 2 else META
                    ks, qs = slice(512 * c, 512 * c + w), slice(T - 2, T)
                    if c == 0:
                        wait_read(pe, ("tm", h))
                    nc.tensor.matmul(side[0:2, 0:w], q_h[b][0:QK, qs], k_h[b][0:QK, ks], start=True, stop=False)
                    nc.tensor.matmul(side[0:2, 0:w], q_l[b][:, qs], k_h[b][0:QK, ks], start=False, stop=False)
                    ins = nc.tensor.matmul(side[0:2, 0:w], q_h[b][0:QK, qs], k_l[b][:, ks], start=False, stop=True)
                elif kind == "xt":
                    pe.wait_ge(sem["x_prob"], 1)
                    for t in range(NT):
                        n = rows(t)
                        ins = nc.tensor.transpose(side[0:n, NX * t:NX * t + NX], x_row[:, P * t:P * t + n],
                                                  ident[0:NX, 0:NX])
                elif kind == "xo":
                    ins = meta_pv(HEADS - 1)
                ins.then_inc(sem["side_done"], 1)

            def meta_pv(m):
                side = side_of(("xo", HEADS - 1))
                if m == 0:
                    wait_read(pe, ("xt", HEADS - 1))
                for t in range(NT):
                    n = rows(t)
                    ins = nc.tensor.matmul(side[:, 4 * m:4 * m + 4], v[0:n, t, 2 * VD * m:2 * VD * (m + 1)],
                                           x_e[0:n, t, m, :], start=t == 0, stop=t == XT)
                return ins

            def place_job(h, s, js, i):
                if js[i]:
                    job(js[i])
                elif h == HEADS - 1 and s in (6, 7):
                    meta_pv(4 * (s - 6) + i)

            def scores(g, c):
                h, s = divmod(g, SLOTS)
                b = h % 2
                ks = slice(P * s, P * s + rows(g))
                cs = slice(512 * c, 512 * c + 512)
                if c == 0:
                    if s == 0:
                        pe.wait_ge(sem["row_in"], 16 * (h + 1))
                    if g >= 2:
                        pe.wait_ge(sem["e_hi"], g - 1)
                out = s_ps(g)[0:rows(g), cs]
                nc.tensor.matmul(out, k_h[b][:, ks], q_h[b][:, cs], start=True, stop=False)
                nc.tensor.matmul(out, k_h[b][0:QK, ks], q_l[b][:, cs], start=False, stop=False)
                ins = nc.tensor.matmul(out, k_l[b][:, ks], q_h[b][0:QK, cs], start=False, stop=True)
                if c == 1:
                    ins.then_inc(sem["s_done"], 1)

            def pv(g, c):
                h, s = divmod(g, SLOTS)
                n = rows(g)
                if s in POOL_LOW:
                    pe.wait_ge(sem["e_lo_pool"], pool_lows(g))
                else:
                    pe.wait_ge(sem["e_lo"], lows(g) - 1 + c)
                if s == 0 and h and c == 0:
                    pe.wait_ge(sem["o_low"], h)
                    pe.wait_ge(sem["o_hi"], h)
                vt = v[0:n, s, 2 * VD * h:2 * VD * (h + 1)]
                cs = slice(512 * c, 512 * c + 512)
                nc.tensor.matmul(o_ps[:, cs], vt, e_h[g % 3][0:n, cs], start=s == 0, stop=False)
                ins = nc.tensor.matmul(o_ps[:, cs], vt, e_l[g % 2][0:n, cs], start=False, stop=s == XT)
                if c == 1:
                    ins.then_inc(sem["pv_done"], 1)

            for h, s in steps:
                if (h, s) == (0, 0):
                    pe.wait_ge(sem["b_set"], 4)
                js = side_jobs(h, s)
                g = SLOTS * h + s
                for c in range(2):
                    if 0 <= g < G:
                        scores(g, c)
                    place_job(h, s, js, c)
                for c in range(2):
                    if 0 <= g - 2 < G:
                        pv(g - 2, c)
                    place_job(h, s, js, 2 + c)


Q2 = SEQ + 2
M_H = M_A
M_HN = M_H + XT * D
M_HNL = M_HN + KD * Q2
M_3 = M_HNL + KD * Q2


M_WO = M_HN + KD * (D // 2)
M_UP = M_3 + 2 * KD * (D // 2) + 4096


def out_phase(nc, place, con, yl, ym, h, raw0, hn_h, hn_l, up, bank, dram, sem):
    half = D // 2
    at = M_3
    wo_h = [place("wo_h0", M_WO, (KD, half), F32R), place("wo_h1", at, (KD, half), F32R)]; at += KD * half
    wo_l = [place("wo_l0", M_WO + KD * half, (KD, half), F32R), place("wo_l1", at, (KD, half), F32R)]; at += KD * half
    ys_at = M_WO + 2 * KD * half
    ysum = [place(f"ysum{w}", ys_at + (Q2 + 6) * w, (Q2,)) for w in range(2)]
    ysq = [place(f"ysq{w}", ys_at + (Q2 + 6) * (2 + w), (Q2,)) for w in range(2)]
    assert ys_at + 4 * (Q2 + 6) <= M_3
    y_h = [place(f"y_h{b}", at + 2048 * b, (KD, P), F32R) for b in range(2)]
    y_l = [place(f"y_l{b}", at + 2048 * b + 1024, (KD, P), F32R) for b in range(2)]; at += 4096
    assert at == M_UP
    raw1 = [place(f"wo_raw1{b}", at + half * b, (half,)) for b in range(4)]; at += 4 * half
    hn = place("hn", at, (D,)); at += D
    fg = place("ffn_g", at, (D,)); at += D
    hm = place("h_meta", at, (D,), parts=2); at += D
    junk = place("h_sq", at, (D,)); at += D
    assert at <= M_YM, (at, M_YM)
    par, ident, ones = con["par"], con["ident"], con["ones"]
    stat = con["stat"].rearrange("p a b -> p (a b)")
    r_y, ss2, r2 = stat[:, 0:2 * NT], stat[:, 32:32 + NT], stat[:, 48:48 + NT]
    side = bank(6, 2)

    def rows(i):
        return P if i < XT else 2

    def cols(i):
        return slice(2 + P * i, 2 + P * i + P) if i < XT else slice(0, 2)

    def yl_cols(i):
        return slice(META + P * i, META + P * i + P) if i < XT else slice(META - 2, META)

    def ym_cols(i):
        return slice(P * i, P * i + P) if i < XT else slice(SEQ, Q2)

    units = [(0, i) for i in [XT] + list(range(XT))] + [(1, i) for i in range(NT)]

    def raw_of(m):
        return raw0[m] if m < KD else raw1[m % 4]

    def res(i):
        return h[:, i, :] if i < XT else hm

    with nc.Block() as block:
        @block.sync
        def _(sp):
            sp.dma_start(hm, dram["meta_tm"][META - 2:META, :]).then_inc(sem["res_in"], 16)
            sp.dma_start(fg, dram["ffn_g"]).then_inc(sem["res_in"], 16)
            for k in range(KD):
                if k >= 4:
                    sp.wait_ge(sem["wo_lo"], KD + k - 3)
                sp.dma_start(raw1[k % 4], dram["w_out"][P * k:P * k + P, half:]).then_inc(sem["wo_in"][k % 4], 16)
            sp.wait_ge(sem["wo_lo"], 2 * KD)
            sp.dma_start(up["raw"], dram["w_up"][0].rearrange("p a k n -> p (a k) n")).then_inc(sem["up_in"], 16)

        @block.gpsimd
        def _(pool):
            for u, (c, i) in enumerate(units):
                n = rows(i)
                pool.wait_ge(sem["y_hi"], 2 * u + 1)
                nc.gpsimd.tensor_tensor(y_l[u % 2][:, 0:LF, 0:n], yl[:, :, yl_cols(i)], f32(y_h[u % 2][:, 0:LF, 0:n]),
                                        ALU.subtract).then_inc(sem["y_lo"], 1)
                pool.wait_ge(sem["y_hi"], 2 * u + 2)
                nc.gpsimd.tensor_tensor(y_l[u % 2][:, LF:, 0:n], ym[:, :, ym_cols(i)], f32(y_h[u % 2][:, LF:, 0:n]),
                                        ALU.subtract).then_inc(sem["y_lo"], 1)
            pool.wait_ge(sem["wo_mm"], 2 * NT)
            pool.wait_ge(sem["up_hi"], 1)
            nc.gpsimd.tensor_tensor(up["l"], up["raw"], f32(up["h"]), ALU.subtract).then_inc(sem["up_lo"], 1)

        @block.scalar
        def _(act):
            def split_y(u):
                c, i = units[u]
                n = rows(i)
                if u >= 2:
                    act.wait_ge(sem["wo_mm"], u - 1)
                nc.scalar.activation(y_h[u % 2][:, 0:LF, 0:n], yl[:, :, yl_cols(i)], ACT.Copy).then_inc(sem["y_hi"], 1)
                nc.scalar.activation(y_h[u % 2][:, LF:, 0:n], ym[:, :, ym_cols(i)], ACT.Copy).then_inc(sem["y_hi"], 1)

            def split_w(m):
                k = m % KD
                if m < KD:
                    act.wait_ge(sem["wo_first"], 16 * KD)
                else:
                    act.wait_ge(sem["wo_in"][k % 4], 16 * (k // 4 + 1))
                g = par[:, COLS["out_g"] + k:COLS["out_g"] + k + 1]
                nc.scalar.activation(wo_h[m // KD][:, k, :], raw_of(m), ACT.Copy, scale=g).then_inc(sem["wo_hi"], 1)

            split_y(0)
            for k in range(KD):
                split_w(k)
                if k == 3:
                    split_y(1)
            for k in range(KD):
                w = k // LF
                if k == LF:
                    split_y(2)
                if k >= 2:
                    act.wait_ge(sem["ysum"], k - 1)
                if w == 0:
                    nc.scalar.activation(ysq[k % 2][:, 0:2], yl[:, k, META - 2:META], ACT.Square).then_inc(sem["ysq"], 1)
                    nc.scalar.activation(ysq[k % 2][:, 2:], yl[:, k, META:], ACT.Square).then_inc(sem["ysq"], 1)
                else:
                    nc.scalar.activation(ysq[k % 2][:, 0:2], ym[:, k - LF, SEQ:], ACT.Square).then_inc(sem["ysq"], 1)
                    nc.scalar.activation(ysq[k % 2][:, 2:], ym[:, k - LF, 0:SEQ], ACT.Square).then_inc(sem["ysq"], 1)
            split_y(3)
            act.wait_ge(sem["y_var"], 2)
            nc.scalar.activation(r_y[:, 0:2 * XT], r_y[:, 0:2 * XT], ACT.Sqrt).then_inc(sem["y_std"], 1)
            nc.scalar.activation(r_y[0:2, 2 * XT:], r_y[0:2, 2 * XT:], ACT.Sqrt).then_inc(sem["y_std"], 1)

            def square_h(t):
                i = units[NT + t][1]
                n = rows(i)
                act.wait_ge(sem["h_done"], 2 * (NT + t) + 2)
                nc.scalar.activation(junk[0:n], res(i)[0:n], ACT.Square, accum_out=ss2[0:n, t:t + 1]).then_inc(sem["h_sq"], 1)

            def std_h(t):
                n = rows(units[NT + t][1])
                act.wait_ge(sem["h_var"], t + 1)
                nc.scalar.activation(ss2[0:n, t:t + 1], ss2[0:n, t:t + 1], ACT.Sqrt).then_inc(sem["h_std"], 1)

            def high_h(t):
                i = units[NT + t][1]
                n = rows(i)
                act.wait_ge(sem["hn_t"], t + 1)
                if t == 0:
                    act.wait_ge(sem["wo_mm"], NT)
                nc.scalar.activation(hn_h[:, :, cols(i)], side.rearrange("p (k n) -> p k n", k=KD)[:, :, 0:n], ACT.Copy)\
                  .then_inc(sem["hn_hi"], 1)

            for u in range(2, 2 * NT):
                if u > 3:
                    split_y(u)
                if u - 2 < KD:
                    split_w(KD + u - 2)
                t = u - NT - 1
                if t >= 0:
                    square_h(t)
                    std_h(t)
                if t >= 1:
                    high_h(t - 1)
            square_h(NT - 1)
            std_h(NT - 1)
            act.wait_ge(sem["wo_mm"], 2 * NT)
            act.wait_ge(sem["up_in"], 16)
            nc.scalar.activation(up["h"], up["raw"], ACT.Copy).then_inc(sem["up_hi"], 1)
            high_h(NT - 2)
            high_h(NT - 1)

        @block.vector
        def _(dve):
            link = chain(dve, sem["dve_link4"])

            def split_w(m):
                k = m % KD
                g = par[:, COLS["out_g"] + k:COLS["out_g"] + k + 1]
                dve.wait_ge(sem["wo_hi"], m + 1)
                nc.vector.scalar_tensor_tensor(out=wo_l[m // KD][:, k, :], in0=raw_of(m), scalar=g,
                                               in1=f32(wo_h[m // KD][:, k, :]), op0=ALU.mult, op1=ALU.subtract)\
                  .then_inc(sem["wo_lo"], 1)

            for k in range(KD):
                split_w(k)
            for k in range(KD):
                w = k // LF
                dve.wait_ge(sem["ysq"], 2 * k + 2)
                if k % LF == 0:
                    nc.vector.tensor_copy(ysum[w], ysq[k % 2]).then_inc(sem["ysum"], 1)
                else:
                    dve.wait_ge(sem["ysum"], k)
                    nc.vector.tensor_tensor(ysum[w], ysum[w], ysq[k % 2], ALU.add).then_inc(sem["ysum"], 1)
            dve.wait_ge(sem["yss_mm"], 1)
            ss = side[:, 0:4 * NT].rearrange("p (i t) -> p i t", t=2)[:, :, 0]
            nc.vector.tensor_scalar(r_y[:, 0:2 * XT], ss[:, 0:2 * XT], 1.0 / LRU, EPS, ALU.mult, ALU.add)\
              .then_inc(sem["y_var"], 1)
            nc.vector.tensor_scalar(r_y[0:2, 2 * XT:], ss[0:2, 2 * XT:], 1.0 / LRU, EPS, ALU.mult, ALU.add)\
              .then_inc(sem["y_var"], 1)
            dve.wait_ge(sem["y_std"], 2)
            link(nc.vector.reciprocal(r_y[:, 0:2 * XT], r_y[:, 0:2 * XT]))
            link(nc.vector.reciprocal(r_y[0:2, 2 * XT:], r_y[0:2, 2 * XT:]))
            dve.wait_ge(sem["res_in"], 16 * (2 + XT))

            def add_groups(u):
                c, i = units[u]
                n = rows(i)
                cs = slice(half * c, half * c + half)
                dve.wait_ge(sem["wo_mm"], u + 1)
                for w in range(2):
                    r = r_y[0:n, 2 * i + w:2 * i + w + 1]
                    nc.vector.scalar_tensor_tensor(out=res(i)[0:n, cs], in0=bank(2 * (u % 3) + w)[0:n], scalar=r,
                                                   in1=res(i)[0:n, cs], op0=ALU.mult, op1=ALU.add)\
                      .then_inc(sem["h_done"], 1)
                    dve.wait_ge(sem["h_done"], 2 * u + w + 1)

            def normalise(t):
                i = units[NT + t][1]
                n = rows(i)
                dve.wait_ge(sem["h_sq"], t + 1)
                nc.vector.tensor_scalar(ss2[0:n, t:t + 1], ss2[0:n, t:t + 1], 1.0 / D, EPS, ALU.mult, ALU.add)\
                  .then_inc(sem["h_var"], 1)
                dve.wait_ge(sem["h_std"], t + 1)
                link(nc.vector.reciprocal(r2[0:n, t:t + 1], ss2[0:n, t:t + 1]))
                if t:
                    dve.wait_ge(sem["hn_t"], t)
                nc.vector.scalar_tensor_tensor(out=hn[0:n], in0=res(i)[0:n], scalar=r2[0:n, t:t + 1], in1=fg[0:n],
                                               op0=ALU.mult, op1=ALU.mult).then_inc(sem["hn"], 1)

            def low_h(t):
                i = units[NT + t][1]
                n = rows(i)
                dve.wait_ge(sem["hn_hi"], t + 1)
                nc.vector.tensor_tensor(hn_l[:, :, cols(i)], side.rearrange("p (k n) -> p k n", k=KD)[:, :, 0:n],
                                        f32(hn_h[:, :, cols(i)]), ALU.subtract).then_inc(sem["hn_lo"], 1)

            for u in range(2 * NT):
                add_groups(u)
                if u < KD:
                    split_w(KD + u)
                t = u - NT
                if t >= 0:
                    normalise(t)
                if t >= 1:
                    low_h(t - 1)
            low_h(NT - 1)

        @block.tensor
        def _(pe):
            def transpose_h(t):
                n = rows(units[NT + t][1])
                pe.wait_ge(sem["hn"], t + 1)
                if t:
                    pe.wait_ge(sem["hn_lo"], t)
                for k in range(KD):
                    ins = nc.tensor.transpose(side[:, P * k:P * k + n], hn[0:n, P * k:P * k + P], ident[0:n, 0:n])
                ins.then_inc(sem["hn_t"], 1)

            for u, (c, i) in enumerate(units):
                n = rows(i)
                pe.wait_ge(sem["y_lo"], 2 * u + 2)
                if u >= 3:
                    pe.wait_ge(sem["h_done"], 2 * (u - 2))
                for k in range(KD):
                    if u == 0 or (c == 1 and u == NT):
                        pe.wait_ge(sem["wo_lo"], KD * c + k + 1)
                    w = k // LF
                    ins = split_products(nc, bank(2 * (u % 3) + w)[0:n], y_h[u % 2][:, k, 0:n], y_l[u % 2][:, k, 0:n],
                                         wo_h[c][:, k, :], wo_l[c][:, k, :], k % LF == 0, k % LF == LF - 1)
                ins.then_inc(sem["wo_mm"], 1)
                if u == 2:
                    pe.wait_ge(sem["ysum"], KD)
                    for j in range(NT):
                        m = rows(j)
                        for w in range(2):
                            o = side[0:m, 2 * (2 * j + w):2 * (2 * j + w) + 2]
                            ins = nc.tensor.matmul(o, ysum[w][:, cols(j)], ones[:, 0:2], start=True, stop=True)
                    ins.then_inc(sem["yss_mm"], 1)
                t = u - NT - 1
                if t >= 0:
                    if t == 0:
                        pe.wait_ge(sem["y_var"], 2)
                    transpose_h(t)
            transpose_h(NT - 1)


def up_map(place):
    return {"h": place("up_h0", M_3, (2 * KD, P), F32R), "l": place("up_l0", M_3 + 2 * KD * P, (2 * KD, P), F32R),
            "raw": place("up_raw", M_UP, (2 * KD, P))}


def ffn_phase(nc, place, con, h, hn_h, hn_l, up_0, bank, dram, out, sem):
    at = M_3
    up_h, up_l, dn_h, dn_l, a_h, a_l, dn_raw = [], [], [], [], [], [], []
    up_raw = up_0["raw"]
    for e in range(2):
        up_h.append(up_0["h"] if e == 0 else place("up_h1", at, (2 * KD, P), F32R)); at += 2 * KD * P
        up_l.append(up_0["l"] if e == 0 else place("up_l1", at, (2 * KD, P), F32R)); at += 2 * KD * P
    for e in range(2):
        if e == 1:
            assert at == M_UP
            at += 2 * KD * P
        dn_h.append(place(f"dn_h{e}", at, (D,), F32R)); at += D
        dn_l.append(place(f"dn_l{e}", at, (D,), F32R)); at += D
        a_h.append(place(f"a_h{e}", at, (SEQ,), F32R)); at += SEQ
        a_l.append(place(f"a_l{e}", at, (SEQ,), F32R)); at += SEQ
    for e in range(2):
        dn_raw.append(place(f"dn_raw{e}", at, (D,))); at += D
    assert at <= WORDS, at
    at = M_YL
    gs = place("gate", at, (Q2 + 2,)); at += Q2 + 6
    cv = place("gate_conv", at, (SEQ,)); at += SEQ
    pr = place("ffn_act", at, (SEQ,)); at += SEQ
    par = con["par"]
    third = Q2 // 3
    assert third * 3 == Q2 and third % 2 == 0
    GROUPS = NFF // 2
    NU = 2 * XT

    g_ps = bank(0, 3).rearrange("p (c n) -> p c n", c=3)[:, :, 0:third]
    u_ps = bank(3, 2)

    def reads(g, n):
        return NU * g + n + 1

    def over_groups(eng, first, steady, last):
        first(0)
        with eng.Fori(1, GROUPS - 1) as g:
            steady(g)
        last(GROUPS - 1)

    with nc.Block() as block:
        @block.sync
        def _(sp):
            def load(g, wait=True):
                for e in range(2):
                    t = 2 * g + e
                    if wait or e:
                        sp.wait_ge(sem["up_lo"], t)
                        sp.dma_start(up_raw, dram["w_up"][bass.ds(t, 1)].rearrange("o p a k n -> p (o a k) n"))\
                          .then_inc(sem["up_in"], 16)
                    if wait:
                        sp.wait_ge(sem["dn_lo"], t - 1)
                    sp.dma_start(dn_raw[e], dram["w_down"].rearrange("(t p) n -> t p n", p=P)[bass.ds(t, 1)]
                                 .rearrange("o p n -> p (o n)")).then_inc(sem["dn_in"][e], 16)

            load(0, False)
            with sp.Fori(1, GROUPS) as g:
                load(g)
            for u in range(NU):
                i, c = divmod(u, 2)
                sp.wait_ge(sem["dn_read"], reads(GROUPS - 1, u + 1))
                sp.dma_start(out[P * i:P * i + P, 512 * c:512 * c + 512], h[:, i, 512 * c:512 * c + 512])\
                  .then_inc(sem["stored"], 16)
            sp.wait_ge(sem["stored"], 16 * NU)

        @block.gpsimd
        def _(pool):
            def low_up(t, e):
                pool.wait_ge(sem["up_hi"], t + 1)
                nc.gpsimd.tensor_tensor(up_l[e], up_raw, f32(up_h[e]), ALU.subtract).then_inc(sem["up_lo"], 1)

            def low_dn(t, e):
                pool.wait_ge(sem["dn_hi"], t + 1)
                nc.gpsimd.tensor_tensor(dn_l[e], dn_raw[e], f32(dn_h[e]), ALU.subtract).then_inc(sem["dn_lo"], 1)

            low_up(1, 1)

            def group(g, more=True):
                for e in range(2):
                    low_dn(2 * g + e, e)
                    if more:
                        low_up(2 * g + 2 + e, e)

            over_groups(pool, group, group, lambda g: group(g, False))

        @block.scalar
        def _(act):
            def high_up(t, e):
                act.wait_ge(sem["up_in"], 16 * t + 16)
                nc.scalar.activation(up_h[e], up_raw, ACT.Copy).then_inc(sem["up_hi"], 1)

            high_up(1, 1)

            def group(g, down=True, more=True):
                for e in range(2):
                    t = 2 * g + e
                    act.wait_ge(sem["gate_mm"], t + 1)
                    if down or e:
                        act.wait_ge(sem["conv2"], t)
                    nc.scalar.activation(gs[:, 0:Q2].rearrange("p (c n) -> p c n", c=3), g_ps, ACT.Copy)\
                      .then_inc(sem["gate_read"], 1)
                    act.wait_ge(sem["conv2"], t + 1)
                    nc.scalar.activation(cv, cv, ACT.Silu).then_inc(sem["silu"], 1)
                    if down:
                        act.wait_ge(sem["dn_mm"], NU * g)
                    act.wait_ge(sem["dn_in"][e], 16 * g + 16)
                    nc.scalar.activation(dn_h[e], dn_raw[e], ACT.Copy).then_inc(sem["dn_hi"], 1)
                    act.wait_ge(sem["prod"], t + 1)
                    nc.scalar.activation(a_h[e], pr, ACT.Copy).then_inc(sem["a_hi"], 1)
                    if more:
                        act.wait_ge(sem["up_mm"], t + 1)
                        high_up(t + 2, e)

            over_groups(act, lambda g: group(g, down=False), group, lambda g: group(g, more=False))

        @block.vector
        def _(dve):
            nc.vector.memset(gs[:, Q2:Q2 + 2], 0.0).then_inc(sem["dn_read"], 1)
            dve.wait_ge(sem["dn_read"], 1)

            def col(name, i):
                return par[:, bass.ds(COLS[name] + i, 1)]

            def group(g, down=True):
                for e in range(2):
                    t = 2 * g + e
                    dve.wait_ge(sem["gate_read"], t + 1)
                    if down or e:
                        dve.wait_ge(sem["prod"], t)
                    nc.vector.tensor_scalar(cv, gs[:, 1:1 + SEQ], col("ffn_w", 3 * t), col("ffn_b", t),
                                            ALU.mult, ALU.add).then_inc(sem["conv_a"], 1)
                    dve.wait_ge(sem["conv_a"], 2 * t + 1)
                    nc.vector.scalar_tensor_tensor(out=cv, in0=gs[:, 2:2 + SEQ], scalar=col("ffn_w", 3 * t + 1), in1=cv,
                                                   op0=ALU.mult, op1=ALU.add).then_inc(sem["conv_a"], 1)
                    dve.wait_ge(sem["conv_a"], 2 * t + 2)
                    nc.vector.scalar_tensor_tensor(out=cv, in0=gs[:, 3:3 + SEQ], scalar=col("ffn_w", 3 * t + 2), in1=cv,
                                                   op0=ALU.mult, op1=ALU.add).then_inc(sem["conv2"], 1)
                    dve.wait_ge(sem["silu"], t + 1)
                    dve.wait_ge(sem["up_mm"], t + 1)
                    if down or e:
                        dve.wait_ge(sem["a_lo"], t)
                    nc.vector.tensor_tensor(pr, u_ps, cv, ALU.mult).then_inc(sem["prod"], 1)
                    if e == 0 and down:
                        add_down(g - 1)
                    dve.wait_ge(sem["a_hi"], t + 1)
                    nc.vector.tensor_tensor(a_l[e], pr, f32(a_h[e]), ALU.subtract).then_inc(sem["a_lo"], 1)

            def add_down(g):
                for u in range(NU):
                    i, c = divmod(u, 2)
                    r = h[:, i, 512 * c:512 * c + 512]
                    if u == 0:
                        dve.wait_ge(sem["dn_read"], reads(g, 0))
                    dve.wait_ge(sem["dn_mm"], NU * g + u + 1)
                    nc.vector.tensor_tensor(r, bank(5 + u % 3), r, ALU.add).then_inc(sem["dn_read"], 1)

            over_groups(dve, lambda g: group(g, down=False), group, group)
            add_down(GROUPS - 1)

        @block.tensor
        def _(pe):
            def up(g, e, first):
                t = 2 * g + e
                pe.wait_ge(sem["up_lo"], t + 1)
                if not first:
                    pe.wait_ge(sem["gate_read"], t)
                for k in range(KD):
                    for c in range(3):
                        cs = slice(third * c, third * c + third)
                        ins = split_products(nc, g_ps[:, c], up_h[e][:, k, :], up_l[e][:, k, :], hn_h[:, k, cs],
                                             hn_l[:, k, cs], k == 0, k == KD - 1)
                ins.then_inc(sem["gate_mm"], 1)
                if not first:
                    pe.wait_ge(sem["prod"], t)
                for k in range(KD):
                    for c in range(2):
                        cs = slice(2 + 512 * c, 2 + 512 * c + 512)
                        ins = split_products(nc, u_ps[:, 512 * c:512 * c + 512], up_h[e][:, KD + k, :],
                                             up_l[e][:, KD + k, :], hn_h[:, k, cs], hn_l[:, k, cs], k == 0, k == KD - 1)
                ins.then_inc(sem["up_mm"], 1)

            def down(g):
                pe.wait_ge(sem["a_lo"], 2 * g + 2)
                pe.wait_ge(sem["dn_lo"], 2 * g + 2)
                pe.wait_ge(sem["dn_read"], reads(g, 0))
                for u in range(NU):
                    i, c = divmod(u, 2)
                    ts, cs = slice(P * i, P * i + P), slice(512 * c, 512 * c + 512)
                    if u >= 3:
                        pe.wait_ge(sem["dn_read"], reads(g, u - 2))
                    for e in range(2):
                        ins = split_products(nc, bank(5 + u % 3), a_h[e][:, ts], a_l[e][:, ts], dn_h[e][:, cs],
                                             dn_l[e][:, cs], e == 0, e == 1)
                    ins.then_inc(sem["dn_mm"], 1)

            def group(g):
                up(g, 0, False)
                down(g - 1)
                up(g, 1, False)

            def first(g):
                up(g, 0, True)
                up(g, 1, False)

            over_groups(pe, first, group, group)
            down(GROUPS - 1)


SEMS = """par_in gw_in con_in x_hi x_sq x_lo x_acc ones pads w_split gw_split xc_hi xc_lo a_ready a_sq scanned gelu
y_lru lam_e lam_done w_hi gw_hi w1_split w_tanh std conv unit_done unit_read_act unit_read_dve var_lru
sqrt_lru pool_link act_link dve_link uq_in ukv_in csq uq_hi ukv_hi uq_lo v_hi v_lo roped c_hi c_lo kv_var
kv_std kv_rstd q_mm kv_mm st_mm squares summed kvs k_scaled q_scaled head_var head_std dve_link2 tables
csq_act pe_sq ukv_lo q_read rope_done sel_in b_set e_summed e_full e_hi e_lo e_lo_pool side_done side_hi
side_read_act side_read_dve s_done pv_done o_low o_sum x_y x_exp dve_link3 o_hi x_max x_row_in x_in row_in
x_prob wo_first wo_lo wo_hi res_in y_hi y_lo ysq ysum y_var y_std yss_mm wo_mm h_done h_sq h_var h_std hn
hn_t hn_hi hn_lo dve_link4 up_in up_hi up_lo dn_hi dn_lo gate_mm up_mm gate_read conv_a conv2 silu prod a_hi
a_lo dn_mm dn_read stored""".split()


def build(nc, dram, out):
    with ExitStack() as ctx:
        place = Place(nc)
        con = constants(place)
        sem = {n: ctx.enter_context(nc.semaphore(n)) for n in SEMS}
        sem["xt_in"] = [ctx.enter_context(nc.semaphore(f"xt_in{b}")) for b in range(4)]
        sem["wo_in"] = [ctx.enter_context(nc.semaphore(f"wo_in{b}")) for b in range(4)]
        sem["dn_in"] = [ctx.enter_context(nc.semaphore(f"dn_in{b}")) for b in range(2)]
        sem["w_in"] = [ctx.enter_context(nc.semaphore(f"w_in{b}")) for b in range(2)]
        all_banks = ctx.enter_context(nc.psum_tensor("banks", [P, 8 * 512], F32))

        def bank(b, n=1):
            return all_banks[:, 512 * b:512 * (b + n)]

        yl = place("y_lru", M_YL, (LF, T))
        cq = place("cq", M_CQ, (3, T))
        kpe = place("kpe_fm", M_KPE, (T,), parts=ROPE)
        xpad = place("xpad", M_KPE, (T + 3,))
        lat = latent_map(place)
        mix_phase(nc, place, con, yl, cq, (kpe, xpad), lat, [bank(b) for b in range(8)], dram, sem)
        qk = place("qk", M_QK, (NT, 2 * HEADS * QK))
        v = place("v", M_V, (NT, HEADS * 2 * VD), F32R)
        qkv_phase(nc, place, con, cq, kpe, lat, qk, v, bank, sem)
        ym = place("y_mla", M_YM, (KD // 2, SEQ + 2))
        h = place("h", M_H, (XT, D))
        wo_raw = [place(f"wo_raw0{k}", M_HN + D // 2 * k, (D // 2,)) for k in range(KD)]
        attention_phase(nc, place, con, qk, v, ym, h, wo_raw, bank, dram, sem)
        hn_h = place("hn_h", M_HN, (KD, Q2), F32R)
        hn_l = place("hn_l", M_HNL, (KD, Q2), F32R)
        up_0 = up_map(place)
        out_phase(nc, place, con, yl, ym, h, wo_raw, hn_h, hn_l, up_0, bank, dram, sem)
        ffn_phase(nc, place, con, h, hn_h, hn_l, up_0, bank, dram, out, sem)


def _pack(inputs):
    a = {k: np.ascontiguousarray(np.asarray(v)) for k, v in inputs.items()}
    h0 = np.concatenate([a["meta_tokens"], a["x"][0]], axis=0)

    def cols(v):
        v = v.reshape(-1, v.shape[-1] // P, P)
        return v.transpose(1, 0, 2).reshape(-1, P).T

    par = np.zeros((P, NCOL), np.float32)
    gate_b = np.stack([a["lru_b_a"][0], a["lru_b_x"][0]], 1).reshape(4, LRU)
    head_g = np.zeros((2, P), np.float32)
    head_g[:, 0:NOPE] = np.stack([a["q_norm_g"][0], a["k_norm_g"][0]])[:, 0:NOPE]
    head_g[:, NOPE:QK] = 1.0
    for name, v in [("mix_g", a["norm_mix_g"][0]), ("conv_w", a["conv_lru_w"][0]), ("conv_b", a["conv_lru_b"][0]),
                    ("gate_b", gate_b), ("lam", a["lru_lambda"][0]), ("q_g", a["q_latent_g"][0]),
                    ("kv_g", a["kv_latent_g"][0]), ("qk_g", head_g.reshape(-1)),
                    ("out_g", np.concatenate([a["lru_gate_g"][0], a["mla_out_g"][0]])),
                    ("ffn_w", a["conv_ffn_w"][0]), ("ffn_b", a["conv_ffn_b"][0])]:
        c = cols(v)
        par[:, COLS[name]:COLS[name] + c.shape[1]] = c
    gw = np.zeros((P, LF, 2, 2, P), np.float32)
    for d in range(2):
        for w, name in enumerate(["lru_w_a", "lru_w_x"]):
            for h in range(8):
                o = 64 * (h % 2)
                gw[o:o + 64, h // 2, d, w, o:o + 64] = a[name][0, d, h]
    inv = (10000.0 ** (-np.arange(0, ROPE, 2, dtype=np.float32) / ROPE)).astype(np.float32)
    ang = np.arange(T, dtype=np.float32)[:, None] * inv[None, :]
    cos, sin = np.cos(ang), np.sin(ang)
    rc, rs = np.zeros((P, NT, ROPE), np.float32), np.zeros((P, NT, ROPE), np.float32)
    for i in range(NT):
        n, t0 = token_rows(i)
        rc[:n, i] = np.concatenate([cos[t0:t0 + n], cos[t0:t0 + n]], 1)
        rs[:n, i] = np.concatenate([-sin[t0:t0 + n], sin[t0:t0 + n]], 1)
    gqk = np.broadcast_to(np.stack([a["q_norm_g"][0], a["k_norm_g"][0]])[None], (P, 2, QK))
    up = a["w_ffn_up"][0].reshape(KD, P, 2, NFF, P).transpose(3, 1, 2, 0, 4)
    return {
        "x_tm": a["x"][0], "meta_tm": a["meta_tokens"],
        "x_fm": np.ascontiguousarray(h0.T.reshape(KD, P, T)),
        "par": par, "gate_w": gw.reshape(P, 4 * LF, P), "w_in": a["w_in"][0],
        "ident": np.eye(P, dtype=np.float32), "gqk": np.ascontiguousarray(gqk), "rope_c": rc, "rope_s": rs,
        "w_uq": a["w_uq"][0], "w_ukv": a["w_ukv"][0], "w_out": a["w_out"][0],
        "ffn_g": np.ascontiguousarray(np.broadcast_to(a["norm_ffn_g"][0][None], (P, D))),
        "w_up": np.ascontiguousarray(up), "w_down": a["w_ffn_down"][0],
        "sel": _selectors(),
    }


def _selectors():
    s = np.zeros((P, XT, VD), np.float32)
    for i in range(XT):
        s[i, i] = 1.0
        s[32 + i, i] = 1.0
    return s


def kernel(**inputs):
    import concourse.bacc as _bacc
    from concourse.bass_utils import run_bass_kernel_spmd as _run

    nc = _bacc.Bacc("TRN2", target_bir_lowering=False, num_devices=1)
    arrays, dram = {}, {}
    for name, a in _pack(inputs).items():
        arrays[f"in_{name}"] = a
        dram[name] = nc.dram_tensor(f"in_{name}", a.shape, mybir.dt.from_np(a.dtype), kind="ExternalInput").ap()
    out = nc.dram_tensor("out_0", (SEQ, D), F32, kind="ExternalOutput").ap()
    build(nc, dram, out)
    r = _run(nc, [arrays], core_ids=[0])
    return r.results[0]["out_0"].reshape(1, SEQ, D)
```
